# Optimizing a Trainium2 kernel written in Bass

```python
import jax, jax.numpy as jnp
from jax import lax
import numpy as np

D_MODEL = 2048
BATCH = 1
SEQ = 256
DEPTH = 1

CHUNK = 64

D_MIX = D_MODEL
D_LRU = D_MIX // 2
D_POOL = D_MIX - D_LRU
LRU_HEADS = 16
LRU_HEAD_DIM = D_LRU // LRU_HEADS
CONV_WIDTH = 4
LRU_C = 8.0
POOL_WINDOWS = (2, 4, 8, 16)
POOL_GROUPS = len(POOL_WINDOWS)
POOL_GROUP_DIM = D_POOL // POOL_GROUPS
D_FF = ((8 * D_MODEL + 3 * 256 - 1) // (3 * 256)) * 256
N_MOD = 6
EPS = 1e-6


def rmsnorm(x, g):
    xf = x.astype(jnp.float32)
    y = xf * lax.rsqrt(jnp.mean(xf * xf, axis=-1, keepdims=True) + EPS)
    return (y * g.astype(jnp.float32)).astype(x.dtype)

def modulate(h, shift, scale):
    return h * (1 + scale[:, None, :]) + shift[:, None, :]

def causal_dwconv(x, w, b):
    y = lax.conv_general_dilated(
        x, w[:, None, :].astype(x.dtype), window_strides=(1,),
        padding=[(CONV_WIDTH - 1, 0)],
        dimension_numbers=("NWC", "WIO", "NWC"),
        feature_group_count=x.shape[-1])
    return y + b.astype(x.dtype)

def rg_lru(x, w_a, b_a, w_i, b_i, lam):
    bsz, seq, _ = x.shape
    xf = x.astype(jnp.float32)
    xh = xf.reshape(bsz, seq, LRU_HEADS, LRU_HEAD_DIM)
    r = jax.nn.sigmoid(jnp.einsum("bshi,hij->bshj", xh, w_a.astype(jnp.float32)).reshape(bsz, seq, D_LRU)
                       + b_a.astype(jnp.float32))
    i = jax.nn.sigmoid(jnp.einsum("bshi,hij->bshj", xh, w_i.astype(jnp.float32)).reshape(bsz, seq, D_LRU)
                       + b_i.astype(jnp.float32))
    log_a = LRU_C * r * jax.nn.log_sigmoid(lam.astype(jnp.float32))
    a = jnp.exp(log_a)
    mult = jnp.sqrt(-jnp.expm1(2.0 * log_a))
    u = mult * (i * xf)

    def combine(left, right):
        a1, b1 = left
        a2, b2 = right
        return a1 * a2, a2 * b1 + b2

    _, h = lax.associative_scan(combine, (a, u), axis=1)
    return h

def pool_mixer(x, w_pool, ls_pool):
    bsz, seq, _ = x.shape
    xf = x.astype(jnp.float32)
    cs0 = jnp.concatenate([jnp.zeros((bsz, 1, D_POOL), jnp.float32), jnp.cumsum(xf, axis=1)], axis=1)
    pos1 = jnp.arange(1, seq + 1, dtype=jnp.float32)
    outs = []
    for g, w in enumerate(POOL_WINDOWS):
        sl = slice(g * POOL_GROUP_DIM, (g + 1) * POOL_GROUP_DIM)
        c0 = cs0[..., sl]
        upper = c0[:, 1:]
        lower = jnp.concatenate([jnp.zeros((bsz, w - 1, POOL_GROUP_DIM), jnp.float32),
                                 c0[:, :seq - w + 1]], axis=1)
        count = jnp.minimum(pos1, float(w))[None, :, None]
        outs.append((upper - lower) / count - xf[..., sl])
    pooled = jnp.stack(outs, axis=2)
    y = jnp.einsum("bsgc,gcd->bsgd", pooled, w_pool.astype(jnp.float32)) * ls_pool.astype(jnp.float32)
    return y.reshape(bsz, seq, D_POOL)

def first_inputs(seed: int = 0) -> dict:
    key = jax.random.key(seed)
    ks = jax.random.split(key, 24)
    f32 = jnp.float32
    nrm = lambda k, shape, s: jax.random.normal(k, shape, f32) * s
    a0 = jax.random.uniform(ks[12], (DEPTH, D_LRU), f32, 0.9, 0.999)
    s0 = a0 ** (1.0 / LRU_C)
    lam = jnp.log(s0) - jnp.log1p(-s0)
    return {
        "x": nrm(ks[0], (BATCH, SEQ, D_MODEL), 1.0),
        "c": nrm(ks[1], (BATCH, D_MODEL), 1.0),
        "w_ada": nrm(ks[2], (DEPTH, D_MODEL, N_MOD * D_MODEL), 0.5 * D_MODEL ** -0.5),
        "b_ada": nrm(ks[3], (DEPTH, N_MOD * D_MODEL), 0.02),
        "g_norm_mix": 1.0 + nrm(ks[4], (DEPTH, D_MODEL), 0.05),
        "w_in": nrm(ks[5], (DEPTH, D_MODEL, 2 * D_LRU + D_POOL), D_MODEL ** -0.5),
        "w_conv": nrm(ks[6], (DEPTH, CONV_WIDTH, D_LRU), CONV_WIDTH ** -0.5),
        "b_conv": nrm(ks[7], (DEPTH, D_LRU), 0.02),
        "w_rg_a": nrm(ks[8], (DEPTH, LRU_HEADS, LRU_HEAD_DIM, LRU_HEAD_DIM), LRU_HEAD_DIM ** -0.5),
        "b_rg_a": nrm(ks[9], (DEPTH, D_LRU), 0.02),
        "w_rg_i": nrm(ks[10], (DEPTH, LRU_HEADS, LRU_HEAD_DIM, LRU_HEAD_DIM), LRU_HEAD_DIM ** -0.5),
        "b_rg_i": nrm(ks[11], (DEPTH, D_LRU), 0.02),
        "lru_lambda": lam,
        "w_pool": nrm(ks[13], (DEPTH, POOL_GROUPS, POOL_GROUP_DIM, POOL_GROUP_DIM), POOL_GROUP_DIM ** -0.5),
        "ls_pool": 1.0 + nrm(ks[14], (DEPTH, POOL_GROUPS, POOL_GROUP_DIM), 0.1),
        "w_out": nrm(ks[15], (DEPTH, D_MIX, D_MODEL), D_MIX ** -0.5),
        "g_norm_ffn": 1.0 + nrm(ks[16], (DEPTH, D_MODEL), 0.05),
        "w_ffn_gate": nrm(ks[17], (DEPTH, D_MODEL, D_FF), D_MODEL ** -0.5),
        "w_ffn_up": nrm(ks[18], (DEPTH, D_MODEL, D_FF), D_MODEL ** -0.5),
        "w_ffn_down": nrm(ks[19], (DEPTH, D_FF, D_MODEL), D_FF ** -0.5),
        "g_norm_final": 1.0 + nrm(ks[20], (D_MODEL,), 0.05),
    }

def first_block(x, c, w_ada, b_ada, g_norm_mix, w_in, w_conv, b_conv, w_rg_a, b_rg_a,
              w_rg_i, b_rg_i, lru_lambda, w_pool, ls_pool, w_out, g_norm_ffn,
              w_ffn_gate, w_ffn_up, w_ffn_down, g_norm_final):
    dt = x.dtype
    c_act = jax.nn.silu(c)
    for l in range(DEPTH):
        mod = c_act @ w_ada[l] + b_ada[l]
        sh1, sc1, gt1, sh2, sc2, gt2 = jnp.split(mod, N_MOD, axis=-1)

        h = modulate(rmsnorm(x, g_norm_mix[l]), sh1, sc1)
        proj = h @ w_in[l]
        xr = proj[..., :D_LRU]
        gr = proj[..., D_LRU:2 * D_LRU]
        xp = proj[..., 2 * D_LRU:]
        xr = causal_dwconv(xr, w_conv[l], b_conv[l])
        hr = rg_lru(xr, w_rg_a[l], b_rg_a[l], w_rg_i[l], b_rg_i[l], lru_lambda[l])
        y_lru = (hr * jax.nn.gelu(gr.astype(jnp.float32))).astype(dt)
        y_pool = pool_mixer(xp, w_pool[l], ls_pool[l]).astype(dt)
        y = jnp.concatenate([y_lru, y_pool], axis=-1) @ w_out[l]
        x = x + gt1[:, None, :] * y

        h = modulate(rmsnorm(x, g_norm_ffn[l]), sh2, sc2)
        f = (jax.nn.silu(h @ w_ffn_gate[l]) * (h @ w_ffn_up[l])) @ w_ffn_down[l]
        x = x + gt2[:, None, :] * f
    return rmsnorm(x, g_norm_final)


N_HEADS_MLA = 8
Q_LORA_RANK = 512
KV_LORA_RANK = 512
QK_NOPE_DIM = 128
QK_ROPE_DIM = 64
QK_HEAD_DIM = QK_NOPE_DIM + QK_ROPE_DIM
V_HEAD_DIM = 128
MLA_WIDTH = N_HEADS_MLA * V_HEAD_DIM
N_HEADS_SB = 8
SB_HEAD_DIM = 128
SB_WIDTH = N_HEADS_SB * SB_HEAD_DIM
D_FF_2 = -(-8 * D_MODEL // (3 * 256)) * 256
D_IN = Q_LORA_RANK + KV_LORA_RANK + QK_ROPE_DIM + 3 * SB_WIDTH + 2 * D_MODEL
Q_BLOCK = 128
ROPE_THETA = 10000.0


def _rms(x, g):
    xf = x.astype(jnp.float32)
    y = xf * lax.rsqrt(jnp.mean(xf * xf, axis=-1, keepdims=True) + EPS)
    return (y * g.astype(jnp.float32)).astype(x.dtype)

def _rope(x, pos):
    half = x.shape[-1] // 2
    freqs = ROPE_THETA ** (-jnp.arange(half, dtype=jnp.float32) / half)
    ang = pos.astype(jnp.float32)[..., None] * freqs
    cos = jnp.cos(ang)[:, :, None, :]
    sin = jnp.sin(ang)[:, :, None, :]
    xf = x.astype(jnp.float32)
    x1, x2 = xf[..., :half], xf[..., half:]
    return jnp.concatenate([x1 * cos - x2 * sin, x1 * sin + x2 * cos], axis=-1).astype(x.dtype)

def _mla_attention(q, k, v):
    S = q.shape[2]
    scale = QK_HEAD_DIM ** -0.5
    outs = []
    for i in range(S // Q_BLOCK):
        end = (i + 1) * Q_BLOCK
        qb = q[:, :, i * Q_BLOCK:end]
        s = jnp.einsum('bhqd,bhkd->bhqk', qb, k[:, :, :end]).astype(jnp.float32) * scale
        qi = i * Q_BLOCK + jnp.arange(Q_BLOCK)
        ki = jnp.arange(end)
        s = jnp.where(ki[None, :] <= qi[:, None], s, -jnp.inf)
        p = jax.nn.softmax(s, axis=-1).astype(v.dtype)
        outs.append(jnp.einsum('bhqk,bhkd->bhqd', p, v[:, :, :end]))
    return jnp.concatenate(outs, axis=2)

def _stick_breaking(q, k, v):
    S = q.shape[2]
    scale = SB_HEAD_DIM ** -0.5
    outs = []
    for i in range(S // Q_BLOCK):
        end = (i + 1) * Q_BLOCK
        qb = q[:, :, i * Q_BLOCK:end]
        z = jnp.einsum('bhqd,bhkd->bhqk', qb, k[:, :, :end]).astype(jnp.float32) * scale
        qi = i * Q_BLOCK + jnp.arange(Q_BLOCK)
        ki = jnp.arange(end)
        mask = ki[None, :] < qi[:, None]
        log_beta = jax.nn.log_sigmoid(z)
        log_one_minus = jnp.where(mask, jax.nn.log_sigmoid(-z), 0.0)
        tail = lax.cumsum(log_one_minus, axis=3, reverse=True) - log_one_minus
        a = jnp.where(mask, jnp.exp(log_beta + tail), 0.0).astype(v.dtype)
        outs.append(jnp.einsum('bhqk,bhkd->bhqd', a, v[:, :, :end]))
    return jnp.concatenate(outs, axis=2)

def _layer(x, c_act, pos, w_ada, b_ada, g_norm1, g_norm2, w_in, g_q_latent, g_kv_latent,
           w_uq, w_ukv, g_q_head, g_k_head, w_proj_mla, w_proj_sb, w_out, w_ffn_in, w_ffn_out):
    B, S, _ = x.shape
    ada = (c_act @ w_ada + b_ada)[:, None, :]
    sh1, sc1, gt1, sh2, sc2, gt2 = jnp.split(ada, 6, axis=-1)

    h = _rms(x, g_norm1) * (1 + sc1) + sh1
    proj = h @ w_in
    offs = np.cumsum([Q_LORA_RANK, KV_LORA_RANK, QK_ROPE_DIM, SB_WIDTH, SB_WIDTH, SB_WIDTH, D_MODEL])
    c_q, c_kv, k_pe, q_sb, k_sb, v_sb, gl_a, gl_b = jnp.split(proj, [int(o) for o in offs], axis=-1)

    q = (_rms(c_q, g_q_latent) @ w_uq).reshape(B, S, N_HEADS_MLA, QK_HEAD_DIM)
    kv = (_rms(c_kv, g_kv_latent) @ w_ukv).reshape(B, S, N_HEADS_MLA, QK_NOPE_DIM + V_HEAD_DIM)
    k_nope, v = kv[..., :QK_NOPE_DIM], kv[..., QK_NOPE_DIM:]
    k_pe_h = jnp.broadcast_to(k_pe[:, :, None, :], (B, S, N_HEADS_MLA, QK_ROPE_DIM))
    k = jnp.concatenate([k_nope, k_pe_h], axis=-1)
    q = _rms(q, g_q_head)
    k = _rms(k, g_k_head)
    q = jnp.concatenate([q[..., :QK_NOPE_DIM], _rope(q[..., QK_NOPE_DIM:], pos)], axis=-1)
    k = jnp.concatenate([k[..., :QK_NOPE_DIM], _rope(k[..., QK_NOPE_DIM:], pos)], axis=-1)
    y_a = _mla_attention(q.transpose(0, 2, 1, 3), k.transpose(0, 2, 1, 3), v.transpose(0, 2, 1, 3))
    y_a = y_a.transpose(0, 2, 1, 3).reshape(B, S, MLA_WIDTH)

    to_heads = lambda t: t.reshape(B, S, N_HEADS_SB, SB_HEAD_DIM).transpose(0, 2, 1, 3)
    y_b = _stick_breaking(to_heads(q_sb), to_heads(k_sb), to_heads(v_sb))
    y_b = y_b.transpose(0, 2, 1, 3).reshape(B, S, SB_WIDTH)

    merged = jax.nn.sigmoid(gl_a) * (y_a @ w_proj_mla) + jax.nn.sigmoid(gl_b) * (y_b @ w_proj_sb)
    x = x + gt1 * (merged @ w_out)

    h2 = _rms(x, g_norm2) * (1 + sc2) + sh2
    gate, up = jnp.split(h2 @ w_ffn_in, 2, axis=-1)
    x = x + gt2 * ((jax.nn.silu(gate) * up) @ w_ffn_out)
    return x

def second_inputs(seed: int = 0) -> dict:
    key = jax.random.key(seed)
    ks = jax.random.split(key, 24)
    f32 = jnp.float32

    def nrm(k, shape, fan_in):
        return jax.random.normal(k, shape, f32) * (fan_in ** -0.5)

    def gain(k, n):
        return 1.0 + 0.02 * jax.random.normal(k, (DEPTH, n), f32)

    x = jax.random.normal(ks[0], (BATCH, SEQ, D_MODEL), f32)
    c = jax.random.normal(ks[1], (BATCH, D_MODEL), f32)
    offset = jax.random.randint(ks[2], (BATCH, 1), 0, 1024, dtype=jnp.int32)
    positions = offset + jnp.arange(SEQ, dtype=jnp.int32)[None, :]
    return {
        "x": x,
        "c": c,
        "positions": positions,
        "w_ada": nrm(ks[3], (DEPTH, D_MODEL, 6 * D_MODEL), D_MODEL),
        "b_ada": 0.02 * jax.random.normal(ks[4], (DEPTH, 6 * D_MODEL), f32),
        "g_norm1": gain(ks[5], D_MODEL),
        "g_norm2": gain(ks[6], D_MODEL),
        "w_in": nrm(ks[7], (DEPTH, D_MODEL, D_IN), D_MODEL),
        "g_q_latent": gain(ks[8], Q_LORA_RANK),
        "g_kv_latent": gain(ks[9], KV_LORA_RANK),
        "w_uq": nrm(ks[10], (DEPTH, Q_LORA_RANK, N_HEADS_MLA * QK_HEAD_DIM), Q_LORA_RANK),
        "w_ukv": nrm(ks[11], (DEPTH, KV_LORA_RANK, N_HEADS_MLA * (QK_NOPE_DIM + V_HEAD_DIM)), KV_LORA_RANK),
        "g_q_head": gain(ks[12], QK_HEAD_DIM),
        "g_k_head": gain(ks[13], QK_HEAD_DIM),
        "w_proj_mla": nrm(ks[14], (DEPTH, MLA_WIDTH, D_MODEL), MLA_WIDTH),
        "w_proj_sb": nrm(ks[15], (DEPTH, SB_WIDTH, D_MODEL), SB_WIDTH),
        "w_out": nrm(ks[16], (DEPTH, D_MODEL, D_MODEL), D_MODEL),
        "w_ffn_in": nrm(ks[17], (DEPTH, D_MODEL, 2 * D_FF_2), D_MODEL),
        "w_ffn_out": nrm(ks[18], (DEPTH, D_FF_2, D_MODEL), D_FF_2),
    }

def second_block(x, c, positions, w_ada, b_ada, g_norm1, g_norm2, w_in, g_q_latent, g_kv_latent,
              w_uq, w_ukv, g_q_head, g_k_head, w_proj_mla, w_proj_sb, w_out, w_ffn_in, w_ffn_out):
    c_act = jax.nn.silu(c)
    for l in range(DEPTH):
        x = _layer(x, c_act, positions, w_ada[l], b_ada[l], g_norm1[l], g_norm2[l], w_in[l],
                   g_q_latent[l], g_kv_latent[l], w_uq[l], w_ukv[l], g_q_head[l], g_k_head[l],
                   w_proj_mla[l], w_proj_sb[l], w_out[l], w_ffn_in[l], w_ffn_out[l])
    return x


def setup_inputs(seed=0):
    out = dict(first_inputs(seed))
    for name, value in second_inputs(seed + 1).items():
        if name != "x":
            out[name + "_2"] = value
    return out


def reference(
    x, c, w_ada, b_ada, g_norm_mix, w_in, w_conv, b_conv, w_rg_a, b_rg_a, w_rg_i, b_rg_i,
    lru_lambda, w_pool, ls_pool, w_out, g_norm_ffn, w_ffn_gate, w_ffn_up, w_ffn_down,
    g_norm_final, c_2, positions_2, w_ada_2, b_ada_2, g_norm1_2, g_norm2_2, w_in_2,
    g_q_latent_2, g_kv_latent_2, w_uq_2, w_ukv_2, g_q_head_2, g_k_head_2, w_proj_mla_2,
    w_proj_sb_2, w_out_2, w_ffn_in_2, w_ffn_out_2,
):
    x = first_block(
        x, c, w_ada, b_ada, g_norm_mix, w_in, w_conv, b_conv, w_rg_a, b_rg_a, w_rg_i, b_rg_i,
        lru_lambda, w_pool, ls_pool, w_out, g_norm_ffn, w_ffn_gate, w_ffn_up, w_ffn_down,
        g_norm_final,
    )
    return second_block(
        x, c_2, positions_2, w_ada_2, b_ada_2, g_norm1_2, g_norm2_2, w_in_2, g_q_latent_2,
        g_kv_latent_2, w_uq_2, w_ukv_2, g_q_head_2, g_k_head_2, w_proj_mla_2, w_proj_sb_2,
        w_out_2, w_ffn_in_2, w_ffn_out_2,
    )


_drawn_inputs = setup_inputs


def setup_inputs(seed=0):
    import zlib

    import numpy as np

    out = dict(_drawn_inputs(seed))
    spreads = {}
    factors = {'g_norm_mix': 3.612,
     'b_conv': 4.468,
     'b_rg_a': 8.0,
     'b_rg_i': 8.0,
     'ls_pool': 2.705,
     'g_norm_ffn': 3.661,
     'g_norm1_2': 7.178,
     'g_norm2_2': 4.204,
     'g_q_latent_2': 8.0,
     'g_kv_latent_2': 8.0,
     'g_q_head_2': 8.0,
     'g_k_head_2': 8.0}
    for name, (base, spread) in spreads.items():
        noise = np.random.default_rng([zlib.crc32(name.encode()), seed]).standard_normal(out[name].shape)
        drawn = base * np.exp(spread * noise) if base else spread * noise
        out[name] = __import__('jax').numpy.asarray(drawn.astype(out[name].dtype))
    for name, factor in factors.items():
        out[name] = (out[name] * factor).astype(out[name].dtype)
    return out
```

```python
import numpy as np
from contextlib import ExitStack

import concourse.bass as bass
from concourse import mybir

F32 = mybir.dt.float32
F32R = mybir.dt.float32r
I32 = mybir.dt.int32
ALU = mybir.AluOpType
ACT = mybir.ActivationFunctionType
AX_X = mybir.AxisListType.X

T = 256
D = 2048
P = 128
KT = D // P
D_FF = 5632
LRU = 1024
HEADS = 8
EPS = 1e-6
COLS = 512
ADA_COLS = 1024
NF = D_FF // COLS

PARAMS = [("b_ada", 96), ("b_ada_2", 96), ("c", 16), ("c_2", 16), ("g_norm_mix", 16), ("g_norm_ffn", 16),
          ("g_norm_final", 16), ("g_norm1_2", 16), ("g_norm2_2", 16), ("w_conv", 32), ("b_conv", 8),
          ("b_rg_a", 8), ("b_rg_i", 8), ("lru_lambda", 8), ("ls_pool", 8), ("g_q_latent_2", 4),
          ("g_kv_latent_2", 4), ("g_q_head_2", 1), ("g_k_head_2", 1), ("q_rope", 1), ("k_rope", 1)]
COL = {}
_at = 0
for _name, _n in PARAMS:
    COL[_name] = _at
    _at += _n
assert _at <= 512

PERM, TRI, EVEN, ODD, SB_ONE, SB_NEG, MLA_NEG, FREQ, SIGN, N_CONST = 0, 128, 256, 384, 512, 896, 1280, 1664, 1665, 1792
IDENT, ONES, INV, N_BASE = 0, 128, 256, 320

U_WIN1, U_WOUT1, U_FFN1, U_WIN2, U_LAT, U_PROJ, U_WOUT2, U_FFN2 = 0, 24, 40, 172, 236, 244, 260, 276
N_UNITS = 408

A_FFN1, B_FFN1, C_FFN1 = 3 + 2 + 2 * NF, 3 + 2, 2 * NF
A_WIN2, B_WIN2 = A_FFN1 + 8, B_FFN1 + 8
LAT = [("A", 8), ("B", 12), ("C", 16), ("A", 0), ("B", 4), ("C", 20), ("A", 24)]
A_LAT, B_LAT, C_LAT = A_WIN2 + 3, B_WIN2 + 2, C_FFN1 + 1 + 2
A_END, C_END = A_LAT + 4 + 2 + 2 * NF, C_LAT + 2 * NF

Q_WIN1, Q_WOUT1, Q_FFN1, Q_WIN2, Q_LAT, Q_PROJ, Q_WOUT2, Q_FFN2 = 0, 4, 8, 12, 16, 18, 22, 26


class Count:

    def __init__(self):
        self.at, self.start, self.per, self.turn = 0, 0, 0, None

    def enter(self, turn, per):
        self.start, self.per, self.turn = self.at, per, turn

    def leave(self, turns):
        assert self.at - self.start == self.per, (self.at - self.start, self.per)
        self.at, self.per = self.start + self.per * turns, 0

    def value(self, more=0, times=1, over=1):
        n = (self.at + more) // over * times
        if not self.per:
            return n
        assert self.per % over == 0
        return self.turn * (self.per // over * times) + n


class Counts:

    def __init__(self):
        self.unit, self.sub = Count(), Count()
        self.A, self.B, self.C = Count(), Count(), Count()
        self.ada, self.ada_group = Count(), Count()
        self.gate, self.hid = Count(), Count()
        self.quad, self.chain = Count(), Count()
        self.all = dict(unit=self.unit, sub=self.sub, A=self.A, B=self.B, C=self.C, ada=self.ada,
                        ada_group=self.ada_group, gate=self.gate, hid=self.hid, quad=self.quad, chain=self.chain)

    def enter(self, turn, **per):
        for name, count in self.all.items():
            count.enter(turn, per.get(name, 0))

    def leave(self, turns):
        for count in self.all.values():
            count.leave(turns)


ADA_AFTER_16 = (0, 1, 3, 5, 7, 8, 10, 12)
ADA_AFTER_24 = (0, 2, 5, 8, 10, 13, 16, 18)
ADA_AFTER_8 = (0, 0, 1, 2, 2, 3, 4, 4)


def build(nc, x, positions, rows_src, weights, ada_w, base_const, att_const, rg_a, rg_i, w_pool, out):
    w_in, w_out, w_gate, w_up, w_down, w_in2, w_uq, w_ukv, w_pa, w_pb, w_out2, w_ffin2, w_ffout2 = weights
    with ExitStack() as ctx:
        here = [-(-nc.sbuf_base // 64) * 64]

        def place(name, shape, dt=F32):
            n = 4
            for s in shape[1:]:
                n *= s
            t = nc.alloc_sbuf_tensor_at(name, shape, dt, offset=here[0])
            here[0] += n
            return t

        arena = here[0]
        R = place("R", [P, 88, T])
        end = here[0]
        here[0] = arena
        HID = place("HID", [P, 4, 2 * T], F32R)
        here[0] = end
        X = place("X", [P, KT, T])
        H = place("H", [P, KT, 2 * T], F32R)
        YF = place("YF", [P, KT, T])
        RAW = [place(f"RAW{i}", [P, 4, COLS]) for i in range(4)]
        WHI = [place(f"WHI{i}", [P, 2, COLS], F32R) for i in range(2)]
        WLO = [place(f"WLO{i}", [P, 2, COLS], F32R) for i in range(2)]
        PRM = place("PRM", [P, 512])
        MOD = place("MOD", [P, 192])
        BASE = place("BASE", [P, N_BASE])
        RS = place("RS", [P, T])
        CA = place("CA", [P, 32])
        MC = place("MC", [P, 16])
        SM = place("SM", [P, 32])
        rf = R[:, :, :].rearrange("p a b -> p (a b)")
        yf = YF[:, :, :].rearrange("p a b -> p (a b)")
        ident, ones = BASE[:, IDENT:IDENT + P], BASE[:, ONES:ONES + P]
        tiles = lambda a, n: rf[:, a * T:(a + n) * T]
        ADA = [tiles(64 + 8 * i, 8).rearrange("p (k n) -> p k n", k=2) for i in range(2)]
        ACC = tiles(80, 4)
        G = tiles(84, 4)
        PRAW = R[:, 0:2, :].rearrange("p a (b c) -> p (a b) c", c=P)
        CON = tiles(64, 7)
        CS = [tiles(71, 1), tiles(72, 1)]

        PS = [ctx.enter_context(nc.psum_tensor(f"PS{i}", [P, 2, 512], F32)) for i in range(4)]
        PAIR = dict(A=PS[0], B=PS[1], C=PS[2])
        flat = lambda pair: PAIR[pair][:, :, :].rearrange("p a b -> p (a b)")
        SMALL, MISC = PS[3][:, 0, :], PS[3][:, 1, :]

        mod_at = lambda layer, which: 96 * layer + 16 * which
        eight = lambda first, t: PS[first + t // 4][:, t // 2 % 2, t % 2 * T:(t % 2 + 1) * T]
        three = lambda t: tiles(t, 3).rearrange("p (a b) -> p a b", a=2)
        KPE = tiles(87, 1)
        SC = three(83)

        sem = lambda n: ctx.enter_context(nc.semaphore(n))
        raw_in = [sem(f"raw_in{i}") for i in range(4)]
        hi_done, lo_done, pe_sub = sem("hi_done"), sem("lo_done"), sem("pe_sub")
        free = {p: sem(f"free_{p}") for p in "ABC"}
        ada_in = [sem(f"ada_in{i}") for i in range(2)]
        ada_op, ada_red, ada_bias = sem("ada_op"), sem("ada_red"), sem("ada_bias")
        yf_quad, h_hi, h_quad = sem("yf_quad"), sem("h_hi"), sem("h_quad")
        act_chain, dve_chain, pool_chain = sem("act_chain"), sem("dve_chain"), sem("pool_chain")
        mix_w, base_in, con_in, pos_in, rows_in, x_rows = (
            sem(n) for n in ("mix_w", "base_in", "con_in", "pos_in", "rows_in", "x_rows"))
        prm_t, prm_ready, praw_zero, cact, x_turned, x_in = (
            sem(n) for n in ("prm_t", "prm_ready", "praw_zero", "cact", "x_turned", "x_in"))
        sq_ready, ssq_ready, ms_ready, rt_ready = (sem(n) for n in ("sq_ready", "ssq_ready", "ms_ready", "rt_ready"))
        x_done, x_step = sem("x_done"), sem("x_step")
        gate_done, up_done, hid_hi, hid_lo = sem("gate_done"), sem("up_done"), sem("hid_hi"), sem("hid_lo")
        conv_step, lam_done, c8_done, rg_mm, rg_sig, a_done, tanh_done, gelu_done, m2_done, root_done = (
            sem(n) for n in ("conv_step", "lam_done", "c8_done", "rg_mm", "rg_sig", "a_done", "tanh_done",
                             "gelu_done", "m2_done", "root_done"))
        pooled, pool_mm, pool_ev = sem("pooled"), sem("pool_mm"), sem("pool_ev")
        lat_sq, lat_ss, lat_ms, lat_rt, lat_ev, ang_done, trig_done = (
            sem(n) for n in ("lat_sq", "lat_ss", "lat_ms", "lat_rt", "lat_ev", "ang_done", "trig_done"))
        z_mm, z_dve, z_act, sp_done, u_mm, w_dve, a_act, y_mm, y_ev = (
            sem(n) for n in ("z_mm", "z_dve", "z_act", "sp_done", "u_mm", "w_dve", "a_act", "y_mm", "y_ev"))
        hd_sq, hd_ss, hd_ms, hd_rt, rope_in, rope_swap, hd_scaled = (
            sem(n) for n in ("hd_sq", "hd_ss", "hd_ms", "hd_rt", "rope_in", "rope_swap", "hd_scaled"))
        s_mm, s_dve, p_act, p_dve, pt_mm, pt_ev, o_mm, o_ev = (
            sem(n) for n in ("s_mm", "s_dve", "p_act", "p_dve", "pt_mm", "pt_ev", "o_mm", "o_ev"))
        s_out = sem("s_out")

        ctx.enter_context(nc.allow_non_contiguous_dma("column blocks of the weights"))
        block = ctx.enter_context(nc.Block())

        @block.sync
        def _(sp):
            c = Counts()

            def slot_free():
                if c.unit.at >= 4:
                    sp.wait_ge(lo_done, c.unit.value(-3, times=2))
                c.unit.at += 1
                return (c.unit.at - 1) % 4

            def load(w, k, col):
                slot = slot_free()
                sp.dma_start(RAW[slot][:, :, :], w[:, bass.ds(k, 4), bass.ds(col, COLS)]).then_inc(raw_in[slot], 16)

            def group(w, col, kq=4):
                for q in range(kq):
                    load(w, 4 * q, col)

            def ffn(wg, gcol, wu, ucol, wd):
                def gate_up(i):
                    group(wg, gcol + i * COLS)
                    group(wu, ucol + i * COLS)

                def down(i):
                    for n in range(4):
                        load(wd, i * 4, n * COLS)

                gate_up(0)
                gate_up(1)
                down(0)
                with sp.Fori(2, NF) as i:
                    c.enter(i - 2, unit=12)
                    gate_up(i)
                    down(i - 1)
                c.leave(NF - 2)
                down(NF - 1)

            sp.dma_start(yf[:, 0:D], x[0:P, :]).then_inc(x_rows, 16)
            sp.dma_start(yf[:, D:2 * D], x[P:2 * P, :]).then_inc(x_rows, 16)
            group(w_in, 0)
            group(w_in, COLS)
            with sp.Fori(1, 3) as i:
                c.enter(i - 1, unit=8)
                group(w_in, i * 1024)
                group(w_in, i * 1024 + COLS)
            c.leave(2)
            for g in range(4):
                group(w_out, g * COLS)
            ffn(w_gate, 0, w_up, 0, w_down)
            group(w_in2, 0)
            group(w_in2, 512)
            OFF = 2 * 512 + 64
            for a, b in ((0, 3), (3, 7)):
                with sp.Fori(a, b) as i:
                    c.enter(i - a, unit=8)
                    group(w_in2, OFF + i * 1024)
                    group(w_in2, OFF + 512 + i * 1024)
                c.leave(b - a)

            slot = slot_free()
            dst = RAW[slot][:, :, :].rearrange("p a (b n) -> p (a b) n", n=P)
            for half in (0, 64):
                sp.dma_start(dst[:, :, half:half + 64], w_in2[:, :, 1024:1088]).then_inc(raw_in[slot], 16)

            def heads(w, per, at, n, first, count):
                slot = slot_free()
                for k in range(4):
                    sp.dma_start(RAW[slot][:, k, :].rearrange("p (h n) -> p h n", n=n),
                                 w[:, k, :].rearrange("p (h m) -> p h m", m=per)[:, first:first + count, at:at + n])\
                        .then_inc(raw_in[slot], 16)

            heads(w_uq, 192, 0, 128, 0, 4)
            heads(w_uq, 192, 0, 128, 4, 4)
            heads(w_uq, 192, 128, 64, 0, 8)
            heads(w_ukv, 256, 0, 128, 0, 4)
            heads(w_ukv, 256, 0, 128, 4, 4)
            heads(w_ukv, 256, 128, 128, 0, 4)
            heads(w_ukv, 256, 128, 128, 4, 4)
            with sp.Fori(0, 4) as i:
                c.enter(i, unit=4)
                group(w_pa, i * COLS, 2)
                group(w_pb, i * COLS, 2)
            c.leave(4)
            for g in range(4):
                group(w_out2, g * COLS)
            ffn(w_ffin2, 0, w_ffin2, D_FF, w_ffout2)
            assert c.unit.at == N_UNITS
            for tb in range(2):
                sp.wait_ge(x_in, 12 + 4 * tb)
                sp.dma_start(out[tb * P:(tb + 1) * P, :], yf[:, tb * D:(tb + 1) * D]).then_inc(s_out, 16)
            sp.wait_ge(s_out, 32)

        EXTRA = {U_LAT: 1, **{U_LAT + 1 + n: 3 for n in range(7)}}

        def landed(eng, c):
            n = c.unit.at
            extra = sum(v for u, v in EXTRA.items() if u % 4 == n % 4 and u <= n)
            eng.wait_ge(raw_in[n % 4], c.unit.value(0, times=16, over=4) + 16 * (1 + extra))

        @block.gpsimd
        def _(pool):
            c = Counts()

            def ada(layer, col):
                for j in range(8):
                    slot = c.ada.at % 2
                    if c.ada.at >= 2:
                        pool.wait_ge(ada_op, c.ada.value(-1, times=2))
                    pool.dma_start(ADA[slot], ada_w[layer][:, 2 * j:2 * j + 2, bass.ds(col, ADA_COLS)])\
                        .then_inc(ada_in[slot], 16)
                    c.ada.at += 1

            def step(ins):
                c.chain.at += 1
                ins.then_inc(pool_chain, 1)
                pool.wait_ge(pool_chain, c.chain.value())

            for g in range(4):
                ada(0, g * ADA_COLS)
            step(pool.memset(tiles(48, 8), 0.0))
            for n, w in enumerate((rg_a, rg_i)):
                dst = tiles(48 + 4 * n, 4).rearrange("p (t j) -> p t j", j=P)
                for half in range(2):
                    pool.dma_start(dst[64 * half:64 * half + 64, :, 64 * half:64 * half + 64], w[half])\
                        .then_inc(mix_w, 16)
            pool.dma_start(tiles(56, 8).rearrange("p (g n) -> p g n", n=T), w_pool).then_inc(mix_w, 16)
            with pool.Fori(0, 3) as i:
                c.enter(i, ada=8)
                ada(0, i * ADA_COLS + 4 * ADA_COLS)
            c.leave(3)

            pool.wait_ge(base_in, 16)
            pool.wait_ge(free["A"], 3)
            pool.wait_ge(free["B"], 3)
            sums = [YF[:, 12:14, :], YF[:, 14:16, :]]
            for g in range(4):
                src = R[:, 16 + 2 * g:18 + 2 * g, :]
                cur, w = src, 2 << g
                for level in range(g + 1):
                    dst, s = sums[level % 2], 1 << level
                    step(pool.tensor_copy(dst[:, :, 0:s], cur[:, :, 0:s]))
                    step(pool.tensor_tensor(dst[:, :, s:T], cur[:, :, s:T], cur[:, :, 0:T - s], ALU.add))
                    cur = dst
                inv = BASE[:, INV + 16 * g:INV + 16 * g + w]
                for a in range(2):
                    step(pool.tensor_tensor(cur[:, a, 0:w], cur[:, a, 0:w], inv, ALU.mult))
                step(pool.tensor_scalar(cur[:, :, w:T], cur[:, :, w:T], 1.0 / w, 1.0, ALU.mult, ALU.mult))
                pool.tensor_tensor(src, cur, src, ALU.subtract).then_inc(pooled, 1)
                pool.wait_ge(pooled, g + 1)

            for b in (7, 8, 9, 10, 11):
                ada(0, b * ADA_COLS)
            with pool.Fori(0, 12) as i:
                c.enter(i, ada=8)
                ada(1, i * ADA_COLS)
            c.leave(12)
            pool.wait_ge(ada_op, c.ada.value(0, times=2))
            pool.dma_start(CON, att_const).then_inc(con_in, 16)
            pool.dma_start(tiles(73, 1).bitcast(I32), positions.to_broadcast([P, T])).then_inc(pos_in, 16)

        @block.scalar
        def _(act):
            c = Counts()

            def step(ins):
                c.chain.at += 1
                ins.then_inc(act_chain, 1)
                act.wait_ge(act_chain, c.chain.value())

            def hi(n=1):
                for _ in range(n):
                    j, slot = c.sub.at % 2, c.unit.at % 4
                    if j == 0:
                        landed(act, c)
                    if c.sub.at >= 2:
                        act.wait_ge(pe_sub, c.sub.value(-1))
                    nc.scalar.activation(WHI[j][:, :, :], RAW[slot][:, 2 * j:2 * j + 2, :], ACT.Copy)\
                        .then_inc(hi_done, 1)
                    c.sub.at += 1
                    c.unit.at += j

            def copy_out(pair, dst, func=ACT.Copy):
                act.wait_ge(pe_sub, c.sub.value(-2))
                nc.scalar.activation(dst, flat(pair), func).then_inc(free[pair], 1)

            def split(waits, src=YF):
                for q, (s, v) in enumerate(waits):
                    act.wait_ge(s, v)
                    nc.scalar.activation(H[:, 4 * q:4 * q + 4, 0:T], src[:, 4 * q:4 * q + 4, :], ACT.Copy)\
                        .then_inc(h_hi, 1)

            def norm(k, ready, value):
                act.wait_ge(ready, value)
                for q in range(4):
                    nc.scalar.activation(YF[:, 4 * q:4 * q + 4, :], X[:, 4 * q:4 * q + 4, :], ACT.Square)\
                        .then_inc(sq_ready, 1)
                act.wait_ge(ms_ready, k + 1)
                nc.scalar.activation(RS[:, :], RS[:, :], ACT.Sqrt).then_inc(rt_ready, 1)

            def win_body(tile, skip=0, before=ACT.Copy, func=ACT.Copy):
                at = lambda n: rf[:, bass.ds((tile + n) * T, 4 * T)]
                for s in range(skip, 16):
                    hi()
                    if s == 1:
                        copy_out("B", at(-4), before)
                    if s == 9:
                        copy_out("A", at(0), func)

            def ffn():
                def gate():
                    act.wait_ge(pe_sub, c.sub.value(-2))
                    if c.gate.at:
                        act.wait_ge(hid_lo, c.gate.value())
                    nc.scalar.activation(G, flat("A"), ACT.Silu).then_inc(gate_done, 1)
                    c.gate.at += 1

                def hidden():
                    act.wait_ge(up_done, c.hid.value(1))
                    nc.scalar.activation(HID[:, :, 0:T], G.rearrange("p (a b) -> p a b", a=4), ACT.Copy)\
                        .then_inc(hid_hi, 1)
                    c.hid.at += 1

                def body(skip=0, subs=24, previous=True):
                    for s in range(skip, subs):
                        hi()
                        if s == 1 and previous:
                            hidden()
                        if s == 9:
                            gate()

                body(skip=2, subs=16, previous=False)
                body()
                with act.Fori(2, NF) as i:
                    c.enter(i - 2, unit=12, sub=24, hid=1, gate=1)
                    body()
                c.leave(NF - 2)
                hi(2)
                hidden()
                hi(6)

            for block_at, r, n, c0, c1, src in rows_src:
                if block_at == 3:
                    act.wait_ge(praw_zero, 1)
                act.dma_start(PRAW[r:r + n, block_at, c0:c1], src).then_inc(rows_in, 16)
            act.dma_start(BASE[:, :], base_const).then_inc(base_in, 16)
            act.wait_ge(prm_ready, 1)
            nc.scalar.activation(CA[:, :], PRM[:, COL["c"]:COL["c"] + 32], ACT.Silu).then_inc(cact, 1)

            hi(2)
            norm(0, x_in, 8)
            split([(yf_quad, q + 1) for q in range(4)])
            for s in range(2, 16):
                hi()
                if s == 9:
                    copy_out("A", tiles(0, 4))
            with act.Fori(1, 3) as i:
                c.enter(i - 1, unit=8, sub=16)
                win_body(i * 8)
            c.leave(2)
            hi(2)
            copy_out("B", tiles(20, 4))

            soft = SM[:, 8:16]
            step(nc.scalar.activation(soft, PRM[:, COL["lru_lambda"]:COL["lru_lambda"] + 8], ACT.Abs))
            step(nc.scalar.activation(soft, soft, ACT.Exp, scale=-1.0))
            nc.scalar.activation(soft, soft, ACT.Ln, bias=1.0).then_inc(lam_done, 1)
            for kind, name in enumerate(("b_rg_a", "b_rg_i")):
                for t in range(8):
                    act.wait_ge(rg_mm, 8 * kind + t // 2 * 2 + 2)
                    nc.scalar.activation(R[:, 32 + 8 * kind + t, :], eight(2 * kind, t), ACT.Sigmoid,
                                         bias=PRM[:, COL[name] + t:COL[name] + t + 1]).then_inc(rg_sig, 1)
            act.wait_ge(c8_done, 1)
            act.wait_ge(rg_sig, 16)
            for t in range(8):
                nc.scalar.activation(R[:, t, :], R[:, 32 + t, :], ACT.Exp, scale=SM[:, t:t + 1]).then_inc(a_done, 1)
            act.wait_ge(a_done, 8)
            for t in range(8):
                nc.scalar.activation(R[:, 32 + t, :], R[:, 32 + t, :], ACT.Tanh, scale=SM[:, t:t + 1])\
                    .then_inc(tanh_done, 1)
            act.wait_ge(free["A"], 3)
            act.wait_ge(free["B"], 2)
            nc.scalar.activation(tiles(8, 8), tiles(8, 8), ACT.Gelu_apprx_tanh).then_inc(gelu_done, 1)
            act.wait_ge(m2_done, 1)
            nc.scalar.activation(tiles(32, 8), tiles(48, 8), ACT.Sqrt, scale=-1.0).then_inc(root_done, 1)
            for t in range(8):
                act.wait_ge(pool_mm, t // 2 * 2 + 2)
                nc.scalar.activation(YF[:, 8 + t, :], eight(0, t), ACT.Copy,
                                     scale=PRM[:, COL["ls_pool"] + t:COL["ls_pool"] + t + 1]).then_inc(pool_ev, 1)
            split([(yf_quad, 5), (yf_quad, 6), (pool_ev, 4), (pool_ev, 8)])

            hi(30)
            hi(2)
            norm(1, free["B"], 5)
            split([(yf_quad, 7 + q) for q in range(4)])
            ffn()
            hi(2)
            norm(2, x_done, 1)
            norm(3, x_done, 2)
            split([(yf_quad, 11 + q) for q in range(4)])
            for s in range(2, 16):
                hi()
                if s == 9:
                    copy_out("A", tiles(0, 4))
            with act.Fori(0, 3) as i:
                c.enter(i, unit=8, sub=16)
                win_body(i * 8 + 8)
            c.leave(3)
            win_body(32, func=ACT.Sigmoid)
            with act.Fori(1, 4) as i:
                c.enter(i - 1, unit=8, sub=16)
                win_body(i * 8 + 32, before=ACT.Sigmoid, func=ACT.Sigmoid)
            c.leave(3)
            hi(2)
            copy_out("B", tiles(60, 4), ACT.Sigmoid)
            hi(2)

            act.wait_ge(free["A"], A_WIN2)
            act.wait_ge(free["B"], B_WIN2)
            for n in range(2):
                nc.scalar.activation(YF[:, 4 * n:4 * n + 4, :], R[:, 4 * n:4 * n + 4, :], ACT.Square)\
                    .then_inc(lat_sq, 1)
            act.wait_ge(lat_ms, 1)
            nc.scalar.activation(tiles(76, 2), tiles(76, 2), ACT.Sqrt).then_inc(lat_rt, 1)
            act.wait_ge(ang_done, 2)
            for n in range(2):
                nc.scalar.activation(CS[n], tiles(74 + n, 1), ACT.Sin).then_inc(trig_done, 1)
            act.wait_ge(pe_sub, 2 * (U_LAT + 1))
            nc.scalar.activation(KPE, PAIR["C"][:, 0, 0:T], ACT.Copy).then_inc(free["C"], 1)

            for hp in range(4):
                act.wait_ge(z_dve, hp + 1)
                step(nc.scalar.activation(tiles(81, 3), tiles(78, 3), ACT.Abs))
                step(nc.scalar.activation(tiles(81, 3), tiles(81, 3), ACT.Exp, scale=-1.0))
                nc.scalar.activation(tiles(81, 3), tiles(81, 3), ACT.Ln, bias=1.0).then_inc(z_act, 1)
                act.wait_ge(w_dve, hp + 1)
                nc.scalar.activation(tiles(81, 3), tiles(84, 3), ACT.Exp).then_inc(a_act, 1)
                act.wait_ge(y_mm, hp + 1)
                nc.scalar.activation(yf[:, (8 + 2 * hp) * T:(10 + 2 * hp) * T], MISC, ACT.Copy).then_inc(y_ev, 1)

            split([(lat_ev, 1), (lat_ev, 1)], src=R)
            for n in range(7):
                hi(2)
                copy_out(LAT[n][0], tiles(LAT[n][1], 4))
            act.wait_ge(free["A"], A_LAT)
            act.wait_ge(free["B"], B_LAT)
            act.wait_ge(free["C"], C_LAT)
            nc.scalar.activation(tiles(77, 1), KPE, ACT.Square).then_inc(hd_sq, 1)
            for hp in range(4):
                if hp:
                    act.wait_ge(hd_ss, hp)
                nc.scalar.activation(tiles(78, 2), tiles(8 + 2 * hp, 2), ACT.Square).then_inc(hd_sq, 1)
                nc.scalar.activation(tiles(80, 1), tiles(16 + hp, 1), ACT.Square).then_inc(hd_sq, 1)
                nc.scalar.activation(tiles(81, 2), tiles(2 * hp, 2), ACT.Square).then_inc(hd_sq, 1)
                act.wait_ge(hd_ms, hp + 1)
                nc.scalar.activation(tiles(73, 4), tiles(73, 4), ACT.Sqrt).then_inc(hd_rt, 1)
                act.wait_ge(s_dve, hp + 1)
                for a in range(2):
                    for qb, (k0, k1) in enumerate(((0, 128), (128, 384))):
                        n = 2 * a + qb
                        ins = nc.scalar.activation(SC[:, a, k0:k1], SC[:, a, k0:k1], ACT.Exp, bias=SM[:, n:n + 1],
                                                   accum_out=SM[:, 4 + n:5 + n])
                ins.then_inc(p_act, 1)
                act.wait_ge(pt_mm, hp + 1)
                nc.scalar.activation(SC, PAIR["B"][:, :, 0:384], ACT.Copy).then_inc(pt_ev, 1)
                act.wait_ge(o_mm, hp + 1)
                nc.scalar.activation(yf[:, 2 * hp * T:(2 * hp + 2) * T], MISC, ACT.Copy).then_inc(o_ev, 1)
            split([(o_ev, 2), (o_ev, 4), (y_ev, 2), (y_ev, 4)])

            hi(30)
            hi(2)
            split([(free["B"], B_LAT + q + 1) for q in range(4)])
            hi(30)
            hi(2)
            norm(4, free["B"], B_LAT + 4 + 2)
            split([(yf_quad, 15 + q) for q in range(4)])
            ffn()
            assert c.unit.at == N_UNITS

        @block.vector
        def _(dve):
            c = Counts()

            def step(ins):
                c.chain.at += 1
                ins.then_inc(dve_chain, 1)
                dve.wait_ge(dve_chain, c.chain.value())

            def lo(n=1):
                for _ in range(n):
                    j, slot = c.sub.at % 2, c.unit.at % 4
                    dve.wait_ge(hi_done, c.sub.value(1))
                    nc.vector.tensor_tensor(WLO[j][:, :, :], RAW[slot][:, 2 * j:2 * j + 2, :],
                                            WHI[j][:, :, :].bitcast(F32), ALU.subtract).then_inc(lo_done, 1)
                    c.sub.at += 1
                    c.unit.at += j

            def ada(j, layer):
                slot = c.ada.at % 2
                dve.wait_ge(ada_in[slot], c.ada.value(2, times=16, over=2))
                for k in range(2):
                    kt = 2 * j + k
                    scalar = CA[:, 16 * layer + kt:16 * layer + kt + 1]
                    if kt == 0:
                        if c.ada_group.at:
                            dve.wait_ge(ada_red, c.ada_group.value())
                        ins = nc.vector.tensor_scalar(ACC, ADA[slot][:, k, :], scalar, None, ALU.mult)
                    else:
                        dve.wait_ge(ada_op, c.ada.value(0, times=2) + k)
                        ins = nc.vector.scalar_tensor_tensor(ACC, ADA[slot][:, k, :], scalar, ACC, ALU.mult, ALU.add)
                    ins.then_inc(ada_op, 1)
                c.ada.at += 1

            def ada_end():
                dve.wait_ge(ada_red, c.ada_group.value(1))
                at = c.ada_group.value(0, times=8)
                nc.vector.tensor_tensor(MOD[:, bass.ds(at, 8)], SMALL[:, 0:8], PRM[:, bass.ds(at, 8)], ALU.add)\
                    .then_inc(ada_bias, 1)
                c.ada_group.at += 1

            def split(n_quads=4, src=YF):
                for q in range(n_quads):
                    c.quad.at += 1
                    dve.wait_ge(h_hi, c.quad.value())
                    nc.vector.tensor_tensor(H[:, 4 * q:4 * q + 4, T:2 * T], src[:, 4 * q:4 * q + 4, :],
                                            H[:, 4 * q:4 * q + 4, 0:T].bitcast(F32), ALU.subtract).then_inc(h_quad, 1)

            def root(k):
                dve.wait_ge(ssq_ready, k + 1)
                nc.vector.tensor_scalar(RS[:, :], MISC[:, 0:T], 1.0 / D, EPS, ALU.mult, ALU.add).then_inc(ms_ready, 1)
                dve.wait_ge(rt_ready, k + 1)
                step(nc.vector.reciprocal(RS[:, :], RS[:, :]))

            def modulated(k, gain, shift, scale, groups):
                dve.wait_ge(ada_bias, groups)
                step(nc.vector.scalar_tensor_tensor(MC[:, :], MOD[:, scale:scale + 16], 1.0, PRM[:, gain:gain + 16],
                                                    ALU.add, ALU.mult))
                root(k)
                for q in range(4):
                    for t in range(4 * q, 4 * q + 4):
                        ins = nc.vector.scalar_tensor_tensor(YF[:, t, :], X[:, t, :], MC[:, t:t + 1], RS[:, :],
                                                             ALU.mult, ALU.mult)
                    step(ins)
                    for t in range(4 * q, 4 * q + 4):
                        ins = nc.vector.tensor_scalar(YF[:, t, :], YF[:, t, :], MOD[:, shift + t:shift + t + 1], None,
                                                      ALU.add)
                    ins.then_inc(yf_quad, 1)

            def residual(pair, g, gate):
                dve.wait_ge(pe_sub, c.sub.value(-2))
                for t in range(4):
                    ins = nc.vector.scalar_tensor_tensor(X[:, 4 * g + t, :], flat(pair)[:, t * T:(t + 1) * T],
                                                         MOD[:, gate + 4 * g + t:gate + 4 * g + t + 1],
                                                         X[:, 4 * g + t, :], ALU.mult, ALU.add)
                ins.then_inc(free[pair], 1)

            def win_body(layer=None, skip=0):
                for s in range(16):
                    if s >= skip:
                        lo()
                    for j in range(8):
                        if layer is not None and ADA_AFTER_16[j] == s:
                            ada(j, layer)
                    if s == 15 and layer is not None:
                        ada_end()

            def ffn(with_ada, gate):
                def product():
                    dve.wait_ge(pe_sub, c.sub.value(-2))
                    dve.wait_ge(gate_done, c.hid.value(1))
                    nc.vector.tensor_tensor(G, flat("B"), G, ALU.mult).then_inc(up_done, 1)

                def hidden():
                    dve.wait_ge(hid_hi, c.hid.value(1))
                    nc.vector.tensor_tensor(HID[:, :, T:2 * T], G.rearrange("p (a b) -> p a b", a=4),
                                            HID[:, :, 0:T].bitcast(F32), ALU.subtract).then_inc(hid_lo, 1)
                    c.hid.at += 1

                def add_down(n):
                    dve.wait_ge(pe_sub, c.sub.value(-2))
                    pair, part = "AC"[n % 2], yf[:, n * 1024:(n + 1) * 1024]
                    nc.vector.tensor_tensor(part, flat(pair), part, ALU.add).then_inc(free[pair], 1)

                def body(skip=0, subs=24, up=True, previous=True, layer=None):
                    after = ADA_AFTER_24 if subs == 24 else ADA_AFTER_16
                    for s in range(subs):
                        if s >= skip:
                            lo()
                        if s == 1 and up:
                            product()
                        if s == 1 and previous:
                            add_down(3)
                        if s == 2 and up:
                            hidden()
                        if s in (19, 21, 23):
                            add_down((s - 19) // 2)
                        for j in range(8):
                            if layer is not None and after[j] == s:
                                ada(j, layer)
                        if s == subs - 1 and layer is not None:
                            ada_end()

                body(skip=2, subs=16, up=False, previous=False, layer=0 if with_ada else None)
                step(nc.vector.memset(yf, 0.0))
                body(previous=False, layer=0 if with_ada else None)
                with dve.Fori(2, NF) as i:
                    c.enter(i - 2, unit=12, sub=24, hid=1, ada=8 * with_ada, ada_group=int(with_ada))
                    body(layer=1 if with_ada else None)
                c.leave(NF - 2)
                lo(2)
                product()
                add_down(3)
                hidden()
                for s in range(2, 8):
                    lo()
                    if s in (3, 5, 7):
                        add_down((s - 3) // 2)

            def ffn_end(gate, a_free, c_free, groups):
                part = yf[:, 3 * 1024:4 * 1024]
                nc.vector.tensor_tensor(part, flat("C"), part, ALU.add).then_inc(free["C"], 1)
                dve.wait_ge(free["A"], a_free)
                dve.wait_ge(free["C"], c_free)
                dve.wait_ge(ada_bias, groups)
                for t in range(KT):
                    nc.vector.scalar_tensor_tensor(X[:, t, :], YF[:, t, :], MOD[:, gate + t:gate + t + 1],
                                                   X[:, t, :], ALU.mult, ALU.add).then_inc(x_step, 1)

            nc.vector.memset(PRAW[:, 3, :], 0.0).then_inc(praw_zero, 1)
            dve.wait_ge(prm_t, 1)
            nc.vector.tensor_copy(PRM[:, :], MISC).then_inc(prm_ready, 1)
            for n in range(8):
                dve.wait_ge(x_turned, n + 1)
                nc.vector.tensor_copy(X[:, 2 * n:2 * n + 2, :].rearrange("p a b -> p (a b)"),
                                      PS[n // 2 % 2][:, n % 2, :]).then_inc(x_in, 1)
            dve.wait_ge(cact, 1)
            dve.wait_ge(prm_ready, 1)
            dve.wait_ge(x_in, 8)
            for g in range(4):
                for j in range(8):
                    ada(j, 0)
                if g == 3:
                    lo(2)
                ada_end()
            modulated(0, COL["g_norm_mix"], mod_at(0, 0), mod_at(0, 1), 4)
            split()
            win_body(0, skip=2)
            with dve.Fori(1, 3) as i:
                c.enter(i - 1, unit=8, sub=16, ada=8, ada_group=1)
                win_body(0)
            c.leave(2)
            lo(2)

            dve.wait_ge(free["A"], 3)
            dve.wait_ge(free["B"], 3)
            tap = lambda j, t: PRM[:, COL["w_conv"] + 8 * j + t:COL["w_conv"] + 8 * j + t + 1]
            for t in range(8):
                nc.vector.tensor_scalar(R[:, 24 + t, :], R[:, t, :], tap(3, t),
                                        PRM[:, COL["b_conv"] + t:COL["b_conv"] + t + 1], ALU.mult, ALU.add)\
                    .then_inc(conv_step, 1)
            for n, j in enumerate((2, 1, 0)):
                s = 3 - j
                dve.wait_ge(conv_step, 8 * (n + 1))
                for t in range(8):
                    nc.vector.scalar_tensor_tensor(R[:, 24 + t, s:T], R[:, t, 0:T - s], tap(j, t), R[:, 24 + t, s:T],
                                                   ALU.mult, ALU.add).then_inc(conv_step, 1)
            dve.wait_ge(lam_done, 1)
            step(nc.vector.scalar_tensor_tensor(SM[:, 0:8], PRM[:, COL["lru_lambda"]:COL["lru_lambda"] + 8], 0.0,
                                                SM[:, 8:16], ALU.min, ALU.subtract))
            nc.vector.tensor_scalar(SM[:, 0:8], SM[:, 0:8], 8.0, None, ALU.mult).then_inc(c8_done, 1)
            dve.wait_ge(rg_sig, 16)
            dve.wait_ge(conv_step, 32)
            step(nc.vector.tensor_tensor(tiles(40, 8), tiles(40, 8), tiles(24, 8), ALU.mult))
            dve.wait_ge(a_done, 8)
            step(nc.vector.tensor_tensor(tiles(48, 8), tiles(0, 8), tiles(0, 8), ALU.mult))
            dve.wait_ge(tanh_done, 8)
            nc.vector.scalar_tensor_tensor(tiles(48, 8), tiles(48, 8), 1.0, tiles(32, 8), ALU.add, ALU.mult)\
                .then_inc(m2_done, 1)
            dve.wait_ge(root_done, 1)
            step(nc.vector.tensor_tensor(tiles(40, 8), tiles(40, 8), tiles(32, 8), ALU.mult))
            for t in range(8):
                ins = nc.vector.tensor_tensor_scan(R[:, 24 + t, :], R[:, t, :], R[:, 40 + t, :], 0.0, ALU.mult, ALU.add)
            step(ins)
            dve.wait_ge(gelu_done, 1)
            for q in range(2):
                nc.vector.tensor_tensor(YF[:, 4 * q:4 * q + 4, :], R[:, 24 + 4 * q:28 + 4 * q, :],
                                        R[:, 8 + 4 * q:12 + 4 * q, :], ALU.mult).then_inc(yf_quad, 1)
            split()

            dve.wait_ge(ada_bias, 6)
            for g in range(4):
                for s in range(8):
                    if g or s >= 2:
                        lo()
                    if g and s == 1:
                        residual("BA"[g % 2], g - 1, mod_at(0, 2))
                    for j in range(8):
                        if g < 3 and ADA_AFTER_8[j] == s:
                            ada(j, 0)
                    if g < 3 and s == 7:
                        ada_end()
            lo(2)
            residual("B", 3, mod_at(0, 2))
            modulated(1, COL["g_norm_ffn"], mod_at(0, 3), mod_at(0, 4), 10)
            split()
            ffn(True, mod_at(0, 5))
            lo(2)
            dve.wait_ge(pe_sub, c.sub.value(-2))
            ffn_end(mod_at(0, 5), A_FFN1, C_FFN1, 12)
            dve.wait_ge(x_step, KT)
            nc.vector.tensor_copy(SM[:, 16:17], X[:, 0, 0:1]).then_inc(x_done, 1)
            root(2)
            for t in range(KT):
                ins = nc.vector.scalar_tensor_tensor(X[:, t, :], X[:, t, :],
                                                     PRM[:, COL["g_norm_final"] + t:COL["g_norm_final"] + t + 1],
                                                     RS[:, :], ALU.mult, ALU.mult)
            ins.then_inc(x_done, 1)
            dve.wait_ge(x_done, 2)
            modulated(3, COL["g_norm1_2"], mod_at(1, 0), mod_at(1, 1), 16)
            split()
            lo(14)
            with dve.Fori(0, 3) as i:
                c.enter(i, unit=8, sub=16, ada=8, ada_group=1)
                win_body(1)
            c.leave(3)
            with dve.Fori(0, 4) as i:
                c.enter(i, unit=8, sub=16)
                win_body()
            c.leave(4)
            lo(2)
            lo(2)

            dve.wait_ge(lat_ss, 2)
            nc.vector.tensor_scalar(tiles(76, 2), SMALL, 1.0 / 512, EPS, ALU.mult, ALU.add).then_inc(lat_ms, 1)
            dve.wait_ge(con_in, 16)
            dve.wait_ge(pos_in, 16)
            ang, turns, whole = KPE, tiles(85, 1), tiles(73, 1).bitcast(I32)
            step(nc.vector.tensor_copy(tiles(86, 1), whole))
            step(nc.vector.tensor_scalar(ang, tiles(86, 1), CON[:, FREQ:FREQ + 1], None, ALU.mult))
            c1 = 6.28125
            c2 = float(np.round((2 * np.pi - c1) * 2 ** 20) / 2 ** 20)
            c3 = float(2 * np.pi - c1 - c2)
            for n, (quarter, shift) in enumerate(((0.25, float(np.pi / 2)), (0.0, 0.0))):
                r = tiles(74 + n, 1)
                step(nc.vector.tensor_scalar(turns, ang, float(1 / (2 * np.pi)), quarter, ALU.mult, ALU.add))
                step(nc.vector.tensor_copy(whole, turns))
                step(nc.vector.tensor_copy(turns, whole))
                step(nc.vector.scalar_tensor_tensor(r, turns, -c1, ang, ALU.mult, ALU.add))
                step(nc.vector.scalar_tensor_tensor(r, turns, -c2, r, ALU.mult, ALU.add))
                step(nc.vector.scalar_tensor_tensor(r, turns, -c3, r, ALU.mult, ALU.add))
                step(nc.vector.tensor_scalar(r, r, shift, 3.1415925, ALU.add, ALU.min))
                nc.vector.tensor_scalar(r, r, -3.1415925, None, ALU.max).then_inc(ang_done, 1)
            dve.wait_ge(lat_rt, 1)
            step(nc.vector.reciprocal(tiles(76, 2), tiles(76, 2)))
            for n, name in enumerate(("g_q_latent_2", "g_kv_latent_2")):
                for t in range(4):
                    ins = nc.vector.scalar_tensor_tensor(R[:, 4 * n + t, :], R[:, 4 * n + t, :],
                                                         PRM[:, COL[name] + t:COL[name] + t + 1], tiles(76 + n, 1),
                                                         ALU.mult, ALU.mult)
            ins.then_inc(lat_ev, 1)
            dve.wait_ge(trig_done, 2)
            step(nc.vector.tensor_scalar(CS[1], CS[1], CON[:, SIGN:SIGN + 1], None, ALU.mult))

            both = lambda at: CON[:, at:at + 384].rearrange("p (a b) -> p a b", a=1).to_broadcast([P, 2, 384])
            for hp in range(4):
                dve.wait_ge(z_mm, hp + 1)
                step(nc.vector.scalar_tensor_tensor(three(78), PAIR["A"][:, :, 0:384], 128 ** -0.5, both(SB_ONE),
                                                    ALU.mult, ALU.mult))
                nc.vector.tensor_tensor(three(78), three(78), both(SB_NEG), ALU.add).then_inc(z_dve, 1)
                dve.wait_ge(z_act, hp + 1)
                nc.vector.scalar_tensor_tensor(tiles(84, 3), tiles(78, 3), 0.0, tiles(81, 3), ALU.max, ALU.add)\
                    .then_inc(sp_done, 1)
                dve.wait_ge(u_mm, hp + 1)
                nc.vector.tensor_tensor(three(84), three(78), PAIR["B"][:, :, 0:384], ALU.subtract).then_inc(w_dve, 1)
                dve.wait_ge(a_act, hp + 1)

            split(2, src=R)
            lo(14)

            col = lambda name: PRM[:, COL[name]:COL[name] + 1]
            step(nc.vector.memset(tiles(30, 2), 0.0))
            for hp in range(4):
                dve.wait_ge(hd_ss, hp + 1)
                nc.vector.tensor_scalar(tiles(73, 4), flat("C"), 1.0 / 192, EPS, ALU.mult, ALU.add).then_inc(hd_ms, 1)
                if hp == 0:
                    nc.vector.tensor_scalar(KPE, KPE, col("k_rope"), None, ALU.mult).then_inc(rope_in, 1)
                nc.vector.tensor_scalar(R[:, 16 + hp, :], R[:, 16 + hp, :], col("q_rope"), None, ALU.mult)\
                    .then_inc(rope_in, 1)
                dve.wait_ge(hd_rt, hp + 1)
                step(nc.vector.reciprocal(tiles(73, 4), tiles(73, 4)))
                for a in range(2):
                    nc.vector.scalar_tensor_tensor(R[:, 8 + 2 * hp + a, :], R[:, 8 + 2 * hp + a, :], col("g_q_head_2"),
                                                   R[:, 73 + a, :], ALU.mult, ALU.mult)
                    nc.vector.scalar_tensor_tensor(R[:, 2 * hp + a, :], R[:, 2 * hp + a, :], col("g_k_head_2"),
                                                   R[:, 75 + a, :], ALU.mult, ALU.mult)
                for n, (tile, half) in enumerate(((KPE, 0), (R[:, 16 + hp, :], 1))):
                    if n == 0 and hp:
                        continue
                    dve.wait_ge(rope_swap, hp + 2)
                    step(nc.vector.tensor_tensor(R[:, 29, :], SMALL[:, half * T:(half + 1) * T], CS[1], ALU.mult))
                    step(nc.vector.tensor_tensor(tile, tile, CS[0], ALU.mult))
                    step(nc.vector.tensor_tensor(tile, tile, R[:, 29, :], ALU.add))
                for a in range(2):
                    h = slice(64 * a, 64 * a + 64)
                    nc.vector.tensor_tensor(R[h, 16 + hp, :], R[h, 16 + hp, :], R[h, 73 + a, :], ALU.mult)
                    ins = nc.vector.tensor_tensor(R[h, 30 + a, :], R[h, 87, :], R[h, 75 + a, :], ALU.mult)
                ins.then_inc(hd_scaled, 1)
                dve.wait_ge(s_mm, hp + 1)
                step(nc.vector.scalar_tensor_tensor(SC, PAIR["A"][:, :, 0:384], 192 ** -0.5, both(MLA_NEG), ALU.mult,
                                                    ALU.add))
                for a in range(2):
                    for qb, (k0, k1) in enumerate(((0, 128), (128, 384))):
                        n = 2 * a + qb
                        ins = nc.vector.tensor_reduce(SM[:, n:n + 1], SC[:, a, k0:k1], AX_X, ALU.max)
                step(ins)
                nc.vector.tensor_scalar(SM[:, 0:4], SM[:, 0:4], -1.0, None, ALU.mult).then_inc(s_dve, 1)
                dve.wait_ge(p_act, hp + 1)
                step(nc.vector.reciprocal(SM[:, 8:12], SM[:, 4:8]))
                for a in range(2):
                    for qb, (k0, k1) in enumerate(((0, 128), (128, 384))):
                        n = 8 + 2 * a + qb
                        ins = nc.vector.tensor_scalar(SC[:, a, k0:k1], SC[:, a, k0:k1], SM[:, n:n + 1], None, ALU.mult)
                ins.then_inc(p_dve, 1)
            split()

            def merge_a(g):
                dve.wait_ge(pe_sub, c.sub.value(-2))
                nc.vector.tensor_tensor(tiles(4 * g, 4), flat("A"), tiles(32 + 4 * g, 4), ALU.mult)\
                    .then_inc(free["A"], 1)

            def merge_b(g):
                dve.wait_ge(pe_sub, c.sub.value(-2))
                gb = tiles(48 + 4 * g, 4)
                step(nc.vector.tensor_tensor(gb, flat("B"), gb, ALU.mult))
                dve.wait_ge(free["A"], A_LAT + g + 1)
                nc.vector.tensor_tensor(yf[:, 4 * g * T:4 * (g + 1) * T], tiles(4 * g, 4), gb, ALU.add)\
                    .then_inc(free["B"], 1)

            for g in range(4):
                for s in range(8):
                    if g or s >= 2:
                        lo()
                    if g and s == 1:
                        merge_b(g - 1)
                    if s == 5:
                        merge_a(g)
            lo(2)
            merge_b(3)
            split()
            for g in range(4):
                for s in range(8):
                    if g or s >= 2:
                        lo()
                    if g and s == 1:
                        residual("BA"[g % 2], g - 1, mod_at(1, 2))
            lo(2)
            residual("B", 3, mod_at(1, 2))
            modulated(4, COL["g_norm2_2"], mod_at(1, 3), mod_at(1, 4), 24)
            split()
            ffn(False, mod_at(1, 5))
            assert c.unit.at == N_UNITS
            dve.wait_ge(pe_sub, 2 * N_UNITS)
            ffn_end(mod_at(1, 5), A_END, C_END, 24)
            for n in range(8):
                dve.wait_ge(x_turned, 8 + n + 1)
                nc.vector.tensor_copy(yf[:, n * 512:(n + 1) * 512], PS[n // 2 % 2][:, n % 2, :]).then_inc(x_in, 1)

        @block.tensor
        def _(pe):
            c = Counts()

            def mm(o, a, b, start, stop=False):
                return nc.tensor.matmul(o, a, b, start=start, stop=stop, skip_group_check=True)

            def sub(pair, src, k0, first, last, kind="W", counted=True):
                j, used, o = c.sub.at % 2, c.all[pair], PAIR[pair]
                pe.wait_ge(lo_done, c.sub.value(1))
                if first and used.at:
                    pe.wait_ge(free[pair], used.value())
                for k in range(8 if kind == "K" else 0):
                    kk, n = k0 + k, slice(k % 4 * P, (k % 4 + 1) * P)
                    mm(o[:, 0, 0:T], WHI[j][:, k // 4, n], src[:, kk, 0:T], first and k == 0)
                    mm(o[:, 0, 0:T], WHI[j][:, k // 4, n], src[:, kk, T:2 * T], False)
                    ins = mm(o[:, 0, 0:T], WLO[j][:, k // 4, n], src[:, kk, 0:T], False, last and k == 7)
                for k in range(0 if kind == "K" else 2):
                    kk, begin, end = k0 + k, first and k == 0, last and k == 1
                    if kind == "W":
                        for t in range(4):
                            dst, n = o[:, t // 2, (t % 2) * T:(t % 2 + 1) * T], slice(t * P, (t + 1) * P)
                            mm(dst, WHI[j][:, k, n], src[:, kk, 0:T], begin and t % 2 == 0)
                            mm(dst, WHI[j][:, k, n], src[:, kk, T:2 * T], False)
                            ins = mm(dst, WLO[j][:, k, n], src[:, kk, 0:T], False, end)
                    if kind == "T":
                        for tb in range(2):
                            hi_x = src[:, kk, tb * P:(tb + 1) * P]
                            lo_x = src[:, kk, T + tb * P:T + (tb + 1) * P]
                            mm(o[:, tb, :], hi_x, WHI[j][:, k, :], begin)
                            mm(o[:, tb, :], lo_x, WHI[j][:, k, :], False)
                            ins = mm(o[:, tb, :], hi_x, WLO[j][:, k, :], False, end)
                ins.then_inc(pe_sub, 1)
                c.sub.at += 1
                used.at += last and counted

            def group(pair, src=H, k0=0, units=4, kind="W", quads=None, ada_after=None, counted=True):
                for s in range(2 * units):
                    if quads is not None and s % 2 == 0:
                        pe.wait_ge(h_quad, quads + s // 2 + 1)
                    sub(pair, src, k0 + 2 * s, s == 0, s == 2 * units - 1, kind, counted)
                    if s == ada_after:
                        ada_sum()

            def ada_sum():
                pe.wait_ge(ada_op, c.ada_group.value(1, times=16))
                if c.ada_group.at:
                    pe.wait_ge(ada_bias, c.ada_group.value())
                for j in range(8):
                    ins = mm(SMALL[:, j:j + 1], ACC[:, j * P:(j + 1) * P], ones[:, 0:1], True, True)
                ins.then_inc(ada_red, 1)
                c.ada_group.at += 1

            def square_sum(k):
                for q in range(4):
                    pe.wait_ge(sq_ready, 4 * k + q + 1)
                    for t in range(4 * q, 4 * q + 4):
                        ins = mm(MISC[:, 0:T], ones, YF[:, t, :], t == 0, t == KT - 1)
                ins.then_inc(ssq_ready, 1)

            def ffn(quads, with_ada):
                def gate(**more):
                    group("A", counted=False, **more)
                    c.gate.at += 1

                def up(**more):
                    if c.gate.at > 1:
                        pe.wait_ge(up_done, c.gate.value(-1))
                    group("B", counted=False, **more)

                def down(ada_after=None):
                    pe.wait_ge(hid_lo, c.hid.value(1))
                    pe.wait_ge(gate_done, c.gate.value())
                    for n in range(4):
                        group("AC"[n % 2], src=HID, units=1, ada_after=ada_after if n == 2 else None)
                    c.hid.at += 1

                ada_24 = 0 if with_ada else None
                gate(quads=quads)
                up(ada_after=5 if with_ada else None)
                gate()
                up()
                down(ada_24)
                with pe.Fori(2, NF) as i:
                    c.enter(i - 2, sub=24, A=2, C=2, hid=1, gate=1, ada_group=int(with_ada))
                    gate()
                    up()
                    down(ada_24)
                c.leave(NF - 2)
                down()

            pe.wait_ge(base_in, 16)
            pe.wait_ge(rows_in, 16 * len(rows_src))
            pe.wait_ge(praw_zero, 1)
            for n in range(4):
                ins = nc.tensor.transpose(MISC[:, n * P:(n + 1) * P], PRAW[:, n, :], ident)
            ins.then_inc(prm_t, 1)
            pe.wait_ge(x_rows, 32)
            for n in range(8):
                if n >= 4:
                    pe.wait_ge(x_in, n - 3)
                for k in range(2):
                    for tb in range(2):
                        at = tb * D + (2 * n + k) * P
                        ins = nc.tensor.transpose(PS[n // 2 % 2][:, n % 2, (2 * k + tb) * P:(2 * k + tb + 1) * P],
                                                  yf[:, at:at + P], ident)
                ins.then_inc(x_turned, 1)

            square_sum(0)
            for g in range(4):
                ada_sum()
            group("A", quads=Q_WIN1)
            group("B", ada_after=5)
            with pe.Fori(1, 3) as i:
                c.enter(i - 1, sub=16, A=1, B=1, ada_group=1)
                group("A")
                group("B", ada_after=5)
            c.leave(2)

            pe.wait_ge(free["A"], 3)
            pe.wait_ge(free["B"], 3)
            pe.wait_ge(conv_step, 32)
            pe.wait_ge(pool_chain, 1)
            pe.wait_ge(mix_w, 16 * 5)
            for kind in range(2):
                if kind == 1:
                    pe.wait_ge(ada_bias, 7)
                for t in range(8):
                    mm(eight(2 * kind, t), tiles(48 + 4 * kind, 4)[:, t * P:(t + 1) * P], R[:, 24 + t, :], True, True)\
                        .then_inc(rg_mm, 1)
            pe.wait_ge(pooled, 4)
            pe.wait_ge(rg_sig, 16)
            for t in range(8):
                g, oc = t // 2, t % 2
                for kc in range(2):
                    ins = mm(eight(0, t), tiles(56 + 2 * g + kc, 1)[:, oc * P:(oc + 1) * P], R[:, 16 + 2 * g + kc, :],
                             kc == 0, kc == 1)
                ins.then_inc(pool_mm, 1)
            pe.wait_ge(pool_ev, 8)

            for g in range(4):
                group("AB"[g % 2], quads=Q_WOUT1 if g == 0 else None, ada_after=5 if g < 3 else None)
            square_sum(1)
            ffn(Q_FFN1, True)
            square_sum(2)
            square_sum(3)

            group("A", quads=Q_WIN2)
            group("B")
            with pe.Fori(0, 2) as i:
                c.enter(i, sub=16, A=1, B=1, ada_group=1)
                group("A")
                group("B", ada_after=5)
            c.leave(2)
            group("A", kind="T")
            group("B", kind="T", ada_after=5)
            with pe.Fori(0, 4) as i:
                c.enter(i, sub=16, A=1, B=1)
                group("A")
                group("B")
            c.leave(4)
            sub("C", H, 0, True, False, "K")
            sub("C", H, 8, False, True, "K")

            pe.wait_ge(ada_bias, 24)
            for n in range(2):
                pe.wait_ge(lat_sq, n + 1)
                for t in range(4):
                    ins = mm(SMALL[:, n * T:(n + 1) * T], ones, YF[:, 4 * n + t, :], t == 0, t == 3)
                ins.then_inc(lat_ss, 1)

            pe.wait_ge(con_in, 16)
            pe.wait_ge(free["A"], A_WIN2)
            pe.wait_ge(free["B"], B_WIN2)
            heads_of = lambda hp: ((0, 2 * hp), (1, 2 * hp + 1))
            value = lambda tile, h, tb: rf[:, (tile + 4 * (h // 4)) * T + tb * 512 + h % 4 * P:][:, 0:P]
            for hp in range(4):
                for a, h in heads_of(hp):
                    q, k = R[:, 8 + h, :], R[:, 16 + h, :]
                    mm(PAIR["A"][:, a, 0:256], k[:, 0:P], q, True, True)
                    ins = mm(PAIR["A"][:, a, 256:384], k[:, P:T], q[:, P:T], True, True)
                ins.then_inc(z_mm, 1)
                pe.wait_ge(sp_done, hp + 1)
                for a, h in heads_of(hp):
                    s, o = three(84)[:, a, :], PAIR["B"][:, a, :]
                    mm(o[:, 0:256], CON[:, TRI:TRI + P], s[:, 0:256], True)
                    mm(o[:, 128:256], ones, s[:, 256:384], False, True)
                    ins = mm(o[:, 256:384], CON[:, TRI:TRI + P], s[:, 256:384], True, True)
                ins.then_inc(u_mm, 1)
                pe.wait_ge(a_act, hp + 1)
                if hp:
                    pe.wait_ge(y_ev, hp)
                for a, h in heads_of(hp):
                    w, o = three(81)[:, a, :], MISC[:, a * T:(a + 1) * T]
                    mm(o, value(24, h, 0), w[:, 0:256], True)
                    ins = mm(o[:, 128:256], value(24, h, 1), w[:, 256:384], False, True)
                ins.then_inc(y_mm, 1)

            for n, (pair, tile) in enumerate(LAT):
                pe.wait_ge(h_quad, Q_LAT + (1 if n < 3 else 2))
                group(pair, k0=0 if n < 3 else 4, units=1, kind="W" if n < 5 else "T")

            pe.wait_ge(free["A"], A_LAT)
            pe.wait_ge(free["B"], B_LAT)
            pe.wait_ge(free["C"], C_LAT)
            pe.wait_ge(y_ev, 4)
            for hp in range(4):
                pe.wait_ge(hd_sq, 1 + 3 * (hp + 1))
                for n, (nope, rope, half) in enumerate(((78, 80, EVEN), (79, 80, ODD), (81, 77, EVEN), (82, 77, EVEN))):
                    o = flat("C")[:, n * T:(n + 1) * T]
                    mm(o, ones, R[:, nope, :], True)
                    ins = mm(o, CON[:, half:half + P], R[:, rope, :], False, True)
                ins.then_inc(hd_ss, 1)
                if hp == 0:
                    pe.wait_ge(rope_in, 1)
                    mm(SMALL[:, 0:T], CON[:, PERM:PERM + P], KPE, True, True).then_inc(rope_swap, 1)
                pe.wait_ge(rope_in, hp + 2)
                mm(SMALL[:, T:2 * T], CON[:, PERM:PERM + P], R[:, 16 + hp, :], True, True).then_inc(rope_swap, 1)
                pe.wait_ge(hd_scaled, hp + 1)
                for a, h in heads_of(hp):
                    q, qr, k, kr = R[:, 8 + h, :], R[:, 16 + hp, :], R[:, h, :], R[:, 30 + a, :]
                    for qs, ks, at in ((slice(0, P), slice(0, P), slice(0, 128)),
                                       (slice(P, T), slice(0, T), slice(128, 384))):
                        mm(PAIR["A"][:, a, at], q[:, qs], k[:, ks], True)
                        ins = mm(PAIR["A"][:, a, at], qr[:, qs], kr[:, ks], False, True)
                ins.then_inc(s_mm, 1)
                pe.wait_ge(p_dve, hp + 1)
                for a in range(2):
                    for b in range(3):
                        n = slice(b * P, (b + 1) * P)
                        ins = nc.tensor.transpose(PAIR["B"][:, a, n], SC[:, a, n], ident)
                ins.then_inc(pt_mm, 1)
                pe.wait_ge(pt_ev, hp + 1)
                if hp:
                    pe.wait_ge(o_ev, hp)
                for a, h in heads_of(hp):
                    p, o = SC[:, a, :], MISC[:, a * T:(a + 1) * T]
                    mm(o, value(20, h, 0), p[:, 0:256], True)
                    ins = mm(o[:, 128:256], value(20, h, 1), p[:, 256:384], False, True)
                ins.then_inc(o_mm, 1)

            pe.wait_ge(h_quad, Q_PROJ + 4)
            with pe.Fori(0, 4) as i:
                c.enter(i, sub=8, A=1, B=1)
                group("A", units=2)
                group("B", units=2, k0=8)
            c.leave(4)
            for g in range(4):
                group("AB"[g % 2], quads=Q_WOUT2 if g == 0 else None)
            square_sum(4)
            ffn(Q_FFN2, False)
            assert c.sub.at == 2 * N_UNITS

            pe.wait_ge(x_step, 2 * KT)
            for n in range(8):
                if n >= 4:
                    pe.wait_ge(x_in, 8 + n - 3)
                for k in range(4):
                    ins = nc.tensor.transpose(PS[n // 2 % 2][:, n % 2, k * P:(k + 1) * P],
                                              X[:, 4 * (n % 4) + k, n // 4 * P:(n // 4 + 1) * P], ident)
                ins.then_inc(x_turned, 1)


def kernel(**inputs):
    import concourse.bacc as _bacc
    from concourse.bass_utils import run_bass_kernel_spmd as _run

    nc = _bacc.Bacc("TRN2", target_bir_lowering=False, num_devices=1)
    arrays = {}

    def dram(name, a):
        a = np.ascontiguousarray(a)
        arrays[f"in_{name}"] = a
        return nc.dram_tensor(f"in_{name}", a.shape, mybir.dt.from_np(a.dtype), kind="ExternalInput").ap()

    ktiles = lambda name: dram(name, np.asarray(inputs[name]).reshape(np.shape(inputs[name])[-2:]))\
        .rearrange("(k p) n -> p k n", p=P)
    weights = [ktiles(n) for n in ("w_in", "w_out", "w_ffn_gate", "w_ffn_up", "w_ffn_down", "w_in_2", "w_uq_2",
                                   "w_ukv_2", "w_proj_mla_2", "w_proj_sb_2", "w_out_2", "w_ffn_in_2",
                                   "w_ffn_out_2")]
    ada_w = [ktiles("w_ada"), ktiles("w_ada_2")]

    rows_src = []
    for name, n in PARAMS:
        source = {"q_rope": "g_q_head_2", "k_rope": "g_k_head_2"}.get(name, name)
        a = dram(f"row_{name}", np.asarray(inputs[source]).reshape(1, -1))
        width = a.shape[1] // n
        if width == P:
            r = 0
            while r < n:
                at = COL[name] + r
                m = min(n - r, P - at % P)
                rows_src.append((at // P, at % P, m, 0, P,
                                 a[:, r * P:(r + m) * P].rearrange("o (r n) -> (o r) n", n=P)))
                r += m
        else:
            at, parts = COL[name], ((0, 64), (64, 128)) if "rope" in name else ((0, 128),)
            for c0, c1 in parts:
                first = 128 if "rope" in name else 0
                rows_src.append((at // P, at % P, 1, c0, c1, a[:, first:first + c1 - c0]))

    gates = [dram(n, np.asarray(inputs[n])[0]).rearrange("(t e) i j -> e i t j", e=2) for n in ("w_rg_a", "w_rg_i")]
    w_pool = dram("w_pool", np.asarray(inputs["w_pool"])[0]).rearrange("g (k p) n -> p (g k) n", p=P)

    base = np.zeros((P, N_BASE), np.float32)
    base[:, IDENT:IDENT + P] = np.eye(P)
    base[:, ONES:ONES + P] = 1.0
    for g in range(4):
        for t in range(16):
            base[:, INV + 16 * g + t] = np.float32(1.0) / np.float32(min(t + 1, 2 << g))
    i = np.arange(P)
    row, col = i[:, None], i[None, :]
    con = np.zeros((P, N_CONST), np.float32)
    con[:, PERM:PERM + P] = (row // 32 ^ 1 == col // 32) & (row % 32 == col % 32)
    con[:, TRI:TRI + P] = row >= col
    con[:, EVEN:EVEN + P] = row < 64
    con[:, ODD:ODD + P] = row >= 64
    one = np.ones((P, 3 * P), np.float32)
    one[:, 0:P] = one[:, 2 * P:] = row < col
    con[:, SB_ONE:SB_ONE + 3 * P] = one
    con[:, SB_NEG:SB_NEG + 3 * P] = (one - 1) * np.float32(1e30)
    for at in (0, 2 * P):
        con[:, MLA_NEG + at:MLA_NEG + at + P] = np.where(col <= row, 0, -1e30)
    con[:, FREQ] = np.float32(10000.0) ** (-(i % 32).astype(np.float32) / np.float32(32))
    con[:, SIGN] = np.where(i % 64 < 32, -1, 1)

    out = nc.dram_tensor("out_0", (T, D), F32, kind="ExternalOutput").ap()
    build(nc, dram("x", np.asarray(inputs["x"])[0]), dram("positions", inputs["positions_2"]), rows_src, weights,
          ada_w, dram("base_const", base), dram("att_const", con), *gates, w_pool, out)
    r = _run(nc, [arrays], core_ids=[0])
    return r.results[0]["out_0"].reshape(1, T, D)
```

```python
import numpy as np
from contextlib import ExitStack

import concourse.bass as bass
from concourse import mybir

F32 = mybir.dt.float32
F32R = mybir.dt.float32r
I32 = mybir.dt.int32
ALU = mybir.AluOpType
ACT = mybir.ActivationFunctionType
AX_X = mybir.AxisListType.X

T = 256
D = 2048
P = 128
KT = D // P
D_FF = 5632
LRU = 1024
HEADS = 8
EPS = 1e-6
COLS = 512
ADA_COLS = 1024
NF = D_FF // COLS

PARAMS = [("b_ada", 96), ("b_ada_2", 96), ("c", 16), ("c_2", 16), ("g_norm_mix", 16), ("g_norm_ffn", 16),
          ("g_norm_final", 16), ("g_norm1_2", 16), ("g_norm2_2", 16), ("w_conv", 32), ("b_conv", 8),
          ("b_rg_a", 8), ("b_rg_i", 8), ("lru_lambda", 8), ("ls_pool", 8), ("g_q_latent_2", 4),
          ("g_kv_latent_2", 4), ("g_q_head_2", 1), ("g_k_head_2", 1), ("q_rope", 1), ("k_rope", 1)]
COL = {}
_at = 0
for _name, _n in PARAMS:
    COL[_name] = _at
    _at += _n
assert _at <= 512

PERM, TRI, EVEN, ODD, SB_ONE, SB_NEG, MLA_NEG, FREQ, SIGN, N_CONST = 0, 128, 256, 384, 512, 896, 1280, 1664, 1665, 1792
IDENT, ONES, INV, N_BASE = 0, 128, 256, 320

U_WIN1, U_WOUT1, U_FFN1, U_WIN2, U_KPE, U_GATES, U_LAT, U_PROJ, U_WOUT2, U_FFN2 = 0, 24, 40, 172, 204, 205, 237, 244, 260, 276
N_UNITS = 408

A_FFN1, B_FFN1, C_FFN1 = 3 + 2 + 2 * NF, 3 + 2, 2 * NF
A_WIN2, B_WIN2 = A_FFN1 + 8, B_FFN1 + 8
LAT = [("A", 8), ("B", 12), ("C", 16), ("A", 0), ("B", 4), ("C", 20), ("A", 24)]
A_LAT, B_LAT, C_LAT = A_WIN2 + 3, B_WIN2 + 2, C_FFN1 + 1 + 2
A_PROJ, B_PROJ, C_PROJ = A_LAT + 2, B_LAT + 2, C_LAT + 4
A_END, C_END = A_PROJ + 2 + 2 * NF, C_PROJ + 2 * NF

Q_WIN1, Q_WOUT1, Q_FFN1, Q_WIN2, Q_LAT, Q_PROJ_B, Q_PROJ_A, Q_WOUT2, Q_FFN2 = 0, 4, 8, 12, 16, 18, 20, 22, 26


class Count:

    def __init__(self):
        self.at, self.start, self.per, self.turn = 0, 0, 0, None

    def enter(self, turn, per):
        self.start, self.per, self.turn = self.at, per, turn

    def leave(self, turns):
        assert self.at - self.start == self.per, (self.at - self.start, self.per)
        self.at, self.per = self.start + self.per * turns, 0

    def value(self, more=0, times=1, over=1):
        n = (self.at + more) // over * times
        if not self.per:
            return n
        assert self.per % over == 0
        return self.turn * (self.per // over * times) + n


class Counts:

    def __init__(self):
        self.unit, self.sub = Count(), Count()
        self.A, self.B, self.C = Count(), Count(), Count()
        self.ada, self.ada_group = Count(), Count()
        self.gate, self.hid = Count(), Count()
        self.quad, self.chain = Count(), Count()
        self.all = dict(unit=self.unit, sub=self.sub, A=self.A, B=self.B, C=self.C, ada=self.ada,
                        ada_group=self.ada_group, gate=self.gate, hid=self.hid, quad=self.quad, chain=self.chain)

    def enter(self, turn, **per):
        for name, count in self.all.items():
            count.enter(turn, per.get(name, 0))

    def leave(self, turns):
        for count in self.all.values():
            count.leave(turns)


ADA_AFTER = {n: [k * last // 15 for k in range(KT)] for n, last in ((16, 12), (24, 19), (8, 4))}


def build(nc, x, positions, rows_src, weights, ada_w, base_const, att_const, rg_a, rg_i, w_pool, out):
    w_in, w_out, w_gate, w_up, w_down, w_in2, w_uq, w_ukv, w_pa, w_pb, w_out2, w_ffin2, w_ffout2 = weights
    with ExitStack() as ctx:
        here = [-(-nc.sbuf_base // 64) * 64]

        def place(name, shape, dt=F32):
            n = 4
            for s in shape[1:]:
                n *= s
            t = nc.alloc_sbuf_tensor_at(name, shape, dt, offset=here[0])
            here[0] += n
            return t

        arena = here[0]
        R = place("R", [P, 88, T])
        end = here[0]
        here[0] = arena
        HID = place("HID", [P, 4, 2 * T], F32R)
        here[0] = end
        X = place("X", [P, KT, T])
        H = place("H", [P, KT, 2 * T], F32R)
        YF = place("YF", [P, KT, T])
        RAW = [place(f"RAW{i}", [P, 4, COLS]) for i in range(4)]
        WHI = [place(f"WHI{i}", [P, 2, COLS], F32R) for i in range(2)]
        WLO = [place(f"WLO{i}", [P, 2, COLS], F32R) for i in range(2)]
        PRM = place("PRM", [P, 512])
        MOD = place("MOD", [P, 192])
        BASE = place("BASE", [P, N_BASE])
        RS = place("RS", [P, T])
        CA = place("CA", [P, 32])
        MC = place("MC", [P, 16])
        SM = place("SM", [P, 32])
        rf = R[:, :, :].rearrange("p a b -> p (a b)")
        yf = YF[:, :, :].rearrange("p a b -> p (a b)")
        ident, ones = BASE[:, IDENT:IDENT + P], BASE[:, ONES:ONES + P]
        tiles = lambda a, n: rf[:, a * T:(a + n) * T]
        ADA = [tiles(64 + 4 * i, 4) for i in range(4)]
        ACC = tiles(80, 4)
        G = tiles(84, 4)
        PRAW = R[:, 0:2, :].rearrange("p a (b c) -> p (a b) c", c=P)
        CON = tiles(64, 7)
        CS = [tiles(71, 1), tiles(72, 1)]

        PS = [ctx.enter_context(nc.psum_tensor(f"PS{i}", [P, 2, 512], F32)) for i in range(4)]
        PAIR = dict(A=PS[0], B=PS[1], C=PS[2])
        flat = lambda pair: PAIR[pair][:, :, :].rearrange("p a b -> p (a b)")
        SMALL, MISC = PS[3][:, 0, :], PS[3][:, 1, :]

        mod_at = lambda layer, which: 96 * layer + 16 * which
        eight = lambda first, t: PS[first + t // 4][:, t // 2 % 2, t % 2 * T:(t % 2 + 1) * T]
        three = lambda t: tiles(t, 3).rearrange("p (a b) -> p a b", a=2)
        KPE = tiles(87, 1)
        SC = three(83)

        sem = lambda n: ctx.enter_context(nc.semaphore(n))
        raw_in = [sem(f"raw_in{i}") for i in range(4)]
        hi_done, lo_done, pe_sub = sem("hi_done"), sem("lo_done"), sem("pe_sub")
        free = {p: sem(f"free_{p}") for p in "ABC"}
        ada_in = [sem(f"ada_in{i}") for i in range(4)]
        ada_op, ada_red, ada_bias = sem("ada_op"), sem("ada_red"), sem("ada_bias")
        yf_quad, h_hi, h_quad = sem("yf_quad"), sem("h_hi"), sem("h_quad")
        act_chain, dve_chain, pool_chain = sem("act_chain"), sem("dve_chain"), sem("pool_chain")
        mix_w, base_in, con_in, pos_in, rows_in, x_rows = (
            sem(n) for n in ("mix_w", "base_in", "con_in", "pos_in", "rows_in", "x_rows"))
        prm_t, prm_ready, praw_zero, cact, x_turned, x_in = (
            sem(n) for n in ("prm_t", "prm_ready", "praw_zero", "cact", "x_turned", "x_in"))
        sq_ready, ssq_ready, ms_ready, rt_ready = (sem(n) for n in ("sq_ready", "ssq_ready", "ms_ready", "rt_ready"))
        x_done, x_step = sem("x_done"), sem("x_step")
        gate_done, up_done, hid_hi, hid_lo = sem("gate_done"), sem("up_done"), sem("hid_hi"), sem("hid_lo")
        conv_step, lam_done, c8_done, rg_mm, rg_sig, a_done, tanh_done, gelu_done, m2_done, root_done = (
            sem(n) for n in ("conv_step", "lam_done", "c8_done", "rg_mm", "rg_sig", "a_done", "tanh_done",
                             "gelu_done", "m2_done", "root_done"))
        pooled, pool_mm, pool_ev = sem("pooled"), sem("pool_mm"), sem("pool_ev")
        lat_sq, lat_ss, lat_ms, lat_rt, lat_ev, ang_done, trig_done = (
            sem(n) for n in ("lat_sq", "lat_ss", "lat_ms", "lat_rt", "lat_ev", "ang_done", "trig_done"))
        z_mm, z_dve, z_act, sp_done, u_mm, w_dve, a_act, y_mm, y_ev = (
            sem(n) for n in ("z_mm", "z_dve", "z_act", "sp_done", "u_mm", "w_dve", "a_act", "y_mm", "y_ev"))
        hd_sq, hd_ss, hd_ms, hd_rt, rope_in, rope_swap, hd_scaled = (
            sem(n) for n in ("hd_sq", "hd_ss", "hd_ms", "hd_rt", "rope_in", "rope_swap", "hd_scaled"))
        s_mm, s_dve, p_act, p_dve, pt_mm, pt_ev, o_mm, o_ev = (
            sem(n) for n in ("s_mm", "s_dve", "p_act", "p_dve", "pt_mm", "pt_ev", "o_mm", "o_ev"))
        s_out = sem("s_out")

        ctx.enter_context(nc.allow_non_contiguous_dma("column blocks of the weights"))
        block = ctx.enter_context(nc.Block())

        @block.sync
        def _(sp):
            c = Counts()

            def slot_free():
                if c.unit.at >= 4:
                    sp.wait_ge(lo_done, c.unit.value(-3, times=2))
                c.unit.at += 1
                return (c.unit.at - 1) % 4

            def load(w, k, col):
                slot = slot_free()
                sp.dma_start(RAW[slot][:, :, :], w[:, bass.ds(k, 4), bass.ds(col, COLS)]).then_inc(raw_in[slot], 16)

            def group(w, col, kq=4):
                for q in range(kq):
                    load(w, 4 * q, col)

            def ffn(wg, gcol, wu, ucol, wd):
                def gate_up(i):
                    group(wg, gcol + i * COLS)
                    group(wu, ucol + i * COLS)

                def down(i):
                    for n in range(4):
                        load(wd, i * 4, n * COLS)

                gate_up(0)
                gate_up(1)
                down(0)
                with sp.Fori(2, NF) as i:
                    c.enter(i - 2, unit=12)
                    gate_up(i)
                    down(i - 1)
                c.leave(NF - 2)
                down(NF - 1)

            sp.dma_start(yf[:, 0:D], x[0:P, :]).then_inc(x_rows, 16)
            sp.dma_start(yf[:, D:2 * D], x[P:2 * P, :]).then_inc(x_rows, 16)
            group(w_in, 0)
            group(w_in, COLS)
            with sp.Fori(1, 3) as i:
                c.enter(i - 1, unit=8)
                group(w_in, i * 1024)
                group(w_in, i * 1024 + COLS)
            c.leave(2)
            for g in range(4):
                group(w_out, g * COLS)
            ffn(w_gate, 0, w_up, 0, w_down)
            group(w_in2, 0)
            group(w_in2, 512)
            OFF = 2 * 512 + 64
            with sp.Fori(0, 3) as i:
                c.enter(i, unit=8)
                group(w_in2, OFF + i * 1024)
                group(w_in2, OFF + 512 + i * 1024)
            c.leave(3)

            slot = slot_free()
            dst = RAW[slot][:, :, :].rearrange("p a (b n) -> p (a b) n", n=P)
            for half in (0, 64):
                sp.dma_start(dst[:, :, half:half + 64], w_in2[:, :, 1024:1088]).then_inc(raw_in[slot], 16)
            with sp.Fori(3, 7) as i:
                c.enter(i - 3, unit=8)
                group(w_in2, OFF + i * 1024)
                group(w_in2, OFF + 512 + i * 1024)
            c.leave(4)

            def heads(w, per, at, n, first, count):
                slot = slot_free()
                for k in range(4):
                    sp.dma_start(RAW[slot][:, k, :].rearrange("p (h n) -> p h n", n=n),
                                 w[:, k, :].rearrange("p (h m) -> p h m", m=per)[:, first:first + count, at:at + n])\
                        .then_inc(raw_in[slot], 16)

            heads(w_uq, 192, 0, 128, 0, 4)
            heads(w_uq, 192, 0, 128, 4, 4)
            heads(w_uq, 192, 128, 64, 0, 8)
            heads(w_ukv, 256, 0, 128, 0, 4)
            heads(w_ukv, 256, 0, 128, 4, 4)
            heads(w_ukv, 256, 128, 128, 0, 4)
            heads(w_ukv, 256, 128, 128, 4, 4)
            for w in (w_pb, w_pa):
                with sp.Fori(0, 2) as i:
                    c.enter(i, unit=4)
                    group(w, i * 2 * COLS, 2)
                    group(w, i * 2 * COLS + COLS, 2)
                c.leave(2)
            for g in range(4):
                group(w_out2, g * COLS)
            ffn(w_ffin2, 0, w_ffin2, D_FF, w_ffout2)
            assert c.unit.at == N_UNITS
            for tb in range(2):
                sp.wait_ge(x_in, 12 + 4 * tb)
                sp.dma_start(out[tb * P:(tb + 1) * P, :], yf[:, tb * D:(tb + 1) * D]).then_inc(s_out, 16)
            sp.wait_ge(s_out, 32)

        EXTRA = {U_KPE: 1, **{U_LAT + n: 3 for n in range(7)}}

        def landed(eng, c):
            n = c.unit.at
            extra = sum(v for u, v in EXTRA.items() if u % 4 == n % 4 and u <= n)
            eng.wait_ge(raw_in[n % 4], c.unit.value(0, times=16, over=4) + 16 * (1 + extra))

        @block.gpsimd
        def _(pool):
            c = Counts()

            def ada(layer, col):
                for k in range(KT):
                    slot = c.ada.at % 4
                    if c.ada.at >= 4:
                        pool.wait_ge(ada_op, c.ada.value(-3))
                    pool.dma_start(ADA[slot], ada_w[layer][:, k, bass.ds(col, ADA_COLS)])\
                        .then_inc(ada_in[slot], 16)
                    c.ada.at += 1

            def step(ins):
                c.chain.at += 1
                ins.then_inc(pool_chain, 1)
                pool.wait_ge(pool_chain, c.chain.value())

            for g in range(4):
                ada(0, g * ADA_COLS)
            step(pool.memset(tiles(48, 8), 0.0))
            for n, w in enumerate((rg_a, rg_i)):
                dst = tiles(48 + 4 * n, 4).rearrange("p (t j) -> p t j", j=P)
                for half in range(2):
                    pool.dma_start(dst[64 * half:64 * half + 64, :, 64 * half:64 * half + 64], w[half])\
                        .then_inc(mix_w, 16)
            pool.dma_start(tiles(56, 8).rearrange("p (g n) -> p g n", n=T), w_pool).then_inc(mix_w, 16)
            with pool.Fori(0, 3) as i:
                c.enter(i, ada=KT)
                ada(0, i * ADA_COLS + 4 * ADA_COLS)
            c.leave(3)

            pool.wait_ge(base_in, 16)
            pool.wait_ge(free["A"], 3)
            pool.wait_ge(free["B"], 3)
            sums = [YF[:, 12:14, :], YF[:, 14:16, :]]
            for g in range(4):
                src = R[:, 16 + 2 * g:18 + 2 * g, :]
                cur, w = src, 2 << g
                for level in range(g + 1):
                    dst, s = sums[level % 2], 1 << level
                    step(pool.tensor_copy(dst[:, :, 0:s], cur[:, :, 0:s]))
                    step(pool.tensor_tensor(dst[:, :, s:T], cur[:, :, s:T], cur[:, :, 0:T - s], ALU.add))
                    cur = dst
                inv = BASE[:, INV + 16 * g:INV + 16 * g + w]
                for a in range(2):
                    step(pool.tensor_tensor(cur[:, a, 0:w], cur[:, a, 0:w], inv, ALU.mult))
                step(pool.tensor_scalar(cur[:, :, w:T], cur[:, :, w:T], 1.0 / w, 1.0, ALU.mult, ALU.mult))
                pool.tensor_tensor(src, cur, src, ALU.subtract).then_inc(pooled, 1)
                pool.wait_ge(pooled, g + 1)

            for b in (7, 8, 9, 10, 11):
                ada(0, b * ADA_COLS)
            with pool.Fori(0, 12) as i:
                c.enter(i, ada=KT)
                ada(1, i * ADA_COLS)
            c.leave(12)
            pool.wait_ge(ada_op, c.ada.value())
            pool.dma_start(CON, att_const).then_inc(con_in, 16)
            pool.dma_start(tiles(73, 1).bitcast(I32), positions.to_broadcast([P, T])).then_inc(pos_in, 16)

        @block.scalar
        def _(act):
            c = Counts()

            def step(ins):
                c.chain.at += 1
                ins.then_inc(act_chain, 1)
                act.wait_ge(act_chain, c.chain.value())

            def hi(n=1):
                for _ in range(n):
                    j, slot = c.sub.at % 2, c.unit.at % 4
                    if j == 0:
                        landed(act, c)
                    if c.sub.at >= 2:
                        act.wait_ge(pe_sub, c.sub.value(-1))
                    nc.scalar.activation(WHI[j][:, :, :], RAW[slot][:, 2 * j:2 * j + 2, :], ACT.Copy)\
                        .then_inc(hi_done, 1)
                    c.sub.at += 1
                    c.unit.at += j

            def copy_out(pair, dst, func=ACT.Copy):
                act.wait_ge(pe_sub, c.sub.value(-2))
                nc.scalar.activation(dst, flat(pair), func).then_inc(free[pair], 1)

            def split(waits, src=YF, first=0):
                for q, (s, v) in enumerate(waits, first):
                    act.wait_ge(s, v)
                    nc.scalar.activation(H[:, 4 * q:4 * q + 4, 0:T], src[:, 4 * q:4 * q + 4, :], ACT.Copy)\
                        .then_inc(h_hi, 1)

            def norm(k, ready, value):
                act.wait_ge(ready, value)
                for q in range(4):
                    nc.scalar.activation(YF[:, 4 * q:4 * q + 4, :], X[:, 4 * q:4 * q + 4, :], ACT.Square)\
                        .then_inc(sq_ready, 1)
                act.wait_ge(ms_ready, k + 1)
                nc.scalar.activation(RS[:, :], RS[:, :], ACT.Sqrt).then_inc(rt_ready, 1)

            def win_body(tile, skip=0, before=ACT.Copy, func=ACT.Copy):
                at = lambda n: rf[:, bass.ds((tile + n) * T, 4 * T)]
                for s in range(skip, 16):
                    hi()
                    if s == 1:
                        copy_out("B", at(-4), before)
                    if s == 9:
                        copy_out("A", at(0), func)

            def ffn():
                def gate():
                    act.wait_ge(pe_sub, c.sub.value(-2))
                    if c.gate.at:
                        act.wait_ge(hid_lo, c.gate.value())
                    nc.scalar.activation(G, flat("A"), ACT.Silu).then_inc(gate_done, 1)
                    c.gate.at += 1

                def hidden():
                    act.wait_ge(up_done, c.hid.value(1))
                    nc.scalar.activation(HID[:, :, 0:T], G.rearrange("p (a b) -> p a b", a=4), ACT.Copy)\
                        .then_inc(hid_hi, 1)
                    c.hid.at += 1

                def body(skip=0, subs=24, previous=True):
                    for s in range(skip, subs):
                        hi()
                        if s == 1 and previous:
                            hidden()
                        if s == 9:
                            gate()

                body(skip=2, subs=16, previous=False)
                body()
                with act.Fori(2, NF) as i:
                    c.enter(i - 2, unit=12, sub=24, hid=1, gate=1)
                    body()
                c.leave(NF - 2)
                hi(2)
                hidden()
                hi(6)

            for block_at, r, n, c0, c1, src in rows_src:
                if block_at == 3:
                    act.wait_ge(praw_zero, 1)
                act.dma_start(PRAW[r:r + n, block_at, c0:c1], src).then_inc(rows_in, 16)
            act.dma_start(BASE[:, :], base_const).then_inc(base_in, 16)
            act.wait_ge(prm_ready, 1)
            nc.scalar.activation(CA[:, :], PRM[:, COL["c"]:COL["c"] + 32], ACT.Silu).then_inc(cact, 1)

            hi(2)
            norm(0, x_in, 8)
            split([(yf_quad, q + 1) for q in range(4)])
            for s in range(2, 16):
                hi()
                if s == 9:
                    copy_out("A", tiles(0, 4))
            with act.Fori(1, 3) as i:
                c.enter(i - 1, unit=8, sub=16)
                win_body(i * 8)
            c.leave(2)
            hi(2)
            copy_out("B", tiles(20, 4))

            soft = SM[:, 8:16]
            step(nc.scalar.activation(soft, PRM[:, COL["lru_lambda"]:COL["lru_lambda"] + 8], ACT.Abs))
            step(nc.scalar.activation(soft, soft, ACT.Exp, scale=-1.0))
            nc.scalar.activation(soft, soft, ACT.Ln, bias=1.0).then_inc(lam_done, 1)
            for kind, name in enumerate(("b_rg_a", "b_rg_i")):
                for t in range(8):
                    act.wait_ge(rg_mm, 8 * kind + t // 2 * 2 + 2)
                    nc.scalar.activation(R[:, 32 + 8 * kind + t, :], eight(2 * kind, t), ACT.Sigmoid,
                                         bias=PRM[:, COL[name] + t:COL[name] + t + 1]).then_inc(rg_sig, 1)
            act.wait_ge(c8_done, 1)
            act.wait_ge(rg_sig, 16)
            for t in range(8):
                nc.scalar.activation(R[:, t, :], R[:, 32 + t, :], ACT.Exp, scale=SM[:, t:t + 1]).then_inc(a_done, 1)
            act.wait_ge(a_done, 8)
            for t in range(8):
                nc.scalar.activation(R[:, 32 + t, :], R[:, 32 + t, :], ACT.Tanh, scale=SM[:, t:t + 1])\
                    .then_inc(tanh_done, 1)
            act.wait_ge(free["A"], 3)
            act.wait_ge(free["B"], 2)
            nc.scalar.activation(tiles(8, 8), tiles(8, 8), ACT.Gelu_apprx_tanh).then_inc(gelu_done, 1)
            act.wait_ge(m2_done, 1)
            nc.scalar.activation(tiles(32, 8), tiles(48, 8), ACT.Sqrt, scale=-1.0).then_inc(root_done, 1)
            for t in range(8):
                act.wait_ge(pool_mm, t // 2 * 2 + 2)
                nc.scalar.activation(YF[:, 8 + t, :], eight(0, t), ACT.Copy,
                                     scale=PRM[:, COL["ls_pool"] + t:COL["ls_pool"] + t + 1]).then_inc(pool_ev, 1)
            split([(yf_quad, 5), (yf_quad, 6), (pool_ev, 4), (pool_ev, 8)])

            hi(30)
            hi(2)
            norm(1, free["B"], 5)
            split([(yf_quad, 7 + q) for q in range(4)])
            ffn()
            hi(2)
            norm(2, x_done, 1)
            norm(3, x_done, 2)
            split([(yf_quad, 11 + q) for q in range(4)])
            for s in range(2, 16):
                hi()
                if s == 9:
                    copy_out("A", tiles(0, 4))
            with act.Fori(0, 2) as i:
                c.enter(i, unit=8, sub=16)
                win_body(i * 8 + 8)
            c.leave(2)
            for s in range(16):
                hi()
                if s == 1:
                    copy_out("B", tiles(20, 4))
                if s in (3, 5):
                    n = (s - 3) // 2
                    nc.scalar.activation(YF[:, 4 * n:4 * n + 4, :], R[:, 4 * n:4 * n + 4, :], ACT.Square)\
                        .then_inc(lat_sq, 1)
                if s == 9:
                    copy_out("A", tiles(24, 4))
                if s == 11:
                    act.wait_ge(lat_ms, 1)
                    nc.scalar.activation(YF[:, 8:10, :], YF[:, 8:10, :], ACT.Sqrt).then_inc(lat_rt, 1)
            hi(2)
            copy_out("B", tiles(28, 4))

            for hp in range(4):
                for s in range(16):
                    hi()
                    if s == 1 and hp == 0:
                        act.wait_ge(pe_sub, c.sub.value(-2))
                        nc.scalar.activation(KPE, PAIR["C"][:, 0, 0:T], ACT.Copy).then_inc(free["C"], 1)
                    if s == 1 and hp:
                        copy_out("B", tiles(8 * hp + 28, 4), ACT.Sigmoid)
                    if s == 4:
                        act.wait_ge(z_dve, hp + 1)
                        step(nc.scalar.activation(tiles(81, 3), tiles(78, 3), ACT.Abs))
                        step(nc.scalar.activation(tiles(81, 3), tiles(81, 3), ACT.Exp, scale=-1.0))
                        nc.scalar.activation(tiles(81, 3), tiles(81, 3), ACT.Ln, bias=1.0).then_inc(z_act, 1)
                    if s == 9:
                        copy_out("A", tiles(8 * hp + 32, 4), ACT.Sigmoid)
                        act.wait_ge(w_dve, hp + 1)
                        nc.scalar.activation(tiles(81, 3), tiles(84, 3), ACT.Exp).then_inc(a_act, 1)
                    if s == 12 and hp == 0:
                        act.wait_ge(ang_done, 2)
                        for n in range(2):
                            nc.scalar.activation(CS[n], tiles(74 + n, 1), ACT.Sin).then_inc(trig_done, 1)
                    if s == 13:
                        act.wait_ge(y_mm, hp + 1)
                        nc.scalar.activation(yf[:, (8 + 2 * hp) * T:(10 + 2 * hp) * T], PAIR["C"][:, 0, :], ACT.Copy)\
                            .then_inc(y_ev, 1)
            hi(2)
            copy_out("B", tiles(60, 4), ACT.Sigmoid)

            split([(lat_ev, 1), (lat_ev, 1)], src=R)
            for n in range(7):
                hi(2)
                copy_out(LAT[n][0], tiles(LAT[n][1], 4))
                if n in (1, 2):
                    split([(y_ev, 2 * n)], first=n + 1)
            act.wait_ge(free["A"], A_LAT)
            act.wait_ge(free["B"], B_LAT)
            act.wait_ge(free["C"], C_LAT)
            nc.scalar.activation(tiles(77, 1), KPE, ACT.Square).then_inc(hd_sq, 1)
            for hp in range(4):
                if hp:
                    act.wait_ge(hd_ss, hp)
                nc.scalar.activation(tiles(78, 2), tiles(8 + 2 * hp, 2), ACT.Square).then_inc(hd_sq, 1)
                nc.scalar.activation(tiles(80, 1), tiles(16 + hp, 1), ACT.Square).then_inc(hd_sq, 1)
                nc.scalar.activation(tiles(81, 2), tiles(2 * hp, 2), ACT.Square).then_inc(hd_sq, 1)
                act.wait_ge(hd_ms, hp + 1)
                nc.scalar.activation(tiles(73, 4), tiles(73, 4), ACT.Sqrt).then_inc(hd_rt, 1)
                hi(2)
                act.wait_ge(s_dve, hp + 1)
                for a in range(2):
                    for qb, (k0, k1) in enumerate(((0, 128), (128, 384))):
                        n = 2 * a + qb
                        ins = nc.scalar.activation(SC[:, a, k0:k1], SC[:, a, k0:k1], ACT.Exp, bias=SM[:, n:n + 1],
                                                   accum_out=SM[:, 4 + n:5 + n])
                ins.then_inc(p_act, 1)
                hi(2)
                act.wait_ge(pt_mm, hp + 1)
                nc.scalar.activation(SC, PAIR["B"][:, :, 0:384], ACT.Copy).then_inc(pt_ev, 1)
                act.wait_ge(o_mm, hp + 1)
                nc.scalar.activation(yf[:, 2 * hp * T:(2 * hp + 2) * T], MISC, ACT.Copy).then_inc(o_ev, 1)
            split([(o_ev, 2), (o_ev, 4)])

            hi(14)
            hi(2)
            split([(free["A"], A_LAT + 1), (free["B"], B_LAT + 1), (free["A"], A_LAT + 2), (free["B"], B_LAT + 2)])
            hi(30)
            hi(2)
            norm(4, free["B"], B_PROJ + 2)
            split([(yf_quad, 15 + q) for q in range(4)])
            ffn()
            assert c.unit.at == N_UNITS

        @block.vector
        def _(dve):
            c = Counts()

            def step(ins):
                c.chain.at += 1
                ins.then_inc(dve_chain, 1)
                dve.wait_ge(dve_chain, c.chain.value())

            def lo(n=1):
                for _ in range(n):
                    j, slot = c.sub.at % 2, c.unit.at % 4
                    dve.wait_ge(hi_done, c.sub.value(1))
                    nc.vector.tensor_tensor(WLO[j][:, :, :], RAW[slot][:, 2 * j:2 * j + 2, :],
                                            WHI[j][:, :, :].bitcast(F32), ALU.subtract).then_inc(lo_done, 1)
                    c.sub.at += 1
                    c.unit.at += j

            def ada(kt, layer):
                slot = c.ada.at % 4
                dve.wait_ge(ada_in[slot], c.ada.value(4, times=16, over=4))
                scalar = CA[:, 16 * layer + kt:16 * layer + kt + 1]
                if kt == 0:
                    if c.ada_group.at:
                        dve.wait_ge(ada_red, c.ada_group.value())
                    ins = nc.vector.tensor_scalar(ACC, ADA[slot], scalar, None, ALU.mult)
                else:
                    dve.wait_ge(ada_op, c.ada.value())
                    ins = nc.vector.scalar_tensor_tensor(ACC, ADA[slot], scalar, ACC, ALU.mult, ALU.add)
                ins.then_inc(ada_op, 1)
                c.ada.at += 1

            def ada_beside(layer, s, subs):
                for kt in range(KT):
                    if ADA_AFTER[subs][kt] == s:
                        ada(kt, layer)
                if s == subs - 1:
                    ada_end()

            def ada_end():
                dve.wait_ge(ada_red, c.ada_group.value(1))
                at = c.ada_group.value(0, times=8)
                nc.vector.tensor_tensor(MOD[:, bass.ds(at, 8)], SMALL[:, 0:8], PRM[:, bass.ds(at, 8)], ALU.add)\
                    .then_inc(ada_bias, 1)
                c.ada_group.at += 1

            def split(n_quads=4, src=YF, first=0):
                for q in range(first, first + n_quads):
                    c.quad.at += 1
                    dve.wait_ge(h_hi, c.quad.value())
                    nc.vector.tensor_tensor(H[:, 4 * q:4 * q + 4, T:2 * T], src[:, 4 * q:4 * q + 4, :],
                                            H[:, 4 * q:4 * q + 4, 0:T].bitcast(F32), ALU.subtract).then_inc(h_quad, 1)

            def root(k):
                dve.wait_ge(ssq_ready, k + 1)
                nc.vector.tensor_scalar(RS[:, :], MISC[:, 0:T], 1.0 / D, EPS, ALU.mult, ALU.add).then_inc(ms_ready, 1)
                dve.wait_ge(rt_ready, k + 1)
                step(nc.vector.reciprocal(RS[:, :], RS[:, :]))

            def modulated(k, gain, shift, scale, groups):
                dve.wait_ge(ada_bias, groups)
                step(nc.vector.scalar_tensor_tensor(MC[:, :], MOD[:, scale:scale + 16], 1.0, PRM[:, gain:gain + 16],
                                                    ALU.add, ALU.mult))
                root(k)
                for q in range(4):
                    for t in range(4 * q, 4 * q + 4):
                        ins = nc.vector.scalar_tensor_tensor(YF[:, t, :], X[:, t, :], MC[:, t:t + 1], RS[:, :],
                                                             ALU.mult, ALU.mult)
                    step(ins)
                    for t in range(4 * q, 4 * q + 4):
                        ins = nc.vector.tensor_scalar(YF[:, t, :], YF[:, t, :], MOD[:, shift + t:shift + t + 1], None,
                                                      ALU.add)
                    ins.then_inc(yf_quad, 1)

            def residual(pair, g, gate):
                dve.wait_ge(pe_sub, c.sub.value(-2))
                for t in range(4):
                    ins = nc.vector.scalar_tensor_tensor(X[:, 4 * g + t, :], flat(pair)[:, t * T:(t + 1) * T],
                                                         MOD[:, gate + 4 * g + t:gate + 4 * g + t + 1],
                                                         X[:, 4 * g + t, :], ALU.mult, ALU.add)
                ins.then_inc(free[pair], 1)

            def win_body(layer=None, skip=0):
                for s in range(16):
                    if s >= skip:
                        lo()
                    if layer is not None:
                        ada_beside(layer, s, 16)

            def ffn(with_ada, gate):
                def product():
                    dve.wait_ge(pe_sub, c.sub.value(-2))
                    dve.wait_ge(gate_done, c.hid.value(1))
                    nc.vector.tensor_tensor(G, flat("B"), G, ALU.mult).then_inc(up_done, 1)

                def hidden():
                    dve.wait_ge(hid_hi, c.hid.value(1))
                    nc.vector.tensor_tensor(HID[:, :, T:2 * T], G.rearrange("p (a b) -> p a b", a=4),
                                            HID[:, :, 0:T].bitcast(F32), ALU.subtract).then_inc(hid_lo, 1)
                    c.hid.at += 1

                def add_down(n):
                    dve.wait_ge(pe_sub, c.sub.value(-2))
                    pair, part = "AC"[n % 2], yf[:, n * 1024:(n + 1) * 1024]
                    nc.vector.tensor_tensor(part, flat(pair), part, ALU.add).then_inc(free[pair], 1)

                def body(skip=0, subs=24, up=True, previous=True, layer=None):
                    for s in range(subs):
                        if s >= skip:
                            lo()
                        if s == 1 and up:
                            product()
                        if s == 1 and previous:
                            add_down(3)
                        if s == 2 and up:
                            hidden()
                        if s in (19, 21, 23):
                            add_down((s - 19) // 2)
                        if layer is not None:
                            ada_beside(layer, s, subs)

                body(skip=2, subs=16, up=False, previous=False, layer=0 if with_ada else None)
                step(nc.vector.memset(yf, 0.0))
                body(previous=False, layer=0 if with_ada else None)
                with dve.Fori(2, NF) as i:
                    c.enter(i - 2, unit=12, sub=24, hid=1, ada=KT * with_ada, ada_group=int(with_ada))
                    body(layer=1 if with_ada else None)
                c.leave(NF - 2)
                lo(2)
                product()
                add_down(3)
                hidden()
                for s in range(2, 8):
                    lo()
                    if s in (3, 5, 7):
                        add_down((s - 3) // 2)

            def ffn_end(gate, a_free, c_free, groups):
                part = yf[:, 3 * 1024:4 * 1024]
                nc.vector.tensor_tensor(part, flat("C"), part, ALU.add).then_inc(free["C"], 1)
                dve.wait_ge(free["A"], a_free)
                dve.wait_ge(free["C"], c_free)
                dve.wait_ge(ada_bias, groups)
                for t in range(KT):
                    nc.vector.scalar_tensor_tensor(X[:, t, :], YF[:, t, :], MOD[:, gate + t:gate + t + 1],
                                                   X[:, t, :], ALU.mult, ALU.add).then_inc(x_step, 1)

            nc.vector.memset(PRAW[:, 3, :], 0.0).then_inc(praw_zero, 1)
            dve.wait_ge(prm_t, 1)
            nc.vector.tensor_copy(PRM[:, :], MISC).then_inc(prm_ready, 1)
            for n in range(8):
                dve.wait_ge(x_turned, n + 1)
                nc.vector.tensor_copy(X[:, 2 * n:2 * n + 2, :].rearrange("p a b -> p (a b)"),
                                      PS[n // 2 % 2][:, n % 2, :]).then_inc(x_in, 1)
            dve.wait_ge(cact, 1)
            dve.wait_ge(prm_ready, 1)
            dve.wait_ge(x_in, 8)
            for g in range(4):
                for kt in range(KT):
                    ada(kt, 0)
                if g == 3:
                    lo(2)
                ada_end()
            modulated(0, COL["g_norm_mix"], mod_at(0, 0), mod_at(0, 1), 4)
            split()
            win_body(0, skip=2)
            with dve.Fori(1, 3) as i:
                c.enter(i - 1, unit=8, sub=16, ada=KT, ada_group=1)
                win_body(0)
            c.leave(2)
            lo(2)

            dve.wait_ge(free["A"], 3)
            dve.wait_ge(free["B"], 3)
            tap = lambda j, t: PRM[:, COL["w_conv"] + 8 * j + t:COL["w_conv"] + 8 * j + t + 1]
            for t in range(8):
                nc.vector.tensor_scalar(R[:, 24 + t, :], R[:, t, :], tap(3, t),
                                        PRM[:, COL["b_conv"] + t:COL["b_conv"] + t + 1], ALU.mult, ALU.add)\
                    .then_inc(conv_step, 1)
            for n, j in enumerate((2, 1, 0)):
                s = 3 - j
                dve.wait_ge(conv_step, 8 * (n + 1))
                for t in range(8):
                    nc.vector.scalar_tensor_tensor(R[:, 24 + t, s:T], R[:, t, 0:T - s], tap(j, t), R[:, 24 + t, s:T],
                                                   ALU.mult, ALU.add).then_inc(conv_step, 1)
            dve.wait_ge(lam_done, 1)
            step(nc.vector.scalar_tensor_tensor(SM[:, 0:8], PRM[:, COL["lru_lambda"]:COL["lru_lambda"] + 8], 0.0,
                                                SM[:, 8:16], ALU.min, ALU.subtract))
            nc.vector.tensor_scalar(SM[:, 0:8], SM[:, 0:8], 8.0, None, ALU.mult).then_inc(c8_done, 1)
            dve.wait_ge(rg_sig, 16)
            dve.wait_ge(conv_step, 32)
            step(nc.vector.tensor_tensor(tiles(40, 8), tiles(40, 8), tiles(24, 8), ALU.mult))
            dve.wait_ge(a_done, 8)
            step(nc.vector.tensor_tensor(tiles(48, 8), tiles(0, 8), tiles(0, 8), ALU.mult))
            dve.wait_ge(tanh_done, 8)
            nc.vector.scalar_tensor_tensor(tiles(48, 8), tiles(48, 8), 1.0, tiles(32, 8), ALU.add, ALU.mult)\
                .then_inc(m2_done, 1)
            dve.wait_ge(root_done, 1)
            step(nc.vector.tensor_tensor(tiles(40, 8), tiles(40, 8), tiles(32, 8), ALU.mult))
            for t in range(8):
                ins = nc.vector.tensor_tensor_scan(R[:, 24 + t, :], R[:, t, :], R[:, 40 + t, :], 0.0, ALU.mult, ALU.add)
            step(ins)
            dve.wait_ge(gelu_done, 1)
            for q in range(2):
                nc.vector.tensor_tensor(YF[:, 4 * q:4 * q + 4, :], R[:, 24 + 4 * q:28 + 4 * q, :],
                                        R[:, 8 + 4 * q:12 + 4 * q, :], ALU.mult).then_inc(yf_quad, 1)
            split()

            dve.wait_ge(ada_bias, 6)
            for g in range(4):
                for s in range(8):
                    if g or s >= 2:
                        lo()
                    if g and s == 1:
                        residual("BA"[g % 2], g - 1, mod_at(0, 2))
                    if g < 3:
                        ada_beside(0, s, 8)
            lo(2)
            residual("B", 3, mod_at(0, 2))
            modulated(1, COL["g_norm_ffn"], mod_at(0, 3), mod_at(0, 4), 10)
            split()
            ffn(True, mod_at(0, 5))
            lo(2)
            dve.wait_ge(pe_sub, c.sub.value(-2))
            ffn_end(mod_at(0, 5), A_FFN1, C_FFN1, 12)
            dve.wait_ge(x_step, KT)
            nc.vector.tensor_copy(SM[:, 16:17], X[:, 0, 0:1]).then_inc(x_done, 1)
            root(2)
            for t in range(KT):
                ins = nc.vector.scalar_tensor_tensor(X[:, t, :], X[:, t, :],
                                                     PRM[:, COL["g_norm_final"] + t:COL["g_norm_final"] + t + 1],
                                                     RS[:, :], ALU.mult, ALU.mult)
            ins.then_inc(x_done, 1)
            dve.wait_ge(x_done, 2)
            modulated(3, COL["g_norm1_2"], mod_at(1, 0), mod_at(1, 1), 16)
            split()
            lo(14)
            with dve.Fori(0, 2) as i:
                c.enter(i, unit=8, sub=16, ada=KT, ada_group=1)
                win_body(1)
            c.leave(2)
            for s in range(16):
                lo()
                ada_beside(1, s, 16)
                if s == 8:
                    dve.wait_ge(lat_ss, 2)
                    nc.vector.tensor_scalar(YF[:, 8:10, :], MISC.rearrange("p (a b) -> p a b", a=2), 1.0 / 512, EPS,
                                            ALU.mult, ALU.add).then_inc(lat_ms, 1)
                if s == 13:
                    dve.wait_ge(lat_rt, 1)
                    step(nc.vector.reciprocal(YF[:, 8:10, :], YF[:, 8:10, :]))
                if s in (14, 15):
                    n = s - 14
                    name = ("g_q_latent_2", "g_kv_latent_2")[n]
                    for t in range(4):
                        ins = nc.vector.scalar_tensor_tensor(R[:, 4 * n + t, :], R[:, 4 * n + t, :],
                                                             PRM[:, COL[name] + t:COL[name] + t + 1], YF[:, 8 + n, :],
                                                             ALU.mult, ALU.mult)
            ins.then_inc(lat_ev, 1)
            lo(2)

            whole, turns, ang = tiles(73, 1).bitcast(I32), tiles(76, 1), tiles(77, 1)
            c1 = 6.28125
            c2 = float(np.round((2 * np.pi - c1) * 2 ** 20) / 2 ** 20)
            c3 = float(2 * np.pi - c1 - c2)

            def angle(n):
                if n == 0:
                    dve.wait_ge(con_in, 16)
                    dve.wait_ge(pos_in, 16)
                    step(nc.vector.tensor_copy(turns, whole))
                    step(nc.vector.tensor_scalar(ang, turns, CON[:, FREQ:FREQ + 1], None, ALU.mult))
                quarter, shift = ((0.25, float(np.pi / 2)), (0.0, 0.0))[n]
                r = tiles(74 + n, 1)
                step(nc.vector.tensor_scalar(turns, ang, float(1 / (2 * np.pi)), quarter, ALU.mult, ALU.add))
                step(nc.vector.tensor_copy(whole, turns))
                step(nc.vector.tensor_copy(turns, whole))
                step(nc.vector.scalar_tensor_tensor(r, turns, -c1, ang, ALU.mult, ALU.add))
                step(nc.vector.scalar_tensor_tensor(r, turns, -c2, r, ALU.mult, ALU.add))
                step(nc.vector.scalar_tensor_tensor(r, turns, -c3, r, ALU.mult, ALU.add))
                step(nc.vector.tensor_scalar(r, r, shift, 3.1415925, ALU.add, ALU.min))
                nc.vector.tensor_scalar(r, r, -3.1415925, None, ALU.max).then_inc(ang_done, 1)

            both = lambda at: CON[:, at:at + 384].rearrange("p (a b) -> p a b", a=1).to_broadcast([P, 2, 384])
            for hp in range(4):
                for s in range(16):
                    lo()
                    if s == 2:
                        dve.wait_ge(z_mm, hp + 1)
                        step(nc.vector.scalar_tensor_tensor(three(78), PAIR["C"][:, :, 0:384], 128 ** -0.5,
                                                            both(SB_ONE), ALU.mult, ALU.mult))
                        nc.vector.tensor_tensor(three(78), three(78), both(SB_NEG), ALU.add).then_inc(z_dve, 1)
                    if s == 5:
                        dve.wait_ge(z_act, hp + 1)
                        if hp:
                            dve.wait_ge(a_act, hp)
                        nc.vector.scalar_tensor_tensor(tiles(84, 3), tiles(78, 3), 0.0, tiles(81, 3), ALU.max, ALU.add)\
                            .then_inc(sp_done, 1)
                    if s == 8:
                        dve.wait_ge(u_mm, hp + 1)
                        nc.vector.tensor_tensor(three(84), three(78), PS[3][:, :, 0:384], ALU.subtract)\
                            .then_inc(w_dve, 1)
                    if s in (6, 9) and hp == 0:
                        angle((s - 6) // 3)
                    if s == 15 and hp == 0:
                        dve.wait_ge(trig_done, 2)
                        step(nc.vector.tensor_scalar(CS[1], CS[1], CON[:, SIGN:SIGN + 1], None, ALU.mult))
            lo(2)

            split(2, src=R)
            for n in range(7):
                lo(2)
                if n in (1, 2):
                    split(1, first=n + 1)

            def merge_b(g):
                dve.wait_ge(pe_sub, c.sub.value(-2))
                nc.vector.tensor_tensor(tiles(48 + 4 * g, 4), flat("C"), tiles(48 + 4 * g, 4), ALU.mult)\
                    .then_inc(free["C"], 1)

            col = lambda name: PRM[:, COL[name]:COL[name] + 1]
            step(nc.vector.memset(tiles(30, 2), 0.0))
            for hp in range(4):
                dve.wait_ge(hd_ss, hp + 1)
                nc.vector.tensor_scalar(tiles(73, 4), flat("C"), 1.0 / 192, EPS, ALU.mult, ALU.add).then_inc(hd_ms, 1)
                if hp == 0:
                    nc.vector.tensor_scalar(KPE, KPE, col("k_rope"), None, ALU.mult).then_inc(rope_in, 1)
                nc.vector.tensor_scalar(R[:, 16 + hp, :], R[:, 16 + hp, :], col("q_rope"), None, ALU.mult)\
                    .then_inc(rope_in, 1)
                dve.wait_ge(hd_rt, hp + 1)
                step(nc.vector.reciprocal(tiles(73, 4), tiles(73, 4)))
                for a in range(2):
                    nc.vector.scalar_tensor_tensor(R[:, 8 + 2 * hp + a, :], R[:, 8 + 2 * hp + a, :], col("g_q_head_2"),
                                                   R[:, 73 + a, :], ALU.mult, ALU.mult)
                    nc.vector.scalar_tensor_tensor(R[:, 2 * hp + a, :], R[:, 2 * hp + a, :], col("g_k_head_2"),
                                                   R[:, 75 + a, :], ALU.mult, ALU.mult)
                for n, (tile, half) in enumerate(((KPE, 0), (R[:, 16 + hp, :], 1))):
                    if n == 0 and hp:
                        continue
                    dve.wait_ge(rope_swap, hp + 2)
                    step(nc.vector.tensor_tensor(R[:, 29, :], SMALL[:, half * T:(half + 1) * T], CS[1], ALU.mult))
                    step(nc.vector.tensor_tensor(tile, tile, CS[0], ALU.mult))
                    step(nc.vector.tensor_tensor(tile, tile, R[:, 29, :], ALU.add))
                for a in range(2):
                    h = slice(64 * a, 64 * a + 64)
                    nc.vector.tensor_tensor(R[h, 16 + hp, :], R[h, 16 + hp, :], R[h, 73 + a, :], ALU.mult)
                    ins = nc.vector.tensor_tensor(R[h, 30 + a, :], R[h, 87, :], R[h, 75 + a, :], ALU.mult)
                ins.then_inc(hd_scaled, 1)
                lo(2)
                dve.wait_ge(s_mm, hp + 1)
                step(nc.vector.scalar_tensor_tensor(SC, PAIR["A"][:, :, 0:384], 192 ** -0.5, both(MLA_NEG), ALU.mult,
                                                    ALU.add))
                for a in range(2):
                    for qb, (k0, k1) in enumerate(((0, 128), (128, 384))):
                        n = 2 * a + qb
                        ins = nc.vector.tensor_reduce(SM[:, n:n + 1], SC[:, a, k0:k1], AX_X, ALU.max)
                step(ins)
                nc.vector.tensor_scalar(SM[:, 0:4], SM[:, 0:4], -1.0, None, ALU.mult).then_inc(s_dve, 1)
                dve.wait_ge(p_act, hp + 1)
                step(nc.vector.reciprocal(SM[:, 8:12], SM[:, 4:8]))
                for a in range(2):
                    for qb, (k0, k1) in enumerate(((0, 128), (128, 384))):
                        n = 8 + 2 * a + qb
                        ins = nc.vector.tensor_scalar(SC[:, a, k0:k1], SC[:, a, k0:k1], SM[:, n:n + 1], None, ALU.mult)
                ins.then_inc(p_dve, 1)
                lo(2)
                merge_b(hp)
            split(2)

            def merge_a(g):
                dve.wait_ge(pe_sub, c.sub.value(-2))
                pair, ga = "AB"[g % 2], tiles(32 + 4 * g, 4)
                step(nc.vector.tensor_tensor(ga, flat(pair), ga, ALU.mult))
                dve.wait_ge(free["C"], C_LAT + g + 1)
                nc.vector.tensor_tensor(yf[:, 4 * g * T:4 * (g + 1) * T], ga, tiles(48 + 4 * g, 4), ALU.add)\
                    .then_inc(free[pair], 1)

            for g in range(4):
                for s in range(4):
                    if g or s >= 2:
                        lo()
                    if g and s == 1:
                        merge_a(g - 1)
            lo(2)
            merge_a(3)
            split()
            for g in range(4):
                for s in range(8):
                    if g or s >= 2:
                        lo()
                    if g and s == 1:
                        residual("BA"[g % 2], g - 1, mod_at(1, 2))
            lo(2)
            residual("B", 3, mod_at(1, 2))
            modulated(4, COL["g_norm2_2"], mod_at(1, 3), mod_at(1, 4), 24)
            split()
            ffn(False, mod_at(1, 5))
            assert c.unit.at == N_UNITS
            dve.wait_ge(pe_sub, 2 * N_UNITS)
            ffn_end(mod_at(1, 5), A_END, C_END, 24)
            for n in range(8):
                dve.wait_ge(x_turned, 8 + n + 1)
                nc.vector.tensor_copy(yf[:, n * 512:(n + 1) * 512], PS[n // 2 % 2][:, n % 2, :]).then_inc(x_in, 1)

        @block.tensor
        def _(pe):
            c = Counts()

            def mm(o, a, b, start, stop=False):
                return nc.tensor.matmul(o, a, b, start=start, stop=stop, skip_group_check=True)

            def sub(pair, src, k0, first, last, kind="W", counted=True):
                j, used, o = c.sub.at % 2, c.all[pair], PAIR[pair]
                pe.wait_ge(lo_done, c.sub.value(1))
                if first and used.at:
                    pe.wait_ge(free[pair], used.value())
                for k in range(8 if kind == "K" else 0):
                    kk, n = k0 + k, slice(k % 4 * P, (k % 4 + 1) * P)
                    mm(o[:, 0, 0:T], WHI[j][:, k // 4, n], src[:, kk, 0:T], first and k == 0)
                    mm(o[:, 0, 0:T], WHI[j][:, k // 4, n], src[:, kk, T:2 * T], False)
                    ins = mm(o[:, 0, 0:T], WLO[j][:, k // 4, n], src[:, kk, 0:T], False, last and k == 7)
                for k in range(0 if kind == "K" else 2):
                    kk, begin, end = k0 + k, first and k == 0, last and k == 1
                    if kind == "W":
                        for t in range(4):
                            dst, n = o[:, t // 2, (t % 2) * T:(t % 2 + 1) * T], slice(t * P, (t + 1) * P)
                            mm(dst, WHI[j][:, k, n], src[:, kk, 0:T], begin and t % 2 == 0)
                            mm(dst, WHI[j][:, k, n], src[:, kk, T:2 * T], False)
                            ins = mm(dst, WLO[j][:, k, n], src[:, kk, 0:T], False, end)
                    if kind == "T":
                        for tb in range(2):
                            hi_x = src[:, kk, tb * P:(tb + 1) * P]
                            lo_x = src[:, kk, T + tb * P:T + (tb + 1) * P]
                            mm(o[:, tb, :], hi_x, WHI[j][:, k, :], begin)
                            mm(o[:, tb, :], lo_x, WHI[j][:, k, :], False)
                            ins = mm(o[:, tb, :], hi_x, WLO[j][:, k, :], False, end)
                ins.then_inc(pe_sub, 1)
                c.sub.at += 1
                used.at += last and counted

            def group(pair, src=H, k0=0, units=4, kind="W", quads=None, ada_after=None, counted=True, then={}):
                for s in range(2 * units):
                    if quads is not None and s % 2 == 0:
                        pe.wait_ge(h_quad, quads + s // 2 + 1)
                    sub(pair, src, k0 + 2 * s, s == 0, s == 2 * units - 1, kind, counted)
                    if s == ada_after:
                        ada_sum()
                    if s in then:
                        then[s]()

            def ada_sum():
                pe.wait_ge(ada_op, c.ada_group.value(1, times=KT))
                if c.ada_group.at:
                    pe.wait_ge(ada_bias, c.ada_group.value())
                for j in range(8):
                    ins = mm(SMALL[:, j:j + 1], ACC[:, j * P:(j + 1) * P], ones[:, 0:1], True, True)
                ins.then_inc(ada_red, 1)
                c.ada_group.at += 1

            def square_sum(k):
                for q in range(4):
                    pe.wait_ge(sq_ready, 4 * k + q + 1)
                    for t in range(4 * q, 4 * q + 4):
                        ins = mm(MISC[:, 0:T], ones, YF[:, t, :], t == 0, t == KT - 1)
                ins.then_inc(ssq_ready, 1)

            def ffn(quads, with_ada):
                def gate(**more):
                    group("A", counted=False, **more)
                    c.gate.at += 1

                def up(**more):
                    if c.gate.at > 1:
                        pe.wait_ge(up_done, c.gate.value(-1))
                    group("B", counted=False, **more)

                def down(ada_after=None):
                    pe.wait_ge(hid_lo, c.hid.value(1))
                    pe.wait_ge(gate_done, c.gate.value())
                    for n in range(4):
                        group("AC"[n % 2], src=HID, units=1, ada_after=ada_after if n == 2 else None)
                    c.hid.at += 1

                ada_24 = 0 if with_ada else None
                gate(quads=quads)
                up(ada_after=5 if with_ada else None)
                gate()
                up()
                down(ada_24)
                with pe.Fori(2, NF) as i:
                    c.enter(i - 2, sub=24, A=2, C=2, hid=1, gate=1, ada_group=int(with_ada))
                    gate()
                    up()
                    down(ada_24)
                c.leave(NF - 2)
                down()

            pe.wait_ge(base_in, 16)
            pe.wait_ge(rows_in, 16 * len(rows_src))
            pe.wait_ge(praw_zero, 1)
            for n in range(4):
                ins = nc.tensor.transpose(MISC[:, n * P:(n + 1) * P], PRAW[:, n, :], ident)
            ins.then_inc(prm_t, 1)
            pe.wait_ge(x_rows, 32)
            for n in range(8):
                if n >= 4:
                    pe.wait_ge(x_in, n - 3)
                for k in range(2):
                    for tb in range(2):
                        at = tb * D + (2 * n + k) * P
                        ins = nc.tensor.transpose(PS[n // 2 % 2][:, n % 2, (2 * k + tb) * P:(2 * k + tb + 1) * P],
                                                  yf[:, at:at + P], ident)
                ins.then_inc(x_turned, 1)

            square_sum(0)
            for g in range(4):
                ada_sum()
            group("A", quads=Q_WIN1)
            group("B", ada_after=5)
            with pe.Fori(1, 3) as i:
                c.enter(i - 1, sub=16, A=1, B=1, ada_group=1)
                group("A")
                group("B", ada_after=5)
            c.leave(2)

            pe.wait_ge(free["A"], 3)
            pe.wait_ge(free["B"], 3)
            pe.wait_ge(conv_step, 32)
            pe.wait_ge(pool_chain, 1)
            pe.wait_ge(mix_w, 16 * 5)
            for kind in range(2):
                if kind == 1:
                    pe.wait_ge(ada_bias, 7)
                for t in range(8):
                    mm(eight(2 * kind, t), tiles(48 + 4 * kind, 4)[:, t * P:(t + 1) * P], R[:, 24 + t, :], True, True)\
                        .then_inc(rg_mm, 1)
            pe.wait_ge(pooled, 4)
            pe.wait_ge(rg_sig, 16)
            for t in range(8):
                g, oc = t // 2, t % 2
                for kc in range(2):
                    ins = mm(eight(0, t), tiles(56 + 2 * g + kc, 1)[:, oc * P:(oc + 1) * P], R[:, 16 + 2 * g + kc, :],
                             kc == 0, kc == 1)
                ins.then_inc(pool_mm, 1)
            pe.wait_ge(pool_ev, 8)

            for g in range(4):
                group("AB"[g % 2], quads=Q_WOUT1 if g == 0 else None, ada_after=5 if g < 3 else None)
            square_sum(1)
            ffn(Q_FFN1, True)
            square_sum(2)
            square_sum(3)

            group("A", quads=Q_WIN2)
            group("B")
            with pe.Fori(0, 2) as i:
                c.enter(i, sub=16, A=1, B=1, ada_group=1)
                group("A")
                group("B", ada_after=5)
            c.leave(2)
            def latents_sum():
                for n in range(2):
                    pe.wait_ge(lat_sq, n + 1)
                    for t in range(4):
                        ins = mm(MISC[:, n * T:(n + 1) * T], ones, YF[:, 4 * n + t, :], t == 0, t == 3)
                    ins.then_inc(lat_ss, 1)

            group("A", kind="T", then={6: latents_sum})
            group("B", kind="T", ada_after=5)
            sub("C", H, 0, True, False, "K")
            sub("C", H, 8, False, True, "K")

            heads_of = lambda hp: ((0, 2 * hp), (1, 2 * hp + 1))
            value = lambda tile, h, tb: rf[:, (tile + 4 * (h // 4)) * T + tb * 512 + h % 4 * P:][:, 0:P]

            def logits(hp):
                if hp == 0:
                    pe.wait_ge(con_in, 16)
                    pe.wait_ge(free["C"], C_FFN1 + 1)
                else:
                    pe.wait_ge(y_ev, hp)
                for a, h in heads_of(hp):
                    q, k = R[:, 8 + h, :], R[:, 16 + h, :]
                    mm(PAIR["C"][:, a, 0:256], k[:, 0:P], q, True, True)
                    ins = mm(PAIR["C"][:, a, 256:384], k[:, P:T], q[:, P:T], True, True)
                ins.then_inc(z_mm, 1)

            def tails(hp):
                pe.wait_ge(sp_done, hp + 1)
                if hp == 0:
                    pe.wait_ge(ada_bias, 24)
                    pe.wait_ge(lat_ms, 1)
                for a, h in heads_of(hp):
                    s, o = three(84)[:, a, :], PS[3][:, a, :]
                    mm(o[:, 0:256], CON[:, TRI:TRI + P], s[:, 0:256], True)
                    mm(o[:, 128:256], ones, s[:, 256:384], False, True)
                    ins = mm(o[:, 256:384], CON[:, TRI:TRI + P], s[:, 256:384], True, True)
                ins.then_inc(u_mm, 1)

            def weighted(hp):
                pe.wait_ge(a_act, hp + 1)
                for a, h in heads_of(hp):
                    w, o = three(81)[:, a, :], PAIR["C"][:, 0, a * T:(a + 1) * T]
                    mm(o, value(24, h, 0), w[:, 0:256], True)
                    ins = mm(o[:, 128:256], value(24, h, 1), w[:, 256:384], False, True)
                ins.then_inc(y_mm, 1)

            for hp in range(4):
                group("A", then={0: lambda: logits(hp), 5: lambda: tails(hp)})
                group("B", then={2: lambda: weighted(hp)})

            for n, (pair, tile) in enumerate(LAT):
                pe.wait_ge(h_quad, Q_LAT + (1 if n < 3 else 2))
                group(pair, k0=0 if n < 3 else 4, units=1, kind="W" if n < 5 else "T")

            pe.wait_ge(free["A"], A_LAT)
            pe.wait_ge(free["B"], B_LAT)
            pe.wait_ge(free["C"], C_LAT)
            pe.wait_ge(y_ev, 4)
            for hp in range(4):
                pe.wait_ge(hd_sq, 1 + 3 * (hp + 1))
                pe.wait_ge(free["C"], C_LAT + hp)
                for n, (nope, rope, half) in enumerate(((78, 80, EVEN), (79, 80, ODD), (81, 77, EVEN), (82, 77, EVEN))):
                    o = flat("C")[:, n * T:(n + 1) * T]
                    mm(o, ones, R[:, nope, :], True)
                    ins = mm(o, CON[:, half:half + P], R[:, rope, :], False, True)
                ins.then_inc(hd_ss, 1)
                if hp == 0:
                    pe.wait_ge(rope_in, 1)
                    mm(SMALL[:, 0:T], CON[:, PERM:PERM + P], KPE, True, True).then_inc(rope_swap, 1)
                pe.wait_ge(rope_in, hp + 2)
                mm(SMALL[:, T:2 * T], CON[:, PERM:PERM + P], R[:, 16 + hp, :], True, True).then_inc(rope_swap, 1)
                pe.wait_ge(hd_ms, hp + 1)
                if hp == 0:
                    pe.wait_ge(h_quad, Q_PROJ_B + 2)
                for s in range(2):
                    sub("C", H, 8 + 2 * s, s == 0, False)
                pe.wait_ge(hd_scaled, hp + 1)
                for a, h in heads_of(hp):
                    q, qr, k, kr = R[:, 8 + h, :], R[:, 16 + hp, :], R[:, h, :], R[:, 30 + a, :]
                    for qs, ks, at in ((slice(0, P), slice(0, P), slice(0, 128)),
                                       (slice(P, T), slice(0, T), slice(128, 384))):
                        mm(PAIR["A"][:, a, at], q[:, qs], k[:, ks], True)
                        ins = mm(PAIR["A"][:, a, at], qr[:, qs], kr[:, ks], False, True)
                ins.then_inc(s_mm, 1)
                for s in range(2, 4):
                    sub("C", H, 8 + 2 * s, False, s == 3)
                pe.wait_ge(p_dve, hp + 1)
                for a in range(2):
                    for b in range(3):
                        n = slice(b * P, (b + 1) * P)
                        ins = nc.tensor.transpose(PAIR["B"][:, a, n], SC[:, a, n], ident)
                ins.then_inc(pt_mm, 1)
                pe.wait_ge(pt_ev, hp + 1)
                if hp:
                    pe.wait_ge(o_ev, hp)
                for a, h in heads_of(hp):
                    p, o = SC[:, a, :], MISC[:, a * T:(a + 1) * T]
                    mm(o, value(20, h, 0), p[:, 0:256], True)
                    ins = mm(o[:, 128:256], value(20, h, 1), p[:, 256:384], False, True)
                ins.then_inc(o_mm, 1)

            pe.wait_ge(h_quad, Q_PROJ_A + 2)
            with pe.Fori(0, 2) as i:
                c.enter(i, sub=8, A=1, B=1)
                group("A", units=2)
                group("B", units=2)
            c.leave(2)
            for g in range(4):
                group("AB"[g % 2], quads=Q_WOUT2 if g == 0 else None)
            square_sum(4)
            ffn(Q_FFN2, False)
            assert c.sub.at == 2 * N_UNITS

            pe.wait_ge(x_step, 2 * KT)
            for n in range(8):
                if n >= 4:
                    pe.wait_ge(x_in, 8 + n - 3)
                for k in range(4):
                    ins = nc.tensor.transpose(PS[n // 2 % 2][:, n % 2, k * P:(k + 1) * P],
                                              X[:, 4 * (n % 4) + k, n // 4 * P:(n // 4 + 1) * P], ident)
                ins.then_inc(x_turned, 1)


def kernel(**inputs):
    import concourse.bacc as _bacc
    from concourse.bass_utils import run_bass_kernel_spmd as _run

    nc = _bacc.Bacc("TRN2", target_bir_lowering=False, num_devices=1)
    arrays = {}

    def dram(name, a):
        a = np.ascontiguousarray(a)
        arrays[f"in_{name}"] = a
        return nc.dram_tensor(f"in_{name}", a.shape, mybir.dt.from_np(a.dtype), kind="ExternalInput").ap()

    ktiles = lambda name: dram(name, np.asarray(inputs[name]).reshape(np.shape(inputs[name])[-2:]))\
        .rearrange("(k p) n -> p k n", p=P)
    weights = [ktiles(n) for n in ("w_in", "w_out", "w_ffn_gate", "w_ffn_up", "w_ffn_down", "w_in_2", "w_uq_2",
                                   "w_ukv_2", "w_proj_mla_2", "w_proj_sb_2", "w_out_2", "w_ffn_in_2",
                                   "w_ffn_out_2")]
    ada_w = [ktiles("w_ada"), ktiles("w_ada_2")]

    rows_src = []
    for name, n in PARAMS:
        source = {"q_rope": "g_q_head_2", "k_rope": "g_k_head_2"}.get(name, name)
        a = dram(f"row_{name}", np.asarray(inputs[source]).reshape(1, -1))
        width = a.shape[1] // n
        if width == P:
            r = 0
            while r < n:
                at = COL[name] + r
                m = min(n - r, P - at % P)
                rows_src.append((at // P, at % P, m, 0, P,
                                 a[:, r * P:(r + m) * P].rearrange("o (r n) -> (o r) n", n=P)))
                r += m
        else:
            at, parts = COL[name], ((0, 64), (64, 128)) if "rope" in name else ((0, 128),)
            for c0, c1 in parts:
                first = 128 if "rope" in name else 0
                rows_src.append((at // P, at % P, 1, c0, c1, a[:, first:first + c1 - c0]))

    gates = [dram(n, np.asarray(inputs[n])[0]).rearrange("(t e) i j -> e i t j", e=2) for n in ("w_rg_a", "w_rg_i")]
    w_pool = dram("w_pool", np.asarray(inputs["w_pool"])[0]).rearrange("g (k p) n -> p (g k) n", p=P)

    base = np.zeros((P, N_BASE), np.float32)
    base[:, IDENT:IDENT + P] = np.eye(P)
    base[:, ONES:ONES + P] = 1.0
    for g in range(4):
        for t in range(16):
            base[:, INV + 16 * g + t] = np.float32(1.0) / np.float32(min(t + 1, 2 << g))
    i = np.arange(P)
    row, col = i[:, None], i[None, :]
    con = np.zeros((P, N_CONST), np.float32)
    con[:, PERM:PERM + P] = (row // 32 ^ 1 == col // 32) & (row % 32 == col % 32)
    con[:, TRI:TRI + P] = row >= col
    con[:, EVEN:EVEN + P] = row < 64
    con[:, ODD:ODD + P] = row >= 64
    one = np.ones((P, 3 * P), np.float32)
    one[:, 0:P] = one[:, 2 * P:] = row < col
    con[:, SB_ONE:SB_ONE + 3 * P] = one
    con[:, SB_NEG:SB_NEG + 3 * P] = (one - 1) * np.float32(1e30)
    for at in (0, 2 * P):
        con[:, MLA_NEG + at:MLA_NEG + at + P] = np.where(col <= row, 0, -1e30)
    con[:, FREQ] = np.float32(10000.0) ** (-(i % 32).astype(np.float32) / np.float32(32))
    con[:, SIGN] = np.where(i % 64 < 32, -1, 1)

    out = nc.dram_tensor("out_0", (T, D), F32, kind="ExternalOutput").ap()
    build(nc, dram("x", np.asarray(inputs["x"])[0]), dram("positions", inputs["positions_2"]), rows_src, weights,
          ada_w, dram("base_const", base), dram("att_const", con), *gates, w_pool, out)
    r = _run(nc, [arrays], core_ids=[0])
    return r.results[0]["out_0"].reshape(1, T, D)
```

```python
import numpy as np
from contextlib import ExitStack

import concourse.bass as bass
from concourse import mybir

F32 = mybir.dt.float32
F32R = mybir.dt.float32r
I32 = mybir.dt.int32
ALU = mybir.AluOpType
ACT = mybir.ActivationFunctionType
AX_X = mybir.AxisListType.X

T = 256
D = 2048
P = 128
KT = D // P
D_FF = 5632
LRU = 1024
HEADS = 8
EPS = 1e-6
COLS = 512
ADA_COLS = 1024
SP_GROUP = 6
NF = D_FF // COLS

PARAMS = [("b_ada", 96), ("b_ada_2", 96), ("g_norm_mix", 16), ("g_norm_ffn", 16),
          ("g_norm_final", 16), ("g_norm1_2", 16), ("g_norm2_2", 16), ("w_conv", 32), ("b_conv", 8),
          ("b_rg_a", 8), ("b_rg_i", 8), ("lru_lambda", 8), ("ls_pool", 8), ("g_q_latent_2", 4),
          ("g_kv_latent_2", 4), ("g_q_head_2", 1), ("g_k_head_2", 1), ("q_rope", 1), ("k_rope", 1)]
COL = {}
_at = 0
for _name, _n in PARAMS:
    COL[_name] = _at
    _at += _n
BLOCKS = -(-_at // P)

PERM, TRI, EVEN, ODD, SB_ONE, SB_NEG, MLA_NEG, FREQ, SIGN, N_CONST = 0, 128, 256, 384, 512, 896, 1280, 1664, 1665, 1792
IDENT, ONES, INV, N_BASE = 0, 128, 256, 320

U_WIN1, U_WOUT1, U_FFN1, U_WIN2, U_KPE, U_GATES, U_LAT, U_PROJ, U_WOUT2, U_FFN2 = 0, 24, 40, 172, 204, 205, 237, 244, 260, 276
N_UNITS = 408

A_FFN1, B_FFN1, C_FFN1 = 3 + 2 + 2 * NF, 3 + 2, 2 * NF
A_WIN2, B_WIN2 = A_FFN1 + 8, B_FFN1 + 8
LAT = [("A", 8), ("B", 12), ("C", 16), ("A", 0), ("B", 4), ("A", 20), ("B", 24)]
A_LAT, B_LAT, C_LAT = A_WIN2 + 3, B_WIN2 + 3, C_FFN1 + 1 + 1
A_PROJ, B_PROJ, C_PROJ = A_LAT + 2, B_LAT + 2, C_LAT + 4
A_END, C_END = A_PROJ + 2 + 2 * NF, C_PROJ + 2 * NF

MERGED = (2, 3, 0, 1)

Q_WIN1, Q_WOUT1, Q_FFN1, Q_WIN2, Q_LAT, Q_PROJ_B, Q_PROJ_A, Q_WOUT2, Q_FFN2 = 0, 4, 8, 12, 16, 18, 20, 22, 26


class Count:

    def __init__(self):
        self.at, self.start, self.per, self.turn = 0, 0, 0, None

    def enter(self, turn, per):
        self.start, self.per, self.turn = self.at, per, turn

    def leave(self, turns):
        assert self.at - self.start == self.per, (self.at - self.start, self.per)
        self.at, self.per = self.start + self.per * turns, 0

    def value(self, more=0, times=1, over=1):
        n = (self.at + more) // over * times
        if not self.per:
            return n
        assert self.per % over == 0
        return self.turn * (self.per // over * times) + n


class Counts:

    def __init__(self):
        self.unit, self.sub = Count(), Count()
        self.A, self.B, self.C = Count(), Count(), Count()
        self.ada, self.ada_group = Count(), Count()
        self.gate, self.hid = Count(), Count()
        self.quad, self.chain = Count(), Count()
        self.all = dict(unit=self.unit, sub=self.sub, A=self.A, B=self.B, C=self.C, ada=self.ada,
                        ada_group=self.ada_group, gate=self.gate, hid=self.hid, quad=self.quad, chain=self.chain)

    def enter(self, turn, **per):
        for name, count in self.all.items():
            count.enter(turn, per.get(name, 0))

    def leave(self, turns):
        for count in self.all.values():
            count.leave(turns)


ADA_AFTER = {n: [first + k * (last - first) // 15 for k in range(KT)] for n, first, last in ((16, 1, 13), (24, 3, 18))}
ADA_BEFORE_W_OUT = 4
ADA_BESIDE_W_OUT = [[] for _ in range(32)]
ADA_SUM_IN_W_OUT = {}
_rest = [(n, k) for n in range(3) for k in range(KT)][ADA_BEFORE_W_OUT:]
for _i, (_n, _k) in enumerate(_rest):
    _s = _i * 29 // (len(_rest) - 1)
    ADA_BESIDE_W_OUT[_s].append((_n, _k))
    if _k == KT - 1:
        ADA_SUM_IN_W_OUT[_s + 1] = _n
        ADA_BESIDE_W_OUT[min(_s + 3, 31)].append((_n, KT))


def build(nc, x, c_rows, positions, rows_src, weights, ada_w, base_const, att_const, rg_a, rg_i, w_pool, out):
    w_in, w_out, w_gate, w_up, w_down, w_in2, w_uq, w_ukv, w_pa, w_pb, w_out2, w_ffin2, w_ffout2 = weights
    with ExitStack() as ctx:
        here = [-(-nc.sbuf_base // 64) * 64]

        def place(name, shape, dt=F32):
            n = 4
            for s in shape[1:]:
                n *= s
            t = nc.alloc_sbuf_tensor_at(name, shape, dt, offset=here[0])
            here[0] += n
            return t

        arena = here[0]
        R = place("R", [P, 88, T])
        end = here[0]
        here[0] = arena
        HID = place("HID", [P, 4, 2 * T], F32R)
        HID_LAST = place("HID_LAST", [P, 4, 2 * T], F32R)
        here[0] = end
        X = place("X", [P, KT, T])
        H = place("H", [P, KT, 2 * T], F32R)
        yf_at = here[0]
        HQ = place("HQ", [P, 4, 2 * T], F32R)
        here[0] = yf_at
        YF = place("YF", [P, KT, T])
        RAW = [place(f"RAW{i}", [P, 4, COLS]) for i in range(4)]
        WHI = [place(f"WHI{i}", [P, 2, COLS], F32R) for i in range(2)]
        WLO = [place(f"WLO{i}", [P, 2, COLS], F32R) for i in range(2)]
        PRM = place("PRM", [P, BLOCKS * P])
        MOD = place("MOD", [P, 192])
        BASE = place("BASE", [P, N_BASE])
        RS = place("RS", [P, T])
        CA = place("CA", [P, 32])
        MC = place("MC", [P, 16])
        SM = place("SM", [P, 32])
        rf = R[:, :, :].rearrange("p a b -> p (a b)")
        yf = YF[:, :, :].rearrange("p a b -> p (a b)")
        ident, ones = BASE[:, IDENT:IDENT + P], BASE[:, ONES:ONES + P]
        tiles = lambda a, n: rf[:, a * T:(a + n) * T]
        ADA = [tiles(64 + 4 * i, 4) for i in range(4)]
        ACC = tiles(80, 4)
        G = tiles(84, 4)
        CRAW = R[0:32, 2, 0:P]
        PRAW = R[:, 0:2, :].rearrange("p a (b c) -> p (a b) c", c=P)
        CON = tiles(64, 7)
        CS = [tiles(71, 1), tiles(72, 1)]

        PS = [ctx.enter_context(nc.psum_tensor(f"PS{i}", [P, 2, 512], F32)) for i in range(4)]
        PAIR = dict(A=PS[0], B=PS[1], C=PS[2])
        flat = lambda pair: PAIR[pair][:, :, :].rearrange("p a b -> p (a b)")
        SMALL, MISC = PS[3][:, 0, :], PS[3][:, 1, :]
        OUT_BANKS = [PS[1][:, 0, :], PS[1][:, 1, :], SMALL, MISC]

        tap = lambda j, t: PRM[:, COL["w_conv"] + 8 * j + t:COL["w_conv"] + 8 * j + t + 1]
        mod_at = lambda layer, which: 96 * layer + 16 * which
        eight = lambda t: PS[t // 4][:, t // 2 % 2, t % 2 * T:(t % 2 + 1) * T]
        three = lambda t: tiles(t, 3).rearrange("p (a b) -> p a b", a=2)
        KPE = tiles(87, 1)
        SC = three(83)
        GAINED = 32
        RS2 = tiles(48, 1)
        KR = lambda hp, a: 28 + 2 * (hp % 2) + a

        sem = lambda n: ctx.enter_context(nc.semaphore(n))
        raw_in = [sem(f"raw_in{i}") for i in range(4)]
        hi_done, lo_done, pe_sub = sem("hi_done"), sem("lo_done"), sem("pe_sub")
        free = {p: sem(f"free_{p}") for p in "ABC"}
        ada_in = [sem(f"ada_in{i}") for i in range(4)]
        ada_in_sp = [sem(f"ada_in_sp{i}") for i in range(4)]
        ada_op, ada_red, ada_bias = sem("ada_op"), sem("ada_red"), sem("ada_bias")
        yf_quad, h_hi, h_quad = sem("yf_quad"), sem("h_hi"), sem("h_quad")
        act_chain, dve_chain, pool_chain = sem("act_chain"), sem("dve_chain"), sem("pool_chain")
        mix_w, base_in, c_in, con_in, pos_in, rows_in, x_rows = (
            sem(n) for n in ("mix_w", "base_in", "c_in", "con_in", "pos_in", "rows_in", "x_rows"))
        c_t, prm_t, prm_ready, praw_zero, cact, x_turned, x_in = (
            sem(n) for n in ("c_t", "prm_t", "prm_ready", "praw_zero", "cact", "x_turned", "x_in"))
        sq_ready, ssq_ready, ms_ready, rt_ready = (sem(n) for n in ("sq_ready", "ssq_ready", "ms_ready", "rt_ready"))
        x_done, x_step = sem("x_done"), sem("x_step")
        gate_done, up_done, hid_hi, hid_lo = sem("gate_done"), sem("up_done"), sem("hid_hi"), sem("hid_lo")
        conv_step, lam_done, c8_done, rg_mm, rg_sig, a_done, tanh_done, gelu_done, m2_done, root_done = (
            sem(n) for n in ("conv_step", "lam_done", "c8_done", "rg_mm", "rg_sig", "a_done", "tanh_done",
                             "gelu_done", "m2_done", "root_done"))
        conv_first, ix_done = sem("conv_first"), sem("ix_done")
        pooled, pool_mm, pool_ev = sem("pooled"), sem("pool_mm"), sem("pool_ev")
        lat_sq, lat_ss, lat_ms, lat_rt, lat_ev, ang_done, trig_done = (
            sem(n) for n in ("lat_sq", "lat_ss", "lat_ms", "lat_rt", "lat_ev", "ang_done", "trig_done"))
        z_mm, z_dve, z_act, sp_done, u_mm, w_dve, a_act, y_mm, y_ev = (
            sem(n) for n in ("z_mm", "z_dve", "z_act", "sp_done", "u_mm", "w_dve", "a_act", "y_mm", "y_ev"))
        hd_sq, hd_ss, hd_ms, hd_rt, rope_in, rope_swap, hd_scaled = (
            sem(n) for n in ("hd_sq", "hd_ss", "hd_ms", "hd_rt", "rope_in", "rope_swap", "hd_scaled"))
        s_mm, s_dve, p_act, p_dve, pt_mm, pt_ev, o_mm, o_ev = (
            sem(n) for n in ("s_mm", "s_dve", "p_act", "p_dve", "pt_mm", "pt_ev", "o_mm", "o_ev"))
        out_ready, s_out = sem("out_ready"), sem("s_out")

        ctx.enter_context(nc.allow_non_contiguous_dma("column blocks of the weights"))
        block = ctx.enter_context(nc.Block())

        @block.sync
        def _(sp):
            c = Counts()

            def slot_free():
                if c.unit.at >= 4:
                    sp.wait_ge(lo_done, c.unit.value(-3, times=2))
                c.unit.at += 1
                return (c.unit.at - 1) % 4

            def load(w, k, col):
                slot = slot_free()
                sp.dma_start(RAW[slot][:, :, :], w[:, bass.ds(k, 4), bass.ds(col, COLS)]).then_inc(raw_in[slot], 16)

            def group(w, col, kq=4):
                for q in range(kq):
                    load(w, 4 * q, col)

            def ffn(wg, gcol, wu, ucol, wd):
                def gate_up(i):
                    group(wg, gcol + i * COLS)
                    group(wu, ucol + i * COLS)

                def down(i):
                    for n in range(4):
                        load(wd, i * 4, n * COLS)

                gate_up(0)
                gate_up(1)
                down(0)
                with sp.Fori(2, NF) as i:
                    c.enter(i - 2, unit=12)
                    gate_up(i)
                    down(i - 1)
                c.leave(NF - 2)
                down(NF - 1)

            sp.dma_start(BASE[:, :], base_const).then_inc(base_in, 16)
            for n, source in enumerate(c_rows):
                sp.dma_start(CRAW[16 * n:16 * n + 16, :], source).then_inc(c_in, 16)
            sp.dma_start(yf[:, 0:D], x[0:P, :]).then_inc(x_rows, 16)
            sp.dma_start(yf[:, D:2 * D], x[P:2 * P, :]).then_inc(x_rows, 16)
            for col in (0, 2 * LRU):
                group(w_in, col)
                group(w_in, col + COLS)
            c.ada.at = SP_GROUP * KT
            for u in range(8):
                load(w_in, 4 * (u % 4), LRU + u // 4 * COLS)
                for k in (2 * u, 2 * u + 1):
                    sp.wait_ge(ada_op, c.ada.value(-3))
                    sp.dma_start(ADA[c.ada.at % 4], ada_w[0][:, k, SP_GROUP * ADA_COLS:(SP_GROUP + 1) * ADA_COLS])\
                        .then_inc(ada_in_sp[c.ada.at % 4], 16)
                    c.ada.at += 1
            for g in range(4):
                group(w_out, g * COLS)
            ffn(w_gate, 0, w_up, 0, w_down)
            group(w_in2, 0)
            group(w_in2, 512)
            OFF = 2 * 512 + 64
            with sp.Fori(0, 3) as i:
                c.enter(i, unit=8)
                group(w_in2, OFF + i * 1024)
                group(w_in2, OFF + 512 + i * 1024)
            c.leave(3)

            slot = slot_free()
            dst = RAW[slot][:, :, :].rearrange("p a (b n) -> p (a b) n", n=P)
            for half in (0, 64):
                sp.dma_start(dst[:, :, half:half + 64], w_in2[:, :, 1024:1088]).then_inc(raw_in[slot], 16)
            with sp.Fori(3, 7) as i:
                c.enter(i - 3, unit=8)
                group(w_in2, OFF + i * 1024)
                group(w_in2, OFF + 512 + i * 1024)
            c.leave(4)

            def heads(w, per, at, n, first, count):
                slot = slot_free()
                for k in range(4):
                    sp.dma_start(RAW[slot][:, k, :].rearrange("p (h n) -> p h n", n=n),
                                 w[:, k, :].rearrange("p (h m) -> p h m", m=per)[:, first:first + count, at:at + n])\
                        .then_inc(raw_in[slot], 16)

            heads(w_uq, 192, 0, 128, 0, 4)
            heads(w_uq, 192, 0, 128, 4, 4)
            heads(w_uq, 192, 128, 64, 0, 8)
            heads(w_ukv, 256, 0, 128, 0, 4)
            heads(w_ukv, 256, 0, 128, 4, 4)
            heads(w_ukv, 256, 128, 128, 0, 4)
            heads(w_ukv, 256, 128, 128, 4, 4)
            with sp.Fori(0, 2) as i:
                c.enter(i, unit=4)
                group(w_pb, i * 2 * COLS, 2)
                group(w_pb, i * 2 * COLS + COLS, 2)
            c.leave(2)
            for g in MERGED:
                group(w_pa, g * COLS, 2)
            for q in MERGED:
                load(w_out2, 4 * q, 0)
            for g in range(1, 4):
                group(w_out2, g * COLS)
            ffn(w_ffin2, 0, w_ffin2, D_FF, w_ffout2)
            assert c.unit.at == N_UNITS
            for n in range(8):
                q, tb = n // 2, n % 2
                sp.wait_ge(out_ready, n + 1)
                sp.dma_start(out[tb * P:(tb + 1) * P, q * 512:(q + 1) * 512], yf[:, n * 512:(n + 1) * 512])\
                    .then_inc(s_out, 16)
            sp.wait_ge(s_out, 8 * 16)

        EXTRA = {U_KPE: 1, **{U_LAT + n: 3 for n in range(7)}}

        def landed(eng, c):
            n = c.unit.at
            extra = sum(v for u, v in EXTRA.items() if u % 4 == n % 4 and u <= n)
            eng.wait_ge(raw_in[n % 4], c.unit.value(0, times=16, over=4) + 16 * (1 + extra))

        @block.gpsimd
        def _(pool):
            c = Counts()

            def ada(layer, col):
                for k in range(KT):
                    slot = c.ada.at % 4
                    if c.ada.at >= 4:
                        pool.wait_ge(ada_op, c.ada.value(-3))
                    pool.dma_start(ADA[slot], ada_w[layer][:, k, bass.ds(col, ADA_COLS)])\
                        .then_inc(ada_in[slot], 16)
                    c.ada.at += 1

            def step(ins):
                c.chain.at += 1
                ins.then_inc(pool_chain, 1)
                pool.wait_ge(pool_chain, c.chain.value())

            for g in range(4):
                ada(0, g * ADA_COLS)
            step(pool.memset(tiles(48, 8), 0.0))
            for n, w in enumerate((rg_a, rg_i)):
                dst = tiles(48 + 4 * n, 4).rearrange("p (t j) -> p t j", j=P)
                for half in range(2):
                    pool.dma_start(dst[64 * half:64 * half + 64, :, 64 * half:64 * half + 64], w[half])\
                        .then_inc(mix_w, 16)
            pool.dma_start(tiles(56, 8).rearrange("p (g n) -> p g n", n=T), w_pool).then_inc(mix_w, 16)
            with pool.Fori(0, 2) as i:
                c.enter(i, ada=KT)
                ada(0, i * ADA_COLS + 4 * ADA_COLS)
            c.leave(2)

            sums = [YF[:, 12:14, :], YF[:, 14:16, :]]

            def window(g):
                src = R[:, 16 + 2 * g:18 + 2 * g, :]
                cur, w = src, 2 << g
                for level in range(g + 1):
                    dst, s = sums[level % 2], 1 << level
                    step(pool.tensor_copy(dst[:, :, 0:s], cur[:, :, 0:s]))
                    step(pool.tensor_tensor(dst[:, :, s:T], cur[:, :, s:T], cur[:, :, 0:T - s], ALU.add))
                    cur = dst
                inv = BASE[:, INV + 16 * g:INV + 16 * g + w]
                for a in range(2):
                    step(pool.tensor_tensor(cur[:, a, 0:w], cur[:, a, 0:w], inv, ALU.mult))
                step(pool.tensor_scalar(cur[:, :, w:T], cur[:, :, w:T], 1.0 / w, 1.0, ALU.mult, ALU.mult))
                pool.tensor_tensor(src, cur, src, ALU.subtract).then_inc(pooled, 1)
                pool.wait_ge(pooled, g + 1)

            pool.wait_ge(base_in, 16)
            pool.wait_ge(free["A"], 2)
            pool.wait_ge(free["B"], 2)
            for g in range(4):
                window(g)
            pool.wait_ge(rg_sig, 16)
            pool.wait_ge(conv_step, 24)
            pool.tensor_tensor(tiles(40, 8), tiles(40, 8), tiles(24, 8), ALU.mult).then_inc(ix_done, 1)
            c.ada.at += KT
            for b in (7, 8, 9, 10, 11):
                ada(0, b * ADA_COLS)
            with pool.Fori(0, 10) as i:
                c.enter(i, ada=KT)
                ada(1, i * ADA_COLS)
            c.leave(10)
            pool.wait_ge(ada_op, c.ada.value())
            pool.dma_start(CON, att_const).then_inc(con_in, 16)
            pool.dma_start(tiles(73, 1).bitcast(I32), positions.to_broadcast([P, T])).then_inc(pos_in, 16)
            pool.wait_ge(free["B"], B_PROJ + 2)
            for g in (10, 11):
                ada(1, g * ADA_COLS)

        @block.scalar
        def _(act):
            c = Counts()

            def step(ins):
                c.chain.at += 1
                ins.then_inc(act_chain, 1)
                act.wait_ge(act_chain, c.chain.value())

            def hi(n=1):
                for _ in range(n):
                    j, slot = c.sub.at % 2, c.unit.at % 4
                    if j == 0:
                        landed(act, c)
                    if c.sub.at >= 2:
                        act.wait_ge(pe_sub, c.sub.value(-1))
                    nc.scalar.activation(WHI[j][:, :, :], RAW[slot][:, 2 * j:2 * j + 2, :], ACT.Copy)\
                        .then_inc(hi_done, 1)
                    c.sub.at += 1
                    c.unit.at += j

            def copy_out(pair, dst, func=ACT.Copy):
                act.wait_ge(pe_sub, c.sub.value(-2))
                nc.scalar.activation(dst, flat(pair), func).then_inc(free[pair], 1)

            def split(waits, src=YF, first=0):
                for q, (s, v) in enumerate(waits, first):
                    act.wait_ge(s, v)
                    nc.scalar.activation(H[:, 4 * q:4 * q + 4, 0:T], src[:, 4 * q:4 * q + 4, :], ACT.Copy)\
                        .then_inc(h_hi, 1)

            def square(q, ready, value):
                act.wait_ge(ready, value)
                nc.scalar.activation(YF[:, 4 * q:4 * q + 4, :], X[:, 4 * q:4 * q + 4, :], ACT.Square)\
                    .then_inc(sq_ready, 1)

            def rms(k, rs=RS[:, :]):
                act.wait_ge(ms_ready, k + 1)
                nc.scalar.activation(rs, rs, ACT.Sqrt).then_inc(rt_ready, 1)

            def split_shifted(quads, shift, groups):
                act.wait_ge(ada_bias, groups)
                for q in range(4):
                    act.wait_ge(yf_quad, quads + q + 1)
                    for t in range(4 * q, 4 * q + 4):
                        ins = nc.scalar.activation(H[:, t, 0:T], YF[:, t, :], ACT.Identity,
                                                   bias=MOD[:, shift + t:shift + t + 1])
                    ins.then_inc(h_hi, 1)

            def win_body(tile, skip=0, before=ACT.Copy, func=ACT.Copy):
                at = lambda n: rf[:, bass.ds((tile + n) * T, 4 * T)]
                for s in range(skip, 16):
                    hi()
                    if s == 1:
                        copy_out("B", at(-4), before)
                    if s == 9:
                        copy_out("A", at(0), func)

            def ffn(quad_done=None):
                def gate():
                    act.wait_ge(pe_sub, c.sub.value(-2))
                    if c.gate.at:
                        act.wait_ge(hid_lo, c.gate.value())
                    nc.scalar.activation(G, flat("A"), ACT.Silu).then_inc(gate_done, 1)
                    c.gate.at += 1

                def hidden(dst=HID):
                    act.wait_ge(up_done, c.hid.value(1))
                    nc.scalar.activation(dst[:, :, 0:T], G.rearrange("p (a b) -> p a b", a=4), ACT.Copy)\
                        .then_inc(hid_hi, 1)
                    c.hid.at += 1

                def body(skip=0, subs=24, previous=True, last=False):
                    for s in range(skip, subs):
                        hi()
                        if s == 2 and previous:
                            hidden()
                        if s == 9:
                            gate()
                        if s == 21 and last:
                            hidden(HID_LAST)

                body(skip=2, subs=16, previous=False)
                body()
                with act.Fori(2, NF - 1) as i:
                    c.enter(i - 2, unit=12, sub=24, hid=1, gate=1)
                    body()
                c.leave(NF - 3)
                body(last=True)
                for s in range(8):
                    hi()
                    if quad_done and s in (5, 7):
                        quad_done((s - 5) // 2)

            act.wait_ge(c_t, 1)
            nc.scalar.activation(CA[:, :], MISC[:, 0:32], ACT.Silu).then_inc(cact, 1)
            for block_at, r, n, c0, c1, src in rows_src:
                if block_at == BLOCKS - 1:
                    act.wait_ge(praw_zero, 1)
                act.dma_start(PRAW[r:r + n, block_at, c0:c1], src).then_inc(rows_in, 16)

            hi(2)
            for q in range(4):
                square(q, x_in, 8)
            rms(0)
            split_shifted(0, mod_at(0, 0), 4)
            for s in range(2, 16):
                hi()
                if s == 9:
                    copy_out("A", tiles(0, 4))
            soft = SM[:, 8:16]

            def sigmoids(n):
                act.wait_ge(rg_mm, 4 * n + 4)
                name, kind = ("b_rg_a", "b_rg_i")[n // 2], n // 2
                for t in range(n % 2 * 4, n % 2 * 4 + 4):
                    nc.scalar.activation(R[:, 32 + 8 * kind + t, :], flat("C")[:, t % 4 * T:(t % 4 + 1) * T],
                                         ACT.Sigmoid, bias=PRM[:, COL[name] + t:COL[name] + t + 1]).then_inc(rg_sig, 1)

            for s in range(16):
                hi()
                if s == 1:
                    copy_out("B", tiles(4, 4))
                    act.wait_ge(free["A"], 1)
                    act.wait_ge(free["B"], 1)
                    for t in range(8):
                        nc.scalar.activation(R[:, 24 + t, :], R[:, t, :], ACT.Identity, scale=tap(3, t),
                                             bias=PRM[:, COL["b_conv"] + t:COL["b_conv"] + t + 1])\
                            .then_inc(conv_first, 1)
                if s == 3:
                    step(nc.scalar.activation(soft, PRM[:, COL["lru_lambda"]:COL["lru_lambda"] + 8], ACT.Abs))
                    step(nc.scalar.activation(soft, soft, ACT.Exp, scale=-1.0))
                    nc.scalar.activation(soft, soft, ACT.Ln, bias=1.0).then_inc(lam_done, 1)
                if s == 9:
                    copy_out("A", tiles(16, 4))
            for s in range(16):
                hi()
                if s == 0:
                    sigmoids(0)
                if s == 1:
                    copy_out("B", tiles(20, 4))
                if s in (4, 7, 10):
                    sigmoids((s - 1) // 3)
                if s in (5, 6):
                    act.wait_ge(c8_done, 1)
                    act.wait_ge(rg_sig, 8)
                    for t in range(4 * (s - 5), 4 * (s - 5) + 4):
                        nc.scalar.activation(R[:, t, :], R[:, 32 + t, :], ACT.Exp, scale=SM[:, t:t + 1])\
                            .then_inc(a_done, 1)
                if s in (8, 9):
                    act.wait_ge(a_done, 8)
                    for t in range(4 * (s - 8), 4 * (s - 8) + 4):
                        nc.scalar.activation(R[:, 32 + t, :], R[:, 32 + t, :], ACT.Tanh, scale=SM[:, t:t + 1])\
                            .then_inc(tanh_done, 1)
                if s == 9:
                    copy_out("A", tiles(8, 4))
                if s == 14:
                    act.wait_ge(m2_done, 1)
                    nc.scalar.activation(tiles(32, 8), tiles(48, 8), ACT.Sqrt, scale=-1.0).then_inc(root_done, 1)
            hi(2)
            copy_out("B", tiles(12, 4))
            act.wait_ge(free["A"], 3)
            act.wait_ge(free["B"], 3)
            nc.scalar.activation(tiles(8, 8), tiles(8, 8), ACT.Gelu_apprx_tanh).then_inc(gelu_done, 1)
            for t in range(8):
                act.wait_ge(pool_mm, t // 2 * 2 + 2)
                nc.scalar.activation(YF[:, 8 + t, :], eight(t), ACT.Copy,
                                     scale=PRM[:, COL["ls_pool"] + t:COL["ls_pool"] + t + 1]).then_inc(pool_ev, 1)
            split([(yf_quad, 5), (yf_quad, 6), (pool_ev, 4), (pool_ev, 8)])

            def w_out_squares(pairs):
                for g in range(4):
                    for s in range(8):
                        if g or s >= 2:
                            hi()
                        if g and s == 3:
                            square(g - 1, *pairs[g - 1])
                hi(2)
                square(3, *pairs[3])

            w_out_squares([(free["A"], 4), (free["B"], 4), (free["A"], 5), (free["B"], 5)])
            rms(1)
            split_shifted(6, mod_at(0, 3), 10)
            def squares(q):
                square(q, x_step, 4 * q + 4)
                for t in range(4 * q, 4 * q + 4):
                    ins = nc.scalar.activation(R[:, GAINED + t, :], X[:, t, :], ACT.Square,
                                               scale=PRM[:, COL["g_norm_final"] + t:COL["g_norm_final"] + t + 1])
                ins.then_inc(sq_ready, 1)

            ffn(squares)
            hi(2)
            squares(2)
            squares(3)
            rms(2)
            rms(3, RS2)
            split_shifted(10, mod_at(1, 0), 16)
            for s in range(2, 16):
                hi()
                if s == 9:
                    copy_out("A", tiles(0, 4))
            with act.Fori(0, 2) as i:
                c.enter(i, unit=8, sub=16)
                win_body(i * 8 + 8)
            c.leave(2)
            for s in range(16):
                hi()
                if s == 1:
                    copy_out("B", tiles(20, 4))
                if s in (3, 5):
                    n = (s - 3) // 2
                    nc.scalar.activation(YF[:, 4 * n:4 * n + 4, :], R[:, 4 * n:4 * n + 4, :], ACT.Square)\
                        .then_inc(lat_sq, 1)
                if s == 9:
                    copy_out("A", tiles(24, 4))
                if s == 11:
                    act.wait_ge(lat_ms, 1)
                    nc.scalar.activation(YF[:, 8:10, :], YF[:, 8:10, :], ACT.Sqrt).then_inc(lat_rt, 1)
            hi(2)
            copy_out("B", tiles(28, 4))

            for hp in range(4):
                for s in range(16):
                    hi()
                    if s == 1 and hp == 0:
                        act.wait_ge(pe_sub, c.sub.value(-2))
                        nc.scalar.activation(KPE, PAIR["C"][:, 0, 0:T], ACT.Copy).then_inc(free["C"], 1)
                    if s == 1 and hp:
                        copy_out("B", tiles(8 * hp + 28, 4), ACT.Sigmoid)
                    if s == 3:
                        act.wait_ge(z_dve, hp + 1)
                        step(nc.scalar.activation(tiles(81, 3), tiles(78, 3), ACT.Abs))
                    if s == 4:
                        step(nc.scalar.activation(tiles(81, 3), tiles(81, 3), ACT.Exp, scale=-1.0))
                    if s == 5:
                        nc.scalar.activation(tiles(81, 3), tiles(81, 3), ACT.Ln, bias=1.0).then_inc(z_act, 1)
                    if s == 7 and hp == 1:
                        act.wait_ge(lat_ev, 1)
                        nc.scalar.activation(HQ[:, :, 0:T], R[:, 0:4, :], ACT.Copy).then_inc(h_hi, 1)
                    if s == 9:
                        copy_out("A", tiles(8 * hp + 32, 4), ACT.Sigmoid)
                    if s == 10:
                        act.wait_ge(w_dve, hp + 1)
                        nc.scalar.activation(tiles(81, 3), tiles(84, 3), ACT.Exp).then_inc(a_act, 1)
                    if s == 13 and hp == 0:
                        act.wait_ge(ang_done, 2)
                        for n in range(2):
                            nc.scalar.activation(CS[n], tiles(74 + n, 1), ACT.Sin).then_inc(trig_done, 1)
                    if s == 15:
                        act.wait_ge(y_mm, hp + 1)
                        nc.scalar.activation(yf[:, (8 + 2 * hp) * T:(10 + 2 * hp) * T], PAIR["C"][:, 0, :], ACT.Copy)\
                            .then_inc(y_ev, 1)
            hi(2)
            copy_out("B", tiles(60, 4), ACT.Sigmoid)

            def head_squares(hp):
                if hp:
                    act.wait_ge(hd_ss, hp)
                nc.scalar.activation(tiles(78, 2), tiles(8 + 2 * hp, 2), ACT.Square).then_inc(hd_sq, 1)
                nc.scalar.activation(tiles(80, 1), tiles(16 + hp, 1), ACT.Square).then_inc(hd_sq, 1)
                nc.scalar.activation(tiles(81, 2), tiles(2 * hp, 2), ACT.Square).then_inc(hd_sq, 1)

            def head_roots(hp):
                act.wait_ge(hd_ms, hp + 1)
                nc.scalar.activation(tiles(73, 4), tiles(73, 4), ACT.Sqrt).then_inc(hd_rt, 1)

            split([(lat_ev, 1)], src=R, first=1)
            for n in range(7):
                hi(2)
                copy_out(LAT[n][0], tiles(LAT[n][1], 4))
                if n in (1, 2):
                    split([(y_ev, 2 * n)], first=n + 1)
                if n == 3:
                    act.wait_ge(free["A"], A_LAT - 1)
                    act.wait_ge(free["C"], C_LAT)
                    nc.scalar.activation(tiles(77, 1), KPE, ACT.Square).then_inc(hd_sq, 1)
                    head_squares(0)
                if n == 4:
                    head_roots(0)
            act.wait_ge(free["A"], A_LAT)
            act.wait_ge(free["B"], B_LAT)

            for hp in range(4):
                if hp < 3:
                    head_squares(hp + 1)
                    head_roots(hp + 1)
                act.wait_ge(s_dve, hp + 1)
                for a in range(2):
                    for qb, (k0, k1) in enumerate(((0, 128), (128, 384))):
                        n = 2 * a + qb
                        ins = nc.scalar.activation(SC[:, a, k0:k1], SC[:, a, k0:k1], ACT.Exp, bias=SM[:, n:n + 1],
                                                   accum_out=SM[:, 4 + n:5 + n])
                ins.then_inc(p_act, 1)
                hi(2)
                act.wait_ge(pt_mm, hp + 1)
                nc.scalar.activation(SC, PAIR["B"][:, :, 0:384], ACT.Copy).then_inc(pt_ev, 1)
                hi(2)
                act.wait_ge(o_mm, hp + 1)
                nc.scalar.activation(yf[:, 2 * hp * T:(2 * hp + 2) * T], MISC, ACT.Copy).then_inc(o_ev, 1)
                if hp % 2:
                    split([(o_ev, hp + 1)], first=hp // 2)

            for n in range(4):
                for t in range(4):
                    if n or t >= 2:
                        hi()
                    if t == 3 and n in (1, 2):
                        split([(free["AB"[n - 1]], (A_LAT, B_LAT)[n - 1] + 1)], first=MERGED[n - 1])
            hi(2)
            split([(free["A"], A_LAT + 2), (free["B"], B_LAT + 2)], first=0)
            w_out_squares([(free["A"], A_PROJ + 1), (free["B"], B_PROJ + 1), (free["A"], A_PROJ + 2),
                           (free["B"], B_PROJ + 2)])
            rms(4)
            split_shifted(14, mod_at(1, 3), 22)
            ffn()
            assert c.unit.at == N_UNITS
            for n in range(8):
                act.wait_ge(x_turned, 8 + n + 1)
                nc.scalar.activation(yf[:, n * 512:(n + 1) * 512], OUT_BANKS[n % 4], ACT.Copy).then_inc(out_ready, 1)

        @block.vector
        def _(dve):
            c = Counts()

            def step(ins):
                c.chain.at += 1
                ins.then_inc(dve_chain, 1)
                dve.wait_ge(dve_chain, c.chain.value())

            def lo(n=1):
                for _ in range(n):
                    j, slot = c.sub.at % 2, c.unit.at % 4
                    dve.wait_ge(hi_done, c.sub.value(1))
                    nc.vector.tensor_tensor(WLO[j][:, :, :], RAW[slot][:, 2 * j:2 * j + 2, :],
                                            WHI[j][:, :, :].bitcast(F32), ALU.subtract).then_inc(lo_done, 1)
                    c.sub.at += 1
                    c.unit.at += j

            def ada(kt, layer, acc=ACC):
                slot = c.ada.at % 4
                if SP_GROUP * KT <= c.ada.at < (SP_GROUP + 1) * KT:
                    dve.wait_ge(ada_in_sp[slot], kt // 4 * 16 + 16)
                else:
                    by_sp = KT if c.ada.at > SP_GROUP * KT else 0
                    dve.wait_ge(ada_in[slot], c.ada.value(4 - by_sp, times=16, over=4))
                scalar = CA[:, 16 * layer + kt:16 * layer + kt + 1]
                if kt == 0:
                    if c.ada_group.at:
                        dve.wait_ge(ada_red, c.ada_group.value())
                    ins = nc.vector.tensor_scalar(acc, ADA[slot], scalar, None, ALU.mult)
                else:
                    dve.wait_ge(ada_op, c.ada.value())
                    ins = nc.vector.scalar_tensor_tensor(acc, ADA[slot], scalar, acc, ALU.mult, ALU.add)
                ins.then_inc(ada_op, 1)
                c.ada.at += 1

            def ada_beside(layer, s, subs):
                for kt in range(KT):
                    if ADA_AFTER[subs][kt] == s:
                        ada(kt, layer)
                if s == subs - 1:
                    ada_end()

            def ada_end():
                dve.wait_ge(ada_red, c.ada_group.value(1))
                at = c.ada_group.value(0, times=8)
                nc.vector.tensor_tensor(MOD[:, bass.ds(at, 8)], SMALL[:, 0:8], PRM[:, bass.ds(at, 8)], ALU.add)\
                    .then_inc(ada_bias, 1)
                c.ada_group.at += 1

            def split(n_quads=4, src=YF, first=0):
                for q in range(first, first + n_quads):
                    c.quad.at += 1
                    dve.wait_ge(h_hi, c.quad.value())
                    nc.vector.tensor_tensor(H[:, 4 * q:4 * q + 4, T:2 * T], src[:, 4 * q:4 * q + 4, :],
                                            H[:, 4 * q:4 * q + 4, 0:T].bitcast(F32), ALU.subtract).then_inc(h_quad, 1)

            def root(k):
                dve.wait_ge(ssq_ready, k + 1)
                nc.vector.tensor_scalar(RS[:, :], MISC[:, 0:T], 1.0 / D, EPS, ALU.mult, ALU.add).then_inc(ms_ready, 1)
                dve.wait_ge(rt_ready, k + 1)
                step(nc.vector.reciprocal(RS[:, :], RS[:, :]))

            def modulated(k, gain, shift, scale, groups, final=False):
                dve.wait_ge(ada_bias, groups)
                step(nc.vector.scalar_tensor_tensor(MC[:, :], MOD[:, scale:scale + 16], 1.0, PRM[:, gain:gain + 16],
                                                    ALU.add, ALU.mult))
                rs = RS[:, :]
                root(k)
                if final:
                    rs = RS2
                    dve.wait_ge(ssq_ready, k + 2)
                    step(nc.vector.scalar_tensor_tensor(rs, SMALL[:, 0:T], 1.0 / D, RS[:, :], ALU.mult, ALU.mult))
                    step(nc.vector.tensor_tensor(rs, rs, RS[:, :], ALU.mult))
                    nc.vector.tensor_scalar(rs, rs, EPS, None, ALU.add).then_inc(ms_ready, 1)
                    dve.wait_ge(x_step, KT)
                for q in range(5):
                    if q < 4 and final:
                        for t in range(4 * q, 4 * q + 4):
                            ins = nc.vector.scalar_tensor_tensor(X[:, t, :], X[:, t, :],
                                                                 PRM[:, COL["g_norm_final"] + t:
                                                                     COL["g_norm_final"] + t + 1],
                                                                 RS[:, :], ALU.mult, ALU.mult)
                        ins.then_inc(x_done, 1)
                        dve.wait_ge(x_done, q + 1)
                        if q == 0:
                            dve.wait_ge(rt_ready, k + 2)
                            step(nc.vector.reciprocal(rs, rs))
                    if q < 4:
                        for t in range(4 * q, 4 * q + 4):
                            ins = nc.vector.scalar_tensor_tensor(YF[:, t, :], X[:, t, :], MC[:, t:t + 1], rs,
                                                                 ALU.mult, ALU.mult)
                        ins.then_inc(yf_quad, 1)
                    if q > 0:
                        c.quad.at += 1
                        dve.wait_ge(h_hi, c.quad.value())
                        for t in range(4 * q - 4, 4 * q):
                            ins = nc.vector.scalar_tensor_tensor(H[:, t, T:2 * T], YF[:, t, :],
                                                                 MOD[:, shift + t:shift + t + 1],
                                                                 H[:, t, 0:T].bitcast(F32), ALU.add, ALU.subtract)
                        ins.then_inc(h_quad, 1)

            def residual(pair, g, gate):
                dve.wait_ge(pe_sub, c.sub.value(-2))
                for t in range(4):
                    ins = nc.vector.scalar_tensor_tensor(X[:, 4 * g + t, :], flat(pair)[:, t * T:(t + 1) * T],
                                                         MOD[:, gate + 4 * g + t:gate + 4 * g + t + 1],
                                                         X[:, 4 * g + t, :], ALU.mult, ALU.add)
                ins.then_inc(free[pair], 1)

            def win_body(layer=None, skip=0):
                for s in range(16):
                    if s >= skip:
                        lo()
                    if layer is not None:
                        ada_beside(layer, s, 16)

            def ffn(layer, loops, gate, a_free, c_free, groups, more):
                def product():
                    dve.wait_ge(pe_sub, c.sub.value(-2))
                    dve.wait_ge(gate_done, c.hid.value(1))
                    nc.vector.tensor_tensor(G, flat("B"), G, ALU.mult).then_inc(up_done, 1)

                def hidden(dst=HID):
                    dve.wait_ge(hid_hi, c.hid.value(1))
                    nc.vector.tensor_tensor(dst[:, :, T:2 * T], G.rearrange("p (a b) -> p a b", a=4),
                                            dst[:, :, 0:T].bitcast(F32), ALU.subtract).then_inc(hid_lo, 1)
                    c.hid.at += 1

                def add_down(n, back=2, gate=None):
                    dve.wait_ge(pe_sub, c.sub.value(-back))
                    pair, part = "AC"[n % 2], yf[:, n * 1024:(n + 1) * 1024]
                    ins = nc.vector.tensor_tensor(part, flat(pair), part, ALU.add)
                    ins.then_inc(free[pair], 1)
                    if gate is not None:
                        dve.wait_ge(free[pair], (a_free if pair == "A" else c_free) - (n < 2))
                        for t in range(4 * n, 4 * n + 4):
                            nc.vector.scalar_tensor_tensor(X[:, t, :], YF[:, t, :], MOD[:, gate + t:gate + t + 1],
                                                           X[:, t, :], ALU.mult, ALU.add).then_inc(x_step, 1)

                def body(skip=0, subs=24, up=True, previous=True, layer=None, last=False):
                    for s in range(subs):
                        if s >= skip:
                            lo()
                        if s == 1 and up:
                            product()
                        if s == 2 and previous:
                            add_down(3, 3)
                        if s == 3 and up:
                            hidden()
                        if s in (19, 21, 23):
                            add_down((s - 19) // 2)
                        if s == 20 and last:
                            product()
                        if s == 22 and last:
                            hidden(HID_LAST)
                        if layer is not None:
                            ada_beside(layer, s, subs)

                body(skip=2, subs=16, up=False, previous=False, layer=layer)
                step(nc.vector.memset(yf, 0.0))
                body(previous=False, layer=layer)
                for first, last, beside in ((2, 2 + loops, 1), (2 + loops, NF - 1, 0)):
                    if first < last:
                        with dve.Fori(first, last) as i:
                            c.enter(i - first, unit=12, sub=24, hid=1, ada=KT * beside, ada_group=beside)
                            body(layer=1 if beside else None)
                        c.leave(last - first)
                body(last=True)
                dve.wait_ge(ada_bias, groups)
                for s in range(8):
                    lo()
                    if s == 2:
                        add_down(3, 3)
                    if s in (3, 5, 7):
                        add_down((s - 3) // 2, gate=gate)
                lo(2 * more)
                add_down(3, 2 * more, gate)

            nc.vector.memset(PRAW[:, BLOCKS - 1, :], 0.0).then_inc(praw_zero, 1)
            dve.wait_ge(cact, 1)
            for kt in range(KT):
                ada(kt, 0)
            dve.wait_ge(prm_t, 1)
            nc.vector.tensor_copy(PRM[:, :], MISC[:, 0:BLOCKS * P]).then_inc(prm_ready, 1)
            for n in range(8):
                dve.wait_ge(x_turned, n + 1)
                nc.vector.tensor_copy(X[:, 2 * n:2 * n + 2, :].rearrange("p a b -> p (a b)"),
                                      PS[n // 2 % 2][:, n % 2, :]).then_inc(x_in, 1)
            dve.wait_ge(prm_ready, 1)
            dve.wait_ge(x_in, 8)
            for g in range(1, 4):
                for kt in range(KT):
                    ada(kt, 0, (ACC, G)[g % 2])
                    if kt == 3:
                        ada_end()
            lo(2)
            ada_end()
            modulated(0, COL["g_norm_mix"], mod_at(0, 0), mod_at(0, 1), 4)
            win_body(0, skip=2)
            def convolution(t):
                dve.wait_ge(conv_first, t + 1)
                for n, j in enumerate((2, 1, 0)):
                    s = 3 - j
                    if n:
                        dve.wait_ge(conv_step, 3 * t + n)
                    nc.vector.scalar_tensor_tensor(R[:, 24 + t, s:T], R[:, t, 0:T - s], tap(j, t), R[:, 24 + t, s:T],
                                                   ALU.mult, ALU.add).then_inc(conv_step, 1)

            for s in range(16):
                lo()
                ada_beside(0, s, 16)
                if 3 <= s < 11:
                    convolution(s - 3)
                if s == 11:
                    dve.wait_ge(lam_done, 1)
                    step(nc.vector.scalar_tensor_tensor(SM[:, 0:8], PRM[:, COL["lru_lambda"]:COL["lru_lambda"] + 8],
                                                        0.0, SM[:, 8:16], ALU.min, ALU.subtract))
                    nc.vector.tensor_scalar(SM[:, 0:8], SM[:, 0:8], 8.0, None, ALU.mult).then_inc(c8_done, 1)
            for s in range(16):
                lo()
                ada_beside(0, s, 16)
                if s >= 14:
                    for kt in range((s - 14) * ADA_BEFORE_W_OUT // 2, (s - 13) * ADA_BEFORE_W_OUT // 2):
                        ada(kt, 0, G)
                if s == 11:
                    dve.wait_ge(a_done, 8)
                    dve.wait_ge(rg_mm, 16)
                    step(nc.vector.tensor_tensor(tiles(48, 8), tiles(0, 8), tiles(0, 8), ALU.mult))
                if s == 12:
                    dve.wait_ge(tanh_done, 8)
                    nc.vector.scalar_tensor_tensor(tiles(48, 8), tiles(48, 8), 1.0, tiles(32, 8), ALU.add, ALU.mult)\
                        .then_inc(m2_done, 1)
            lo(2)
            dve.wait_ge(root_done, 1)
            dve.wait_ge(ix_done, 1)
            step(nc.vector.tensor_tensor(tiles(40, 8), tiles(40, 8), tiles(32, 8), ALU.mult))
            for t in range(8):
                ins = nc.vector.tensor_tensor_scan(R[:, 24 + t, :], R[:, t, :], R[:, 40 + t, :], 0.0, ALU.mult, ALU.add)
            step(ins)
            dve.wait_ge(gelu_done, 1)
            for q in range(2):
                nc.vector.tensor_tensor(YF[:, 4 * q:4 * q + 4, :], R[:, 24 + 4 * q:28 + 4 * q, :],
                                        R[:, 8 + 4 * q:12 + 4 * q, :], ALU.mult).then_inc(yf_quad, 1)
            split()

            dve.wait_ge(ada_bias, 6)
            for g in range(4):
                for s in range(8):
                    if g or s >= 2:
                        lo()
                    if g and s == 1:
                        residual("BA"[g % 2], g - 1, mod_at(0, 2))
                    for n, kt in ADA_BESIDE_W_OUT[8 * g + s]:
                        if kt < KT:
                            ada(kt, 0, (G, ACC)[n % 2])
                        else:
                            ada_end()
            lo(2)
            residual("B", 3, mod_at(0, 2))
            modulated(1, COL["g_norm_ffn"], mod_at(0, 3), mod_at(0, 4), 10)
            ffn(0, NF - 4, mod_at(0, 5), A_FFN1, C_FFN1, 12, more=1)
            modulated(2, COL["g_norm1_2"], mod_at(1, 0), mod_at(1, 1), 16, final=True)
            lo(14)
            with dve.Fori(0, 2) as i:
                c.enter(i, unit=8, sub=16, ada=KT, ada_group=1)
                win_body(1)
            c.leave(2)
            for s in range(16):
                lo()
                ada_beside(1, s, 16)
                if s == 8:
                    dve.wait_ge(lat_ss, 2)
                    nc.vector.tensor_scalar(YF[:, 8:10, :], MISC.rearrange("p (a b) -> p a b", a=2), 1.0 / 512, EPS,
                                            ALU.mult, ALU.add).then_inc(lat_ms, 1)
                if s == 13:
                    dve.wait_ge(lat_rt, 1)
                    step(nc.vector.reciprocal(YF[:, 8:10, :], YF[:, 8:10, :]))
                if s in (14, 15):
                    n = s - 14
                    name = ("g_q_latent_2", "g_kv_latent_2")[n]
                    for t in range(4):
                        ins = nc.vector.scalar_tensor_tensor(R[:, 4 * n + t, :], R[:, 4 * n + t, :],
                                                             PRM[:, COL[name] + t:COL[name] + t + 1], YF[:, 8 + n, :],
                                                             ALU.mult, ALU.mult)
            ins.then_inc(lat_ev, 1)
            lo(2)

            whole, turns, ang = tiles(73, 1).bitcast(I32), tiles(76, 1), tiles(77, 1)
            c1 = 6.28125
            c2 = float(np.round((2 * np.pi - c1) * 2 ** 20) / 2 ** 20)
            c3 = float(2 * np.pi - c1 - c2)

            def angle(n):
                if n == 0:
                    dve.wait_ge(con_in, 16)
                    dve.wait_ge(pos_in, 16)
                    step(nc.vector.tensor_copy(turns, whole))
                    step(nc.vector.tensor_scalar(ang, turns, CON[:, FREQ:FREQ + 1], None, ALU.mult))
                quarter, shift = ((0.25, float(np.pi / 2)), (0.0, 0.0))[n]
                r = tiles(74 + n, 1)
                step(nc.vector.tensor_scalar(turns, ang, float(1 / (2 * np.pi)), quarter, ALU.mult, ALU.add))
                step(nc.vector.tensor_copy(whole, turns))
                step(nc.vector.tensor_copy(turns, whole))
                step(nc.vector.scalar_tensor_tensor(r, turns, -c1, ang, ALU.mult, ALU.add))
                step(nc.vector.scalar_tensor_tensor(r, turns, -c2, r, ALU.mult, ALU.add))
                step(nc.vector.scalar_tensor_tensor(r, turns, -c3, r, ALU.mult, ALU.add))
                step(nc.vector.tensor_scalar(r, r, shift, 3.1415925, ALU.add, ALU.min))
                nc.vector.tensor_scalar(r, r, -3.1415925, None, ALU.max).then_inc(ang_done, 1)

            both = lambda at: CON[:, at:at + 384].rearrange("p (a b) -> p a b", a=1).to_broadcast([P, 2, 384])
            for hp in range(4):
                for s in range(16):
                    lo()
                    if s == 2:
                        dve.wait_ge(z_mm, hp + 1)
                        step(nc.vector.scalar_tensor_tensor(three(78), PAIR["C"][:, :, 0:384], 128 ** -0.5,
                                                            both(SB_ONE), ALU.mult, ALU.mult))
                        nc.vector.tensor_tensor(three(78), three(78), both(SB_NEG), ALU.add).then_inc(z_dve, 1)
                    if s == 6:
                        dve.wait_ge(z_act, hp + 1)
                        if hp:
                            dve.wait_ge(a_act, hp)
                        nc.vector.scalar_tensor_tensor(tiles(84, 3), tiles(78, 3), 0.0, tiles(81, 3), ALU.max, ALU.add)\
                            .then_inc(sp_done, 1)
                    if s == 9:
                        dve.wait_ge(u_mm, hp + 1)
                        nc.vector.tensor_tensor(three(84), three(78), PS[3][:, :, 0:384], ALU.subtract)\
                            .then_inc(w_dve, 1)
                    if s == 8 and hp == 1:
                        c.quad.at += 1
                        dve.wait_ge(h_hi, c.quad.value())
                        nc.vector.tensor_tensor(HQ[:, :, T:2 * T], R[:, 0:4, :], HQ[:, :, 0:T].bitcast(F32),
                                                ALU.subtract).then_inc(h_quad, 1)
                    if s in (7, 11) and hp == 0:
                        angle((s - 7) // 4)
                    if s == 15 and hp == 0:
                        dve.wait_ge(trig_done, 2)
                        step(nc.vector.tensor_scalar(CS[1], CS[1], CON[:, SIGN:SIGN + 1], None, ALU.mult))
            lo(2)

            def merge_b(g):
                dve.wait_ge(pe_sub, c.sub.value(-2))
                nc.vector.tensor_tensor(tiles(48 + 4 * g, 4), flat("C"), tiles(48 + 4 * g, 4), ALU.mult)\
                    .then_inc(free["C"], 1)

            col = lambda name: PRM[:, COL[name]:COL[name] + 1]

            def head_means(hp):
                dve.wait_ge(hd_ss, hp + 1)
                nc.vector.tensor_scalar(tiles(73, 4), flat("C"), 1.0 / 192, EPS, ALU.mult, ALU.add).then_inc(hd_ms, 1)
                if hp == 0:
                    nc.vector.tensor_scalar(KPE, KPE, col("k_rope"), None, ALU.mult).then_inc(rope_in, 1)
                nc.vector.tensor_scalar(R[:, 16 + hp, :], R[:, 16 + hp, :], col("q_rope"), None, ALU.mult)\
                    .then_inc(rope_in, 1)

            def head_reciprocals(hp):
                dve.wait_ge(hd_rt, hp + 1)
                step(nc.vector.reciprocal(tiles(73, 4), tiles(73, 4)))

            def heads_scaled(hp):
                for a in range(2):
                    nc.vector.scalar_tensor_tensor(R[:, 8 + 2 * hp + a, :], R[:, 8 + 2 * hp + a, :], col("g_q_head_2"),
                                                   R[:, 73 + a, :], ALU.mult, ALU.mult)
                    nc.vector.scalar_tensor_tensor(R[:, 2 * hp + a, :], R[:, 2 * hp + a, :], col("g_k_head_2"),
                                                   R[:, 75 + a, :], ALU.mult, ALU.mult)
                dve.wait_ge(rope_swap, hp + 2)
                for n, tile in ((0, KPE), (1, R[:, 16 + hp, :])):
                    if n == 0 and hp:
                        continue
                    step(nc.vector.tensor_tensor(R[:, 86, :], SMALL[:, n * T:(n + 1) * T], CS[1], ALU.mult))
                    step(nc.vector.tensor_tensor(tile, tile, CS[0], ALU.mult))
                    step(nc.vector.tensor_tensor(tile, tile, R[:, 86, :], ALU.add))
                for a in range(2):
                    h = slice(64 * a, 64 * a + 64)
                    nc.vector.tensor_tensor(R[h, 16 + hp, :], R[h, 16 + hp, :], R[h, 73 + a, :], ALU.mult)
                    ins = nc.vector.tensor_tensor(R[h, KR(hp, a), :], R[h, 87, :], R[h, 75 + a, :], ALU.mult)
                ins.then_inc(hd_scaled, 1)

            split(1, src=R, first=1)
            for n in range(7):
                lo(2)
                if n in (1, 2):
                    split(1, first=n + 1)
                if n == 3:
                    step(nc.vector.memset(tiles(28, 4), 0.0))
                if n == 4:
                    head_means(0)
                    head_reciprocals(0)
                if n == 5:
                    heads_scaled(0)
            for hp in range(4):
                dve.wait_ge(s_mm, hp + 1)
                step(nc.vector.scalar_tensor_tensor(SC, PAIR["A"][:, :, 0:384], 192 ** -0.5, both(MLA_NEG), ALU.mult,
                                                    ALU.add))
                for a in range(2):
                    for qb, (k0, k1) in enumerate(((0, 128), (128, 384))):
                        n = 2 * a + qb
                        ins = nc.vector.tensor_reduce(SM[:, n:n + 1], SC[:, a, k0:k1], AX_X, ALU.max)
                step(ins)
                nc.vector.tensor_scalar(SM[:, 0:4], SM[:, 0:4], -1.0, None, ALU.mult).then_inc(s_dve, 1)
                if hp < 3:
                    head_means(hp + 1)
                    head_reciprocals(hp + 1)
                lo(2)
                dve.wait_ge(p_act, hp + 1)
                step(nc.vector.reciprocal(SM[:, 8:12], SM[:, 4:8]))
                for a in range(2):
                    for qb, (k0, k1) in enumerate(((0, 128), (128, 384))):
                        n = 8 + 2 * a + qb
                        ins = nc.vector.tensor_scalar(SC[:, a, k0:k1], SC[:, a, k0:k1], SM[:, n:n + 1], None, ALU.mult)
                ins.then_inc(p_dve, 1)
                if hp < 3:
                    heads_scaled(hp + 1)
                lo(2)
                merge_b(hp)
                if hp == 2:
                    split(1, first=0)
            split(1, first=1)

            def merge_a(n):
                dve.wait_ge(pe_sub, c.sub.value(-2))
                pair, g = "AB"[n % 2], MERGED[n]
                ga = tiles(32 + 4 * g, 4)
                step(nc.vector.tensor_tensor(ga, flat(pair), ga, ALU.mult))
                dve.wait_ge(free["C"], C_PROJ)
                nc.vector.tensor_tensor(yf[:, 4 * g * T:4 * (g + 1) * T], ga, tiles(48 + 4 * g, 4), ALU.add)\
                    .then_inc(free[pair], 1)

            for n in range(4):
                for t in range(4):
                    if n or t >= 2:
                        lo()
                    if n and t == 1:
                        merge_a(n - 1)
                    if t == 3 and n in (1, 2):
                        split(1, first=MERGED[n - 1])
            lo(2)
            merge_a(3)
            split(2, first=0)
            for g in range(4):
                for s in range(8):
                    if g or s >= 2:
                        lo()
                    if g and s == 1:
                        residual("BA"[g % 2], g - 1, mod_at(1, 2))
            lo(2)
            residual("B", 3, mod_at(1, 2))
            modulated(4, COL["g_norm2_2"], mod_at(1, 3), mod_at(1, 4), 22)
            ffn(1, 0, mod_at(1, 5), A_END, C_END, 24, more=0)
            assert c.unit.at == N_UNITS
        @block.tensor
        def _(pe):
            c = Counts()

            def mm(o, a, b, start, stop=False):
                return nc.tensor.matmul(o, a, b, start=start, stop=stop, skip_group_check=True)

            def sub(pair, src, k0, first, last, kind="W", counted=True):
                j, used, o = c.sub.at % 2, c.all[pair], PAIR[pair]
                pe.wait_ge(lo_done, c.sub.value(1))
                if first and used.at:
                    pe.wait_ge(free[pair], used.value())
                for k in range(8 if kind == "K" else 0):
                    kk, n = k0 + k, slice(k % 4 * P, (k % 4 + 1) * P)
                    mm(o[:, 0, 0:T], WHI[j][:, k // 4, n], src[:, kk, 0:T], first and k == 0)
                    mm(o[:, 0, 0:T], WHI[j][:, k // 4, n], src[:, kk, T:2 * T], False)
                    ins = mm(o[:, 0, 0:T], WLO[j][:, k // 4, n], src[:, kk, 0:T], False, last and k == 7)
                for k in range(0 if kind == "K" else 2):
                    kk, begin, end = k0 + k, first and k == 0, last and k == 1
                    if kind == "W":
                        for t in range(4):
                            dst, n = o[:, t // 2, (t % 2) * T:(t % 2 + 1) * T], slice(t * P, (t + 1) * P)
                            mm(dst, WHI[j][:, k, n], src[:, kk, 0:T], begin and t % 2 == 0)
                            mm(dst, WHI[j][:, k, n], src[:, kk, T:2 * T], False)
                            ins = mm(dst, WLO[j][:, k, n], src[:, kk, 0:T], False, end)
                    if kind == "T":
                        for tb in range(2):
                            hi_x = src[:, kk, tb * P:(tb + 1) * P]
                            lo_x = src[:, kk, T + tb * P:T + (tb + 1) * P]
                            mm(o[:, tb, :], hi_x, WHI[j][:, k, :], begin)
                            mm(o[:, tb, :], lo_x, WHI[j][:, k, :], False)
                            ins = mm(o[:, tb, :], hi_x, WLO[j][:, k, :], False, end)
                ins.then_inc(pe_sub, 1)
                c.sub.at += 1
                used.at += last and counted

            def group(pair, src=H, k0=0, units=4, kind="W", quads=None, ada_after=None, counted=True, then={},
                      order=range(4)):
                for s in range(2 * units):
                    if quads is not None and s % 2 == 0:
                        pe.wait_ge(h_quad, quads + s // 2 + 1)
                    sub(pair, src, k0 + 4 * order[s // 2] + s % 2 * 2, s == 0, s == 2 * units - 1, kind, counted)
                    if s == ada_after:
                        ada_sum()
                    if s in then:
                        then[s]()

            def ada_sum(acc=ACC):
                pe.wait_ge(ada_op, c.ada_group.value(1, times=KT))
                if c.ada_group.at:
                    pe.wait_ge(ada_bias, c.ada_group.value())
                for j in range(8):
                    ins = mm(SMALL[:, j:j + 1], acc[:, j * P:(j + 1) * P], ones[:, 0:1], True, True)
                ins.then_inc(ada_red, 1)
                c.ada_group.at += 1

            def square_sum(k, q, ready=None, src=None, dst=None):
                src, dst = (YF, MISC[:, 0:T]) if src is None else (src, dst)
                pe.wait_ge(sq_ready, ready or 4 * k + q + 1)
                for t in range(4 * q, 4 * q + 4):
                    ins = mm(dst, ones, src[:, t, :], t == 0, t == KT - 1)
                if q == 3:
                    ins.then_inc(ssq_ready, 1)

            def w_out_groups(k, quads, with_ada, order=range(4)):
                for g in range(4):
                    then = {6: lambda: square_sum(k, g - 1)} if g else {}
                    for s in range(8):
                        if with_ada and 8 * g + s in ADA_SUM_IN_W_OUT:
                            acc = (G, ACC)[ADA_SUM_IN_W_OUT[8 * g + s] % 2]
                            then[s] = lambda other=then.get(s), acc=acc: (other and other(), ada_sum(acc))
                    group("AB"[g % 2], quads=quads if g == 0 else None, then=then,
                          order=range(4) if g else order)
                square_sum(k, 3)

            def ffn(quads, loops, turn, at=2):
                def gate(**more):
                    group("A", counted=False, **more)
                    c.gate.at += 1

                def up(**more):
                    if c.gate.at > 1:
                        pe.wait_ge(up_done, c.gate.value(-1))
                    group("B", counted=False, **more)

                def down(ada_after=None, turn=None, src=HID, at=None):
                    pe.wait_ge(hid_lo, c.hid.value(1))
                    pe.wait_ge(gate_done, c.gate.value())
                    for n in range(4):
                        group("AC"[n % 2], src=src, units=1, ada_after=ada_after if n == 2 else None,
                              then={1: lambda: turn(0)} if turn and n == at else {})
                    c.hid.at += 1

                gate(quads=quads)
                up(ada_after=5)
                gate()
                up()
                down(ada_after=0)
                for first, last, beside in ((2, 2 + loops, 1), (2 + loops, NF - 1, 0)):
                    if first < last:
                        with pe.Fori(first, last) as i:
                            c.enter(i - first, sub=24, A=2, C=2, hid=1, gate=1, ada_group=beside)
                            gate()
                            up()
                            down(ada_after=0 if beside else None)
                        c.leave(last - first)
                gate()
                up()
                down()
                down(turn=turn, src=HID_LAST, at=at)

            pe.wait_ge(base_in, 16)
            pe.wait_ge(c_in, 32)
            nc.tensor.transpose(MISC[:, 0:32], CRAW, ident[0:32, 0:32]).then_inc(c_t, 1)
            pe.wait_ge(cact, 1)
            pe.wait_ge(rows_in, 16 * len(rows_src))
            pe.wait_ge(praw_zero, 1)
            for n in range(BLOCKS):
                ins = nc.tensor.transpose(MISC[:, n * P:(n + 1) * P], PRAW[:, n, :], ident)
            ins.then_inc(prm_t, 1)
            pe.wait_ge(x_rows, 32)
            for n in range(8):
                if n >= 4:
                    pe.wait_ge(x_in, n - 3)
                for k in range(2):
                    for tb in range(2):
                        at = tb * D + (2 * n + k) * P
                        ins = nc.tensor.transpose(PS[n // 2 % 2][:, n % 2, (2 * k + tb) * P:(2 * k + tb + 1) * P],
                                                  yf[:, at:at + P], ident)
                ins.then_inc(x_turned, 1)

            for g in range(4):
                ada_sum((ACC, G)[g % 2])
                if g == 0:
                    for q in range(4):
                        square_sum(0, q)
            group("A", quads=Q_WIN1)
            group("B", ada_after=5)
            def gates(n):
                kind = n // 2
                if n == 0:
                    pe.wait_ge(conv_step, 24)
                    pe.wait_ge(pool_chain, 1)
                    pe.wait_ge(mix_w, 16 * 5)
                else:
                    pe.wait_ge(rg_sig, 4 * n)
                for t in range(n % 2 * 4, n % 2 * 4 + 4):
                    mm(flat("C")[:, t % 4 * T:(t % 4 + 1) * T], tiles(48 + 4 * kind, 4)[:, t * P:(t + 1) * P],
                       R[:, 24 + t, :], True, True).then_inc(rg_mm, 1)

            group("A")
            group("B", ada_after=5, then={6: lambda: gates(0)})
            group("A", then={2: lambda: gates(1), 5: lambda: gates(2)})
            group("B", ada_after=5, then={0: lambda: gates(3)})

            pe.wait_ge(free["A"], 3)
            pe.wait_ge(free["B"], 3)
            pe.wait_ge(pooled, 4)
            for t in range(8):
                g, oc = t // 2, t % 2
                for kc in range(2):
                    ins = mm(eight(t), tiles(56 + 2 * g + kc, 1)[:, oc * P:(oc + 1) * P], R[:, 16 + 2 * g + kc, :],
                             kc == 0, kc == 1)
                ins.then_inc(pool_mm, 1)
            pe.wait_ge(pool_ev, 8)

            w_out_groups(1, Q_WOUT1, True)
            def sums(q):
                if q == 0:
                    pe.wait_ge(ada_bias, c.ada_group.value())
                square_sum(2, q, 4 * 2 + 2 * q + 1)
                square_sum(3, q, 4 * 2 + 2 * q + 2, R[:, GAINED:GAINED + KT, :], SMALL[:, 0:T])

            ffn(Q_FFN1, NF - 4, sums, 3)
            for q in range(1, 4):
                sums(q)

            group("A", quads=Q_WIN2)
            group("B")
            with pe.Fori(0, 2) as i:
                c.enter(i, sub=16, A=1, B=1, ada_group=1)
                group("A")
                group("B", ada_after=5)
            c.leave(2)
            def latents_sum():
                for n in range(2):
                    pe.wait_ge(lat_sq, n + 1)
                    for t in range(4):
                        ins = mm(MISC[:, n * T:(n + 1) * T], ones, YF[:, 4 * n + t, :], t == 0, t == 3)
                    ins.then_inc(lat_ss, 1)

            group("A", kind="T", then={6: latents_sum})
            group("B", kind="T", ada_after=5)
            sub("C", H, 0, True, False, "K")
            sub("C", H, 8, False, True, "K")

            heads_of = lambda hp: ((0, 2 * hp), (1, 2 * hp + 1))
            value = lambda tile, h, tb: rf[:, (tile + 4 * (h // 4)) * T + tb * 512 + h % 4 * P:][:, 0:P]

            def logits(hp):
                if hp == 0:
                    pe.wait_ge(con_in, 16)
                    pe.wait_ge(free["C"], C_FFN1 + 1)
                else:
                    pe.wait_ge(y_ev, hp)
                for a, h in heads_of(hp):
                    q, k = R[:, 8 + h, :], R[:, 16 + h, :]
                    mm(PAIR["C"][:, a, 0:256], k[:, 0:P], q, True, True)
                    ins = mm(PAIR["C"][:, a, 256:384], k[:, P:T], q[:, P:T], True, True)
                ins.then_inc(z_mm, 1)

            def tails(hp):
                pe.wait_ge(sp_done, hp + 1)
                if hp == 0:
                    pe.wait_ge(ada_bias, 22)
                    pe.wait_ge(lat_ms, 1)
                for a, h in heads_of(hp):
                    s, o = three(84)[:, a, :], PS[3][:, a, :]
                    mm(o[:, 0:256], CON[:, TRI:TRI + P], s[:, 0:256], True)
                    mm(o[:, 128:256], ones, s[:, 256:384], False, True)
                    ins = mm(o[:, 256:384], CON[:, TRI:TRI + P], s[:, 256:384], True, True)
                ins.then_inc(u_mm, 1)

            def weighted(hp):
                pe.wait_ge(a_act, hp + 1)
                for a, h in heads_of(hp):
                    w, o = three(81)[:, a, :], PAIR["C"][:, 0, a * T:(a + 1) * T]
                    mm(o, value(24, h, 0), w[:, 0:256], True)
                    ins = mm(o[:, 128:256], value(24, h, 1), w[:, 256:384], False, True)
                ins.then_inc(y_mm, 1)

            for hp in range(4):
                group("A", then={0: lambda: logits(hp), 6: lambda: tails(hp)})
                group("B", then={4: lambda: weighted(hp)})

            def head_sums(hp):
                pe.wait_ge(hd_sq, 1 + 3 * (hp + 1))
                pe.wait_ge(free["C"], C_LAT + max(hp - 1, 0))
                for n, (nope, rope, half) in enumerate(((78, 80, EVEN), (79, 80, ODD), (81, 77, EVEN), (82, 77, EVEN))):
                    o = flat("C")[:, n * T:(n + 1) * T]
                    mm(o, ones, R[:, nope, :], True)
                    ins = mm(o, CON[:, half:half + P], R[:, rope, :], False, True)
                ins.then_inc(hd_ss, 1)

            def swaps(hp):
                if hp == 0:
                    pe.wait_ge(rope_in, 1)
                    mm(SMALL[:, 0:T], CON[:, PERM:PERM + P], KPE, True, True).then_inc(rope_swap, 1)
                pe.wait_ge(rope_in, hp + 2)
                mm(SMALL[:, T:2 * T], CON[:, PERM:PERM + P], R[:, 16 + hp, :], True, True).then_inc(rope_swap, 1)

            for n, (pair, tile) in enumerate(LAT):
                pe.wait_ge(h_quad, Q_LAT + (1 if n < 3 else 2))
                src, k0 = (HQ, 0) if n < 3 else (H, 4)
                group(pair, src, k0, units=1, kind="W" if n < 5 else "T")
                if n == 4:
                    head_sums(0)
                if n == 5:
                    swaps(0)

            pe.wait_ge(free["A"], A_LAT)
            pe.wait_ge(free["B"], B_LAT)
            pe.wait_ge(y_ev, 4)
            for hp in range(4):
                pe.wait_ge(hd_scaled, hp + 1)
                for a, h in heads_of(hp):
                    q, qr, k, kr = R[:, 8 + h, :], R[:, 16 + hp, :], R[:, h, :], R[:, KR(hp, a), :]
                    for qs, ks, at in ((slice(0, P), slice(0, P), slice(0, 128)),
                                       (slice(P, T), slice(0, T), slice(128, 384))):
                        mm(PAIR["A"][:, a, at], q[:, qs], k[:, ks], True)
                        ins = mm(PAIR["A"][:, a, at], qr[:, qs], kr[:, ks], False, True)
                ins.then_inc(s_mm, 1)
                if hp < 3:
                    head_sums(hp + 1)
                    swaps(hp + 1)
                    pe.wait_ge(hd_ms, hp + 2)
                if hp == 0:
                    pe.wait_ge(h_quad, Q_PROJ_B + 2)
                for s in range(4):
                    sub("C", H, 8 + 2 * s, s == 0, s == 3)
                pe.wait_ge(p_dve, hp + 1)
                for a in range(2):
                    for b in range(3):
                        n = slice(b * P, (b + 1) * P)
                        ins = nc.tensor.transpose(PAIR["B"][:, a, n], SC[:, a, n], ident)
                ins.then_inc(pt_mm, 1)
                pe.wait_ge(pt_ev, hp + 1)
                if hp:
                    pe.wait_ge(o_ev, hp)
                for a, h in heads_of(hp):
                    p, o = SC[:, a, :], MISC[:, a * T:(a + 1) * T]
                    mm(o, value(20, h, 0), p[:, 0:256], True)
                    ins = mm(o[:, 128:256], value(20, h, 1), p[:, 256:384], False, True)
                ins.then_inc(o_mm, 1)

            for n in range(4):
                group("AB"[n % 2], units=2, quads=None if n else Q_PROJ_A)
            w_out_groups(4, Q_WOUT2, False, MERGED)
            def turn(q):
                pe.wait_ge(x_step, KT + 4 * q + 4)
                for tb in range(2):
                    n = 2 * q + tb
                    if n >= 4:
                        pe.wait_ge(out_ready, n - 3)
                    for k in range(4):
                        ins = nc.tensor.transpose(OUT_BANKS[n % 4][:, k * P:(k + 1) * P],
                                                  X[:, 4 * q + k, tb * P:(tb + 1) * P], ident)
                    ins.then_inc(x_turned, 1)

            ffn(Q_FFN2, 0, turn)
            assert c.sub.at == 2 * N_UNITS
            for q in range(1, 4):
                turn(q)


def kernel(**inputs):
    import concourse.bacc as _bacc
    from concourse.bass_utils import run_bass_kernel_spmd as _run

    nc = _bacc.Bacc("TRN2", target_bir_lowering=False, num_devices=1)
    arrays = {}

    def dram(name, a):
        a = np.ascontiguousarray(a)
        arrays[f"in_{name}"] = a
        return nc.dram_tensor(f"in_{name}", a.shape, mybir.dt.from_np(a.dtype), kind="ExternalInput").ap()

    ktiles = lambda name: dram(name, np.asarray(inputs[name]).reshape(np.shape(inputs[name])[-2:]))\
        .rearrange("(k p) n -> p k n", p=P)
    weights = [ktiles(n) for n in ("w_in", "w_out", "w_ffn_gate", "w_ffn_up", "w_ffn_down", "w_in_2", "w_uq_2",
                                   "w_ukv_2", "w_proj_mla_2", "w_proj_sb_2", "w_out_2", "w_ffn_in_2",
                                   "w_ffn_out_2")]
    ada_w = [ktiles("w_ada"), ktiles("w_ada_2")]

    rows_src = []
    for name, n in PARAMS:
        source = {"q_rope": "g_q_head_2", "k_rope": "g_k_head_2"}.get(name, name)
        a = dram(f"row_{name}", np.asarray(inputs[source]).reshape(1, -1))
        width = a.shape[1] // n
        if width == P:
            r = 0
            while r < n:
                at = COL[name] + r
                m = min(n - r, P - at % P)
                rows_src.append((at // P, at % P, m, 0, P,
                                 a[:, r * P:(r + m) * P].rearrange("o (r n) -> (o r) n", n=P)))
                r += m
        else:
            at, parts = COL[name], ((0, 64), (64, 128)) if "rope" in name else ((0, 128),)
            for c0, c1 in parts:
                first = 128 if "rope" in name else 0
                rows_src.append((at // P, at % P, 1, c0, c1, a[:, first:first + c1 - c0]))

    gates = [dram(n, np.asarray(inputs[n])[0]).rearrange("(t e) i j -> e i t j", e=2) for n in ("w_rg_a", "w_rg_i")]
    w_pool = dram("w_pool", np.asarray(inputs["w_pool"])[0]).rearrange("g (k p) n -> p (g k) n", p=P)

    base = np.zeros((P, N_BASE), np.float32)
    base[:, IDENT:IDENT + P] = np.eye(P)
    base[:, ONES:ONES + P] = 1.0
    for g in range(4):
        for t in range(16):
            base[:, INV + 16 * g + t] = np.float32(1.0) / np.float32(min(t + 1, 2 << g))
    i = np.arange(P)
    row, col = i[:, None], i[None, :]
    con = np.zeros((P, N_CONST), np.float32)
    con[:, PERM:PERM + P] = (row // 32 ^ 1 == col // 32) & (row % 32 == col % 32)
    con[:, TRI:TRI + P] = row >= col
    con[:, EVEN:EVEN + P] = row < 64
    con[:, ODD:ODD + P] = row >= 64
    one = np.ones((P, 3 * P), np.float32)
    one[:, 0:P] = one[:, 2 * P:] = row < col
    con[:, SB_ONE:SB_ONE + 3 * P] = one
    con[:, SB_NEG:SB_NEG + 3 * P] = (one - 1) * np.float32(1e30)
    for at in (0, 2 * P):
        con[:, MLA_NEG + at:MLA_NEG + at + P] = np.where(col <= row, 0, -1e30)
    con[:, FREQ] = np.float32(10000.0) ** (-(i % 32).astype(np.float32) / np.float32(32))
    con[:, SIGN] = np.where(i % 64 < 32, -1, 1)

    out = nc.dram_tensor("out_0", (T, D), F32, kind="ExternalOutput").ap()
    c_rows = [dram(n, np.asarray(inputs[n]).reshape(16, P)) for n in ("c", "c_2")]
    build(nc, dram("x", np.asarray(inputs["x"])[0]), c_rows, dram("positions", inputs["positions_2"]), rows_src, weights,
          ada_w, dram("base_const", base), dram("att_const", con), *gates, w_pool, out)
    r = _run(nc, [arrays], core_ids=[0])
    return r.results[0]["out_0"].reshape(1, T, D)
```
